# Optimizing a Trainium2 kernel written in Bass

```python
import math
import jax, jax.numpy as jnp
from jax import lax
import numpy as np

"""One inference step (DEPTH layers) of a hybrid decoder trunk for a prompt group and a sample group sharing weights.

Per layer: pre-RMSNorm -> ONE combined input projection whose columns are partitioned into two parallel head groups
(A: short gated convolution, CONV_DIM channels = 8 groups of 64; B: native sparse attention, 8 query heads / 2 KV heads
of 64 with compressed, selected-block and sliding-window branches, each with its own K/V) -> concat over head groups ->
ONE output projection -> residual; pre-RMSNorm -> hierarchical MoE (top-1 group, top-2 experts in group) -> residual;
sigmoid-gated per-layer input embedding added to the residual. T5 relative bias table shared by all layers.

Inputs: x_prompt (BATCH, SEQ, D_MODEL), x_sample (DEC_BATCH, DEC_SEQ, D_MODEL), p_prompt (DEPTH, BATCH, SEQ, 256),
p_sample (DEPTH, DEC_BATCH, DEC_SEQ, 256), paged caches cache_{k,v}_{cmp,slc} (DEPTH, N_PHYS, PAGE_SIZE, N_KV_HEADS, HEAD_DIM),
window buffers cache_{k,v}_win (DEPTH, DEC_BATCH, min(WINDOW, PAST_LEN), N_KV_HEADS, HEAD_DIM),
state_conv (DEPTH, DEC_BATCH, CONV_K-1, CONV_DIM), page_table (DEC_BATCH, PAST_LEN // PAGE_SIZE) int32, weights.

Returns (y_prompt (BATCH, SEQ, D_MODEL), y_sample (DEC_BATCH, DEC_SEQ, D_MODEL),
  k_cmp_p, v_cmp_p, k_slc_p, v_slc_p: (DEPTH, BATCH, SEQ, N_KV_HEADS, HEAD_DIM) new rows,
  k_win_p, v_win_p: (DEPTH, BATCH, min(WINDOW, SEQ), N_KV_HEADS, HEAD_DIM), conv_p: (DEPTH, BATCH, CONV_K-1, CONV_DIM),
  k_cmp_s, v_cmp_s, k_slc_s, v_slc_s: (DEPTH, DEC_BATCH, DEC_SEQ, N_KV_HEADS, HEAD_DIM) new rows,
  k_win_s, v_win_s: (DEPTH, DEC_BATCH, min(WINDOW, PAST_LEN), N_KV_HEADS, HEAD_DIM) updated buffers,
  conv_s: (DEPTH, DEC_BATCH, CONV_K-1, CONV_DIM) updated buffer).
"""

D_MODEL = 1024
BATCH = 1
SEQ = 512
DEPTH = 1
DEC_BATCH = 8
DEC_SEQ = 4
PAST_LEN = 256
PAGE_SIZE = 128

HEAD_DIM = 64
MIX_DIM = D_MODEL
CONV_DIM = MIX_DIM // 2
CONV_K = 3
ATTN_DIM = MIX_DIM - CONV_DIM
N_HEADS = ATTN_DIM // HEAD_DIM
N_KV_HEADS = 2
GROUP = N_HEADS // N_KV_HEADS
KV_DIM = N_KV_HEADS * HEAD_DIM
N_BRANCH = 3
CMP_BLOCK = 32
CMP_STRIDE = 16
CMP_HIDDEN = 256
SLC_BLOCK = 64
N_SEL = 16
WINDOW = 512
Q_BLOCK = 128
FORCE_SCORE = 1e4
NUM_BUCKETS = 32
MAX_DISTANCE = 128
N_GROUPS = 4
EXPERTS_PER_GROUP = 8
N_EXPERTS = N_GROUPS * EXPERTS_PER_GROUP
TOP_K = 2
D_EXPERT = 512
EXPERT_BLOCK = 128
PLE_DIM = 256
EPS = 1e-6
W_IN_COLS = 3 * CONV_DIM + ATTN_DIM + 6 * KV_DIM + N_BRANCH * N_HEADS

kernel_name = 'hymba_conv_nsa_hmoe_step'

def rms_norm(x, g):
    x32 = x.astype(jnp.float32)
    y = x32 * lax.rsqrt(jnp.mean(x32 * x32, axis=-1, keepdims=True) + EPS)
    return (y * g.astype(jnp.float32)).astype(x.dtype)

def rel_bucket(dist):
    n = jnp.maximum(dist, 0)
    max_exact = NUM_BUCKETS // 2
    nf = jnp.maximum(n, 1).astype(jnp.float32)
    large = max_exact + (jnp.log(nf / max_exact) / math.log(MAX_DISTANCE / max_exact) * (NUM_BUCKETS - max_exact)).astype(jnp.int32)
    large = jnp.minimum(large, NUM_BUCKETS - 1)
    return jnp.where(n < max_exact, n, large)

def masked_softmax(s, mask):
    s = jnp.where(mask, s, -jnp.inf)
    m = jnp.max(s, axis=-1, keepdims=True)
    m = jnp.where(jnp.isfinite(m), m, 0.0)
    p = jnp.exp(s - m)
    return p / jnp.maximum(jnp.sum(p, axis=-1, keepdims=True), 1e-30)

def _split_points():
    sizes = [CONV_DIM] * 3 + [ATTN_DIM] + [KV_DIM] * 6 + [N_BRANCH * N_HEADS]
    return [int(v) for v in np.cumsum(sizes)[:-1]]

def _project(x, w_in_l, norm_l, qn_l, kn_l):
    B, T, _ = x.shape
    z = rms_norm(x, norm_l) @ w_in_l
    xh, bg, cg, q, kc, vc, ks, vs, kw, vw, gt = jnp.split(z, _split_points(), axis=-1)
    kv = lambda t: t.reshape(B, T, N_KV_HEADS, HEAD_DIM)
    q = rms_norm(q.reshape(B, T, N_HEADS, HEAD_DIM), qn_l)
    gates = jax.nn.sigmoid(gt.astype(jnp.float32)).reshape(B, T, N_HEADS, N_BRANCH)
    return (cg * xh, bg, q, kv(kc), kv(vc), rms_norm(kv(ks), kn_l[1]), kv(vs),
            rms_norm(kv(kw), kn_l[2]), kv(vw), gates)

def short_conv(u_prev, u, w):
    T = u.shape[1]
    up = jnp.concatenate([u_prev, u], axis=1)
    y = w[0] * up[:, 0:T]
    for k in range(1, CONV_K):
        y = y + w[k] * up[:, k:k + T]
    return y, up[:, T:]

def compress(rows, pe, w1, w2):
    B, Tk = rows.shape[:2]
    n_chunk = Tk // CMP_STRIDE
    r = CMP_BLOCK // CMP_STRIDE
    n_cmp = n_chunk - r + 1
    chunks = rows[:, :n_chunk * CMP_STRIDE].reshape(B, n_chunk, CMP_STRIDE, N_KV_HEADS, HEAD_DIM)
    blocks = jnp.concatenate([chunks[:, j:j + n_cmp] for j in range(r)], axis=2) + pe[:, None, :]
    flat = blocks.transpose(0, 1, 3, 2, 4).reshape(B, n_cmp, N_KV_HEADS, CMP_BLOCK * HEAD_DIM)
    return jax.nn.gelu(flat @ w1) @ w2

def nsa_attend(q, gates, pos_q, k_cmp, v_cmp, k_slc, v_slc, k_win, v_win, pos_win, rel_bias):
    B, Tq = q.shape[:2]
    scale = HEAD_DIM ** -0.5
    qg = q.reshape(B, Tq, N_KV_HEADS, GROUP, HEAD_DIM)
    rb = rel_bias.astype(jnp.float32).reshape(NUM_BUCKETS, N_KV_HEADS, GROUP)

    def dense_bias(dist):
        return rb[rel_bucket(dist)].transpose(0, 2, 3, 1)[None]

    n_cmp = k_cmp.shape[1]
    c_start = jnp.arange(n_cmp, dtype=jnp.int32) * CMP_STRIDE
    d_c = pos_q[:, None] - (c_start + CMP_BLOCK - 1)[None, :]
    s_c = jnp.einsum('bqhgd,bnhd->bqhgn', qg, k_cmp).astype(jnp.float32) * scale + dense_bias(d_c)
    p_c = masked_softmax(s_c, (d_c >= 0)[None, :, None, None, :])
    o_c = jnp.einsum('bqhgn,bnhd->bqhgd', p_c.astype(v_cmp.dtype), v_cmp)

    Tk = k_slc.shape[1]
    n_slc = -(-Tk // SLC_BLOCK)
    pad = n_slc * SLC_BLOCK - Tk
    s_start = jnp.arange(n_slc, dtype=jnp.int32) * SLC_BLOCK
    overlap = ((c_start[:, None] < s_start[None, :] + SLC_BLOCK) &
               (c_start[:, None] + CMP_BLOCK > s_start[None, :])).astype(jnp.float32)
    imp = jnp.einsum('bqhgn,ns->bqhs', p_c, overlap)
    q_blk = pos_q // SLC_BLOCK
    j = jnp.arange(n_slc, dtype=jnp.int32)[None, :]
    forced = (j == 0) | (j == q_blk[:, None]) | (j == q_blk[:, None] - 1)
    valid = s_start[None, :] <= pos_q[:, None]
    imp = jnp.where(valid[None, :, None, :], imp + jnp.where(forced, FORCE_SCORE, 0.0)[None, :, None, :], -jnp.inf)
    n_sel = min(N_SEL, n_slc)
    _, idx = lax.top_k(imp, n_sel)
    idx = idx.transpose(0, 2, 1, 3)

    def blocks_of(t):
        t = jnp.pad(t, ((0, 0), (0, pad), (0, 0), (0, 0)))
        return t.reshape(B, n_slc, SLC_BLOCK, N_KV_HEADS, HEAD_DIM).transpose(0, 3, 1, 2, 4)

    bi = jnp.arange(B)[:, None, None, None]
    hi = jnp.arange(N_KV_HEADS)[None, :, None, None]
    nk = n_sel * SLC_BLOCK
    k_sel = blocks_of(k_slc)[bi, hi, idx].reshape(B, N_KV_HEADS, Tq, nk, HEAD_DIM)
    v_sel = blocks_of(v_slc)[bi, hi, idx].reshape(B, N_KV_HEADS, Tq, nk, HEAD_DIM)
    pos_sel = (idx[..., None] * SLC_BLOCK + jnp.arange(SLC_BLOCK, dtype=jnp.int32)).reshape(B, N_KV_HEADS, Tq, nk)
    d_s = pos_q[None, None, :, None] - pos_sel
    bias_s = rb[rel_bucket(d_s), hi].transpose(0, 2, 1, 4, 3)
    s_s = jnp.einsum('bqhgd,bhqkd->bqhgk', qg, k_sel).astype(jnp.float32) * scale + bias_s
    p_s = masked_softmax(s_s, (d_s >= 0).transpose(0, 2, 1, 3)[:, :, :, None, :])
    o_s = jnp.einsum('bqhgk,bhqkd->bqhgd', p_s.astype(v_sel.dtype), v_sel)

    d_w = pos_q[:, None] - pos_win[None, :]
    mask_w = (d_w >= 0) & (d_w < WINDOW) & (pos_win[None, :] >= 0)
    s_w = jnp.einsum('bqhgd,bkhd->bqhgk', qg, k_win).astype(jnp.float32) * scale + dense_bias(d_w)
    p_w = masked_softmax(s_w, mask_w[None, :, None, None, :])
    o_w = jnp.einsum('bqhgk,bkhd->bqhgd', p_w.astype(v_win.dtype), v_win)

    g = gates.reshape(B, Tq, N_KV_HEADS, GROUP, N_BRANCH)
    o = g[..., 0:1] * o_c + g[..., 1:2] * o_s + g[..., 2:3] * o_w
    return o.reshape(B, Tq, ATTN_DIM).astype(q.dtype)

def nsa_prompt(q, gates, k_cmp, v_cmp, k_slc, v_slc, k_win, v_win, rel_bias):
    B, T = q.shape[:2]
    n_blk = T // Q_BLOCK
    band = WINDOW + Q_BLOCK
    pad = lambda t: jnp.pad(t, ((0, 0), (WINDOW, 0), (0, 0), (0, 0)))
    kw_p, vw_p = pad(k_win), pad(v_win)

    def one(i):
        s = i * Q_BLOCK
        sl = lambda t, n: lax.dynamic_slice_in_dim(t, s, n, axis=1)
        pos_q = s + jnp.arange(Q_BLOCK, dtype=jnp.int32)
        pos_w = s - WINDOW + jnp.arange(band, dtype=jnp.int32)
        return nsa_attend(sl(q, Q_BLOCK), sl(gates, Q_BLOCK), pos_q, k_cmp, v_cmp, k_slc, v_slc,
                          sl(kw_p, band), sl(vw_p, band), pos_w, rel_bias)

    o = lax.map(one, jnp.arange(n_blk, dtype=jnp.int32))
    return o.transpose(1, 0, 2, 3).reshape(B, T, ATTN_DIM)

def moe_ffn(h, w_rg, b_rg, w_re, b_re, w_g, w_u, w_d):
    N, D = h.shape
    p_grp = jax.nn.softmax((h @ w_rg).astype(jnp.float32) + b_rg.astype(jnp.float32), axis=-1)
    grp = jnp.argmax(p_grp, axis=-1)
    gw = jnp.take_along_axis(p_grp, grp[:, None], axis=1)[:, 0]
    le = ((h @ w_re).astype(jnp.float32) + b_re.astype(jnp.float32)).reshape(N, N_GROUPS, EXPERTS_PER_GROUP)
    le_g = jnp.take_along_axis(le, grp[:, None, None], axis=1)[:, 0]
    w2, e_loc = lax.top_k(jax.nn.softmax(le_g, axis=-1), TOP_K)
    w2 = w2 / jnp.sum(w2, axis=-1, keepdims=True) * gw[:, None]
    e_idx = grp[:, None] * EXPERTS_PER_GROUP + e_loc
    A = N * TOP_K
    flat_e = e_idx.reshape(-1).astype(jnp.int32)
    flat_w = w2.reshape(-1)
    flat_tok = jnp.arange(A, dtype=jnp.int32) // TOP_K
    counts = jnp.bincount(flat_e, length=N_EXPERTS)
    padded = (counts + EXPERT_BLOCK - 1) // EXPERT_BLOCK * EXPERT_BLOCK
    pad_end = jnp.cumsum(padded)
    pad_start = pad_end - padded
    seg_start = jnp.cumsum(counts) - counts
    order = jnp.argsort(flat_e)
    e_sorted = flat_e[order]
    tok_sorted = flat_tok[order]
    dest = pad_start[e_sorted] + jnp.arange(A, dtype=jnp.int32) - seg_start[e_sorted]
    n_blk = (A + N_EXPERTS * (EXPERT_BLOCK - 1) + EXPERT_BLOCK - 1) // EXPERT_BLOCK
    P = n_blk * EXPERT_BLOCK
    slot_tok = jnp.full((P,), N, jnp.int32).at[dest].set(tok_sorted)
    h_pad = jnp.concatenate([h, jnp.zeros((1, D), h.dtype)], axis=0)
    xb = h_pad[slot_tok].reshape(n_blk, EXPERT_BLOCK, D)
    blk_expert = jnp.clip(jnp.searchsorted(pad_end, jnp.arange(n_blk, dtype=jnp.int32) * EXPERT_BLOCK, side='right'), 0, N_EXPERTS - 1)

    def run(args):
        xe, e = args
        return (jax.nn.silu(xe @ w_g[e]) * (xe @ w_u[e])) @ w_d[e]

    yb = lax.map(run, (xb, blk_expert)).reshape(P, D)
    y_assign = yb[dest].astype(jnp.float32) * flat_w[order][:, None]
    return jax.ops.segment_sum(y_assign, tok_sorted, num_segments=N).astype(h.dtype)

def _post(x, conv_out, attn_out, p, w_out_l, norm_ffn_l, moe_w, norm_ple_l, w_ple_l, w_pg_l, b_pg_l):
    h = x + jnp.concatenate([conv_out, attn_out], axis=-1) @ w_out_l
    hn = rms_norm(h, norm_ffn_l)
    h = h + moe_ffn(hn.reshape(-1, D_MODEL), *moe_w).reshape(h.shape)
    gate = jax.nn.sigmoid((rms_norm(h, norm_ple_l) @ w_pg_l).astype(jnp.float32) + b_pg_l.astype(jnp.float32))
    return h + (gate * (p @ w_ple_l).astype(jnp.float32)).astype(h.dtype)

def setup_inputs(seed: int = 0) -> dict:
    key = jax.random.key(seed)
    keys = iter(jax.random.split(key, 48))

    def nrm(shape, scale):
        return jax.random.normal(next(keys), shape, jnp.float32) * scale

    def gain(shape):
        return 1.0 + nrm(shape, 0.1)

    n_pages = PAST_LEN // PAGE_SIZE
    n_used = DEC_BATCH * n_pages
    n_phys = n_used + max(1, n_used // 4)
    w_buf = min(WINDOW, PAST_LEN)
    page_shape = (DEPTH, n_phys, PAGE_SIZE, N_KV_HEADS, HEAD_DIM)
    win_shape = (DEPTH, DEC_BATCH, w_buf, N_KV_HEADS, HEAD_DIM)
    return {
        'x_prompt': nrm((BATCH, SEQ, D_MODEL), 1.0),
        'x_sample': nrm((DEC_BATCH, DEC_SEQ, D_MODEL), 1.0),
        'p_prompt': nrm((DEPTH, BATCH, SEQ, PLE_DIM), 1.0),
        'p_sample': nrm((DEPTH, DEC_BATCH, DEC_SEQ, PLE_DIM), 1.0),
        'cache_k_cmp': nrm(page_shape, 1.0),
        'cache_v_cmp': nrm(page_shape, 1.0),
        'cache_k_slc': nrm(page_shape, 1.0),
        'cache_v_slc': nrm(page_shape, 1.0),
        'cache_k_win': nrm(win_shape, 1.0),
        'cache_v_win': nrm(win_shape, 1.0),
        'state_conv': nrm((DEPTH, DEC_BATCH, CONV_K - 1, CONV_DIM), 1.0),
        'page_table': jax.random.permutation(next(keys), n_phys)[:n_used].reshape(DEC_BATCH, n_pages).astype(jnp.int32),
        'w_in': nrm((DEPTH, D_MODEL, W_IN_COLS), D_MODEL ** -0.5),
        'w_out': nrm((DEPTH, MIX_DIM, D_MODEL), MIX_DIM ** -0.5),
        'conv_w': nrm((DEPTH, CONV_K, CONV_DIM), CONV_K ** -0.5),
        'norm_mix': gain((DEPTH, D_MODEL)),
        'norm_ffn': gain((DEPTH, D_MODEL)),
        'norm_ple': gain((DEPTH, D_MODEL)),
        'q_norm': gain((DEPTH, HEAD_DIM)),
        'k_norm': gain((DEPTH, N_BRANCH, HEAD_DIM)),
        'cmp_pe_k': nrm((DEPTH, CMP_BLOCK, HEAD_DIM), 0.1),
        'cmp_w1_k': nrm((DEPTH, CMP_BLOCK * HEAD_DIM, CMP_HIDDEN), (CMP_BLOCK * HEAD_DIM) ** -0.5),
        'cmp_w2_k': nrm((DEPTH, CMP_HIDDEN, HEAD_DIM), CMP_HIDDEN ** -0.5),
        'cmp_pe_v': nrm((DEPTH, CMP_BLOCK, HEAD_DIM), 0.1),
        'cmp_w1_v': nrm((DEPTH, CMP_BLOCK * HEAD_DIM, CMP_HIDDEN), (CMP_BLOCK * HEAD_DIM) ** -0.5),
        'cmp_w2_v': nrm((DEPTH, CMP_HIDDEN, HEAD_DIM), CMP_HIDDEN ** -0.5),
        'rel_bias': nrm((NUM_BUCKETS, N_HEADS), 0.5),
        'w_router_group': nrm((DEPTH, D_MODEL, N_GROUPS), D_MODEL ** -0.5),
        'b_router_group': nrm((DEPTH, N_GROUPS), 0.01),
        'w_router_expert': nrm((DEPTH, D_MODEL, N_EXPERTS), D_MODEL ** -0.5),
        'b_router_expert': nrm((DEPTH, N_EXPERTS), 0.01),
        'w_exp_gate': nrm((DEPTH, N_EXPERTS, D_MODEL, D_EXPERT), D_MODEL ** -0.5),
        'w_exp_up': nrm((DEPTH, N_EXPERTS, D_MODEL, D_EXPERT), D_MODEL ** -0.5),
        'w_exp_down': nrm((DEPTH, N_EXPERTS, D_EXPERT, D_MODEL), D_EXPERT ** -0.5),
        'w_ple': nrm((DEPTH, PLE_DIM, D_MODEL), PLE_DIM ** -0.5),
        'w_ple_gate': nrm((DEPTH, D_MODEL, D_MODEL), D_MODEL ** -0.5),
        'b_ple_gate': nrm((DEPTH, D_MODEL), 0.1),
    }

def reference(x_prompt, x_sample, p_prompt, p_sample, cache_k_cmp, cache_v_cmp, cache_k_slc, cache_v_slc,
              cache_k_win, cache_v_win, state_conv, page_table, w_in, w_out, conv_w, norm_mix, norm_ffn, norm_ple,
              q_norm, k_norm, cmp_pe_k, cmp_w1_k, cmp_w2_k, cmp_pe_v, cmp_w1_v, cmp_w2_v, rel_bias,
              w_router_group, b_router_group, w_router_expert, b_router_expert, w_exp_gate, w_exp_up, w_exp_down,
              w_ple, w_ple_gate, b_ple_gate):
    y_p, y_s = x_prompt, x_sample
    Bp, T = x_prompt.shape[:2]
    Bs, Ts = x_sample.shape[:2]
    past_len = page_table.shape[1] * cache_k_cmp.shape[2]
    w_buf = cache_k_win.shape[2]
    new_p = [[] for _ in range(7)]
    new_s = [[] for _ in range(7)]
    for i in range(DEPTH):
        moe_w = (w_router_group[i], b_router_group[i], w_router_expert[i], b_router_expert[i],
                 w_exp_gate[i], w_exp_up[i], w_exp_down[i])
        post_w = (w_out[i], norm_ffn[i], moe_w, norm_ple[i], w_ple[i], w_ple_gate[i], b_ple_gate[i])

        u, bg, q, kc, vc, ks, vs, kw, vw, gts = _project(y_p, w_in[i], norm_mix[i], q_norm[i], k_norm[i])
        conv_y, conv_st = short_conv(jnp.zeros((Bp, CONV_K - 1, CONV_DIM), u.dtype), u, conv_w[i])
        kc_blk = rms_norm(compress(kc, cmp_pe_k[i], cmp_w1_k[i], cmp_w2_k[i]), k_norm[i, 0])
        vc_blk = compress(vc, cmp_pe_v[i], cmp_w1_v[i], cmp_w2_v[i])
        attn = nsa_prompt(q, gts, kc_blk, vc_blk, ks, vs, kw, vw, rel_bias)
        y_p = _post(y_p, bg * conv_y, attn, p_prompt[i], *post_w)
        wp = min(WINDOW, T)
        for lst, val in zip(new_p, (kc, vc, ks, vs, kw[:, T - wp:], vw[:, T - wp:], conv_st)):
            lst.append(val)

        u, bg, q, kc, vc, ks, vs, kw, vw, gts = _project(y_s, w_in[i], norm_mix[i], q_norm[i], k_norm[i])
        conv_y, conv_st = short_conv(state_conv[i], u, conv_w[i])
        gather = lambda c: c[page_table].reshape(Bs, past_len, N_KV_HEADS, HEAD_DIM)
        kc_all = jnp.concatenate([gather(cache_k_cmp[i]), kc], axis=1)
        vc_all = jnp.concatenate([gather(cache_v_cmp[i]), vc], axis=1)
        ks_all = jnp.concatenate([gather(cache_k_slc[i]), ks], axis=1)
        vs_all = jnp.concatenate([gather(cache_v_slc[i]), vs], axis=1)
        kw_all = jnp.concatenate([cache_k_win[i], kw], axis=1)
        vw_all = jnp.concatenate([cache_v_win[i], vw], axis=1)
        kc_blk = rms_norm(compress(kc_all, cmp_pe_k[i], cmp_w1_k[i], cmp_w2_k[i]), k_norm[i, 0])
        vc_blk = compress(vc_all, cmp_pe_v[i], cmp_w1_v[i], cmp_w2_v[i])
        pos_q = past_len + jnp.arange(Ts, dtype=jnp.int32)
        pos_w = past_len - w_buf + jnp.arange(w_buf + Ts, dtype=jnp.int32)
        attn = nsa_attend(q, gts, pos_q, kc_blk, vc_blk, ks_all, vs_all, kw_all, vw_all, pos_w, rel_bias)
        y_s = _post(y_s, bg * conv_y, attn, p_sample[i], *post_w)
        for lst, val in zip(new_s, (kc, vc, ks, vs, kw_all[:, Ts:], vw_all[:, Ts:], conv_st)):
            lst.append(val)

    sp = [jnp.stack(v, axis=0) for v in new_p]
    ss = [jnp.stack(v, axis=0) for v in new_s]
    return (y_p, y_s, sp[0], sp[1], sp[2], sp[3], sp[4], sp[5], sp[6],
            ss[0], ss[1], ss[2], ss[3], ss[4], ss[5], ss[6])


_drawn_inputs = setup_inputs


def setup_inputs(seed=0):
    import zlib

    import numpy as np

    out = dict(_drawn_inputs(seed))
    spreads = {}
    factors = {'norm_ple': 3.693,
     'q_norm': 4.39,
     'b_router_group': 31.518,
     'b_router_expert': 5.661,
     'b_ple_gate': 3.449}
    for name, (base, spread) in spreads.items():
        noise = np.random.default_rng([zlib.crc32(name.encode()), seed]).standard_normal(out[name].shape)
        drawn = base * np.exp(spread * noise) if base else spread * noise
        out[name] = __import__('jax').numpy.asarray(drawn.astype(out[name].dtype))
    for name, factor in factors.items():
        out[name] = (out[name] * factor).astype(out[name].dtype)
    return out
```

```python
from contextlib import ExitStack

import numpy as np
import concourse.bass as bass
from concourse import mybir

F32 = mybir.dt.float32
F32R = mybir.dt.float32r
I32 = mybir.dt.int32
U32 = mybir.dt.uint32
ALU = mybir.AluOpType
ACT = mybir.ActivationFunctionType
X = mybir.AxisListType.X

P = 128
D = 1024
DC = D // P
SEQ, NB, NT = 512, 8, 4
NS = NB * NT
N = SEQ + NS
TP = SEQ // P
TT = TP + 1
CONV, HD, NH, NKV = 512, 64, 8, 2
G = NH // NKV
CC = CONV // P
PAST, PAGE = 256, 128
NPG = NB * PAST // PAGE
STRIDE = 16
NCP = SEQ // STRIDE - 1
CS = PAST // STRIDE
NCH = NB * CS
XC = NCH + SEQ // STRIDE + 2
CH = 256
NBR = 3
NE, NG, DE = 32, 4, 512
EG = NE // NG
SLOTS = 64
MAXOV = (2 * N - 1) // SLOTS
JOBS = NE + MAXOV + 1
OVMAX = (N - 1) // SLOTS
PLE = 256
EPS = 1e-6
BIG = 1e30
NBUCK = 32
BREF = 511
BL = 640
KEYS_S = PAST + NT
KC, VC, KS, VS, KW, VW = [i * P for i in range(6)]

C_ID, C_TRI, C_ONE, C_II, C_DESC, C_EID, C_NM, C_HM, C_SEL, C_END = np.cumsum(
    [0, P, P, P, SLOTS, NE, NE, NH, NKV, 2 * P]).tolist()


def rows(t):
    return P if t < TP else NS


def constants():
    c = np.zeros((P, C_END), np.float32)
    i = np.arange(P)
    c[:, C_ID:C_TRI] = np.eye(P)
    c[:, C_TRI:C_ONE] = i[:, None] < i[None, :]
    c[:, C_ONE:C_II] = 1.0
    c[:, C_II:C_DESC] = (i[:, None] % SLOTS) == np.arange(SLOTS)[None, :]
    c[:, C_DESC:C_EID] = NE - np.arange(NE)
    c[:, C_EID:C_NM] = np.arange(NE)
    head = (i % 32) // NT
    c[:, C_NM:C_HM] = head[:, None] == np.arange(NH)
    c[:, C_HM:C_SEL] = (head // G)[:, None] == np.arange(NKV)
    for rt in range(2):
        tok = (rt * 4 + i // 32) * NT + i % NT
        c[:NS, C_SEL + rt * P:C_SEL + (rt + 1) * P] = np.arange(NS)[:, None] == tok[None, :]
    dist = BREF - np.arange(BL)
    n = np.maximum(dist, 0)
    exact = NBUCK // 2
    nf = np.maximum(n, 1).astype(np.float32)
    large = exact + (np.log(nf / np.float32(exact)) / np.float32(np.log(128 / exact))
                     * np.float32(NBUCK - exact)).astype(np.int32)
    bucket = np.where(n < exact, n, np.minimum(large, NBUCK - 1))
    b = np.zeros((NBUCK + 1, BL), np.float32)
    b[bucket, np.arange(BL)] = 1.0
    b[NBUCK] = dist < 0
    tok = np.zeros((P, TT), np.int32)
    for t in range(TT):
        tok[:, t] = t * P + i
    tok[NS:, TP] = 0
    return c, b, tok


class Chain:

    def __init__(self, eng, sem):
        self.eng, self.sem, self.n = eng, sem, 0

    def __call__(self, ins):
        self.n += 1
        ins.then_inc(self.sem, 1)
        self.eng.wait_ge(self.sem, self.n)


SEMS = """
M_in SM_in X_ev X_in X_tr asn_ok bl_out bl_ps bl_sb cb_done cb_ok cm_done cm_exp cm_o cm_p cm_pT
cm_pv cm_sub cm_tr cs_out cs_outd cs_ps cst_in ct_done ct_ok cv_done cv_ok cv_u cv_vec cv_vecc cv_xh
dst_ok dve_chain eps_ok f_exp f_h2 f_hn f_hpT f_mm f_o f_out0 f_out1 f_plT f_sq f_tr f_z g_exp g_ok
g_ps gath gt_done gu_copied hT_ok h_ok hi_ok hid_b hid_done hid_gelu hn_done hn_out hs_done ht_done
ht_ok ic_ok idx_in jei_ok kc_in kcmp_out kt_done kt_ok kv_copied kvout lo_ok op_done op_h ot_ok
ot_ps passed pf_done pt_in r_done r_e2 r_exp r_log r_w2 raw0 raw1 raw2 raw3 raw4 raw5 rb_in rb_ok
root_ok s_qbd sc_out silu_ok so_ok so_ps sq_done ss_done ss_exp ss_o ss_pT ss_pv ss_soft ss_sum
ss_tr tm_done tm_norm tr_done tr_k tr_q u_exp u_o u_pT u_pv u_s u_soft u_tr used vc_in vcmp_out
vec_in w1_in w2_in wc0 wc1 wc2 wc3 winout wout_in wpg_in wq0 wq1 wr_in x0_in x1_in x2_in x3_in x4_in
xT_ok xT_t x_hi x_lo x_tr xn_done y_ok y_out ya0 ya1 ylo_ok ysb_free yz_ok yz_out z_ok z_out
"""


def bcast(ap, n):
    return bass.AP(tensor=ap.tensor, offset=ap.offset, ap=[[0, P], [1, n]])


def build(nc, a, o):
    ctx = ExitStack()
    with ctx:
        base, K = 16512, 1024

        def at(name, shape, off, dt=F32):
            return nc.alloc_sbuf_tensor_at(name, shape, dt, offset=base + int(off))

        def run_of(start):
            cur = [int(start)]

            def place(name, shape, dt=F32):
                off = cur[0]
                cur[0] += -(-int(np.prod(shape[1:])) * 4 // 32) * 32
                return at(name, shape, off, dt)
            return place, cur

        wring = at("wring", [P, 3, DC * 512], 0)
        raw = at("raw", [P, 6, 2048], 0)
        h = at("h", [P, TT, D], 48 * K)
        xT = at("xT", [P, DC, N], 68 * K)
        hiw = at("hiw", [P, 3, 2048], 86 * K, F32R)
        low = at("low", [P, 3, 2048], 110 * K, F32R)
        mixT = at("mixT", [P, DC, N], 86 * K)
        blrow = at("blrow", [P, BL], 96 * K)
        kvt = at("kvt", [P, TT, 6 * P], 103.5 * K)
        junk = at("junk", [P, D], 104 * K)
        qT = at("qT", [P, G, N], 118.5 * K)
        ksT = at("ksT", [P, N], 127 * K)
        kwT = at("kwT", [P, N], 129.25 * K)
        M = at("M", [P, NH, 512], 131.5 * K)
        xn = at("xn", [P, 2, D], 131.5 * K)
        hidt = at("hidt", [P, 2, 2 * XC], 131.5 * K)
        sq = at("sq", [P, D], 139.5 * K)
        qn = at("qn", [P, 2, 512], 143.5 * K)
        RB = 147.5 * K
        X1 = at("X1", [P, 2048], RB)
        X2 = at("X2", [P, 2048], RB + 8 * K)
        w1s = at("w1s", [P, 16, CH], RB + 16 * K)
        XT = at("XT", [P, 8, 2 * XC], RB + 32 * K)
        kcache = at("kcache", [P, NPG, P], RB)
        vcache = at("vcache", [P, NPG, P], RB + 8 * K)
        kcT = at("kcT", [P, NPG, P], RB + 16 * K)
        wout = at("wout", [P, DC, D], RB)
        gffn = at("gffn", [P, D], RB + 32 * K)
        hnt = at("hnt", [P, D], RB + 36 * K)
        cpT = at("cpT", [P, NH, P], RB + 36 * K)
        upp = at("upp", [P, SEQ + 2], 134.5 * K)
        ups = at("ups", [P, NB, 2 + NT], 136.75 * K)
        nsq = at("nsq", [P, P], 137 * K)
        cs_out = at("cs_out", [18, CONV], 143.5 * K)
        cs_in = at("cs_in", [P, CC, 2 + 2 * NB], 145.5 * K)
        sc = at("sc", [P, 2, 512], 68 * K)
        pr = at("pr", [P, 2, 512], 72 * K)
        pT = at("pT", [P, 2, 512], 76 * K)
        oacc = at("oacc", [P, 512], 80 * K)
        cms = at("cms", [P, 256], 82 * K)
        cme = at("cme", [P, 256], 83 * K)
        rsmall, rcur = run_of(134 * K)
        wr = rsmall("wr", [P, DC, NG + NE])
        br = rsmall("br", [P, NG + NE])
        lg = rsmall("lg", [P, TT, NG + NE])
        og = rsmall("og", [P, TT, NG])
        tg = rsmall("tg", [P, TT, NG])
        le = rsmall("le", [P, TT, NE])
        t32 = rsmall("t32", [P, TT, NE])
        oh1 = rsmall("oh1", [P, TT, NE])
        oh2 = rsmall("oh2", [P, TT, NE])
        asn = rsmall("asn", [P, TT, NE])
        slot = rsmall("slot", [P, TT, NE])
        ovs = rsmall("ovs", [P, 4, NE])
        rs = rsmall("rs", [P, 8, TT])
        jex = rsmall("jex", [P, MAXOV, NE])
        jey = rsmall("jey", [P, MAXOV, NE])
        jef = rsmall("jef", [P, MAXOV + 1])
        zslot = rsmall("zslot", [SLOTS, JOBS], I32)
        assert rcur[0] <= RB
        xg = at("xg", [P, D], 134 * K)
        xpack = at("xpack", [P, DC, 2 * SLOTS], 138 * K, F32R)
        Sg = at("Sg", [P, 2, 512], 142 * K)
        sg = at("sg", [P, 256], 146 * K)
        hT32 = at("hT32", [P, 4, SLOTS], 147 * K)
        hpack = at("hpack", [P, 4, 2 * SLOTS], 148 * K, F32R)
        ylo = at("ylo", [P, D], 150 * K)
        ysb = at("ysb", [P, D], 154 * K)
        wpg = at("wpg", [P, DC, D], 158 * K)
        wple = at("wple", [P, 2, D], 68 * K)
        pin = at("pin", [P, TT, PLE], 76 * K)
        bpg = at("bpg", [P, D], 81 * K)
        yga = at("yga", [P, 2, 2, D], 0)
        h2n = at("h2n", [P, D], 16 * K)
        hpT = at("hpT", [P, DC, P], 20 * K)
        plT = at("plT", [P, 2, P], 24 * K)
        sgt = at("sgt", [P, D], 26 * K)
        yo = at("yo", [P, 2, D], 30 * K)
        small, scur = run_of(190.5 * K)
        cst = small("cst", [P, C_END])
        gk = small("gk", [P, 2, P])
        gmix = small("gmix", [P, DC])
        gple = small("gple", [P, DC])
        gq = small("gq", [P, 1])
        gk0 = small("gk0", [P, 1])
        cwT = small("cwT", [P, 12])
        ssq = small("ssq", [P, TT])
        rn = small("rn", [P, TT])
        ss12 = small("ss12", [P, 12])
        gates = small("gates", [P, TT, 24])
        w2s = small("w2s", [P, 2, HD])
        eps = small("eps", [P, 1])
        hb = small("hb", [P, 2])
        vcb = small("vcb", [P, P])
        vcp = small("vcp", [P, P])
        kcbT = small("kcbT", [P, NCH])
        kcpT = small("kcpT", [P, 32])
        Qbd = small("Qbd", [P, NB, 32])
        SM = small("SM", [P, KEYS_S])
        cmb = small("cmb", [P, 2, NCH])
        nmk = small("nmk", [P, 2, NS])
        st = small("st", [P, 40])
        gs = small("gs", [P, 2, NBR])
        tok = small("tok", [P, TT], I32)
        osam = small("osam", [P, 2, P])
        kcb, kcp, g24 = osam[:, 0, :], osam[:, 1, :], osam[:, 1, 0:24]
        upst = small("upst", [P, CC, 2 * NB])
        wts = small("wts", [P, 2, TT])
        dst = small("dst", [P, 2, TT], I32)
        jei = small("jei", [P, MAXOV + 1], I32)
        pti = small("pti", [P, NPG], I32)
        sidx = small("sidx", [SLOTS, JOBS], I32)
        icur = small("icur", [SLOTS, 1], I32)
        assert scur[0] <= 229360 - base, scur[0]

        ps = ctx.enter_context(nc.psum_tensor("ps", [P, 8, 512], F32))
        bline = nc.dram_tensor("biaslines", (NH, P, BL), F32).ap()
        hn_d = nc.dram_tensor("hn_rows", (N, D), F32).ap()
        y_d = nc.dram_tensor("expert_rows", ((JOBS - 1) * SLOTS, D), F32).ap()
        slot_d = nc.dram_tensor("slot_token", (JOBS * SLOTS, 1), I32).ap()

        S = {n: ctx.enter_context(nc.semaphore(n)) for n in SEMS.split()}
        block = ctx.enter_context(nc.Block())

        def eye(n):
            return cst[0:n, C_ID:C_ID + n]

        kv_out = list(enumerate(("k_cmp", "v_cmp", "k_slc", "v_slc", "k_win", "v_win")))
        w_in = a["w_in"].rearrange("(p c) n -> p c n", c=DC)
        TM = [(3 * CONV, 512), (3 * CONV + 512, 512), (3 * CONV + 1024, 280)]
        WGU = [a[f"w_exp_{x}"].rearrange("e (p k c) n -> e p k (c n)", k=2, c=4) for x in ("gate", "up")]
        WD = a["w_exp_down"].rearrange("e (p k c) n -> e p k (c n)", k=2, c=2)
        PIECES = [(w, k) for w in (*WGU, WD) for k in range(2)]

        def load_job(sp, J, e):
            for k, (src, half) in enumerate(PIECES):
                if e is None:
                    part = src[0, :, half, :]
                else:
                    sp.wait_ge(S["lo_ok"], J * 6 + (k - 5))
                    part = src[bass.ds(e, 1), :, half, :].rearrange("e p n -> p (e n)")
                sp.dma_start(raw[:, k, :], part).then_inc(S[f"raw{k}"], 16)

        def run_jobs(eng, job):
            job(0, True)
            with eng.Fori(1, NE) as J:
                job(J, False)
            nov = eng.value_load(jei[0:1, MAXOV:MAXOV + 1], min_val=0, max_val=MAXOV)
            with eng.If(nov > 0):
                with eng.Fori(NE, nov + NE) as J:
                    job(J, False)

        def total(eng):
            return eng.value_load(jei[0:1, MAXOV:MAXOV + 1], min_val=0, max_val=MAXOV) + NE

        def token_cols(dve, done, t, gain, b, ok):
            r = rows(t)
            dve.wait_ge(done, t + 1)
            src = ps[:, b:b + 2, :].rearrange("p k (c n) -> p (k c) n", n=P)[:, :, 0:r]
            to = xT[:, :, t * P:t * P + r]
            if gain is None:
                nc.vector.tensor_copy(to, src).then_inc(ok, 1)
            else:
                nc.vector.tensor_tensor(to, src, gain[:].unsqueeze(2).broadcast_to([P, DC, r]), ALU.mult).then_inc(ok, 1)

        @block.sync
        def _(sp):
            sp.dma_start(cst[:], a["consts"]).then_inc(S["cst_in"], 16)
            for t in range(TP):
                sp.dma_start(h[:, t, :], a["x_prompt"][t * P:(t + 1) * P, :]).then_inc(S[f"x{t}_in"], 16)
            sp.dma_start(h[0:NS, TP, :], a["x_sample"]).then_inc(S[f"x{TP}_in"], 16)
            for g, (c0, n) in enumerate(TM):
                sp.dma_start(wring[:, g, 0:DC * n].rearrange("p (c n) -> p c n", n=n),
                             w_in[:, :, c0:c0 + n]).then_inc(S[f"wq{min(g, 1)}"], 16)
            sp.dma_start(pti[0:1, :], a["page_table"].rearrange("(x b) n -> x (b n)", x=1)).then_inc(S["pt_in"], 16)
            sp.wait_ge(S["pt_in"], 16)

            def page(lp):
                return sp.value_load(pti[0:1, lp:lp + 1], min_val=0, max_val=a["cache_k_cmp"].shape[0] - 1)

            def chunk_rows(which, arrived):
                src = a[f"cache_{which}_cmp"].rearrange("g (c r) n -> g c (r n)", r=STRIDE)
                for lp in range(NPG):
                    pg = page(lp)
                    for hh in range(NKV):
                        sp.dma_start(X1[8 * lp:8 * lp + 8, D * hh:D * (hh + 1)].rearrange("c (r d) -> c r d", d=HD),
                                     src[bass.ds(pg, 1), :, :].rearrange("x c (r g d) -> (x c) r g d", g=NKV, d=HD)[:, :, hh, :])\
                            .then_inc(arrived, 16)
                r0 = SEQ // STRIDE
                for hh in range(NKV):
                    sp.dma_start(X2[r0:r0 + 2, :].rearrange("b (g r d) -> b r g d", g=NKV, d=HD)[:, :, hh, :],
                                 a[f"cmp_pe_{which}"].rearrange("(b r) d -> b r d", b=2)).then_inc(arrived, 16)

            def back(which, arrived):
                sp.wait_ge(S[f"{which}cmp_out"], 16)
                for hh in range(NKV):
                    sp.dma_start(X2[0:SEQ // STRIDE, D * hh:D * (hh + 1)].rearrange("c (r d) -> c r d", d=HD),
                                 o[f"{which}_cmp_p"].rearrange("(c r) (g d) -> c r g d", r=STRIDE, g=NKV)[:, :, hh, :])\
                        .then_inc(arrived, 16)

            sp.dma_start(w1s[:], a["cmp_w1_k"].rearrange("(k p) n -> p k n", p=P)).then_inc(S["w1_in"], 16)
            chunk_rows("k", S["X_in"])
            sp.wait_ge(S["bl_sb"], 1)
            sp.dma_start(bline, blrow[0:NH, :].unsqueeze(1).broadcast_to([NH, P, BL])).then_inc(S["bl_out"], 16)
            sp.wait_ge(S["tm_norm"], TT)
            for i, nm in kv_out:
                done = S["kcmp_out"] if i == 0 else S["vcmp_out"] if i == 1 else S["kvout"]
                sp.dma_start(o[nm + "_p"].rearrange("(t p) c -> p t c", p=P),
                             kvt[:, 0:TP, i * P:(i + 1) * P]).then_inc(done, 16)
                if i < 4:
                    sp.dma_start(o[nm + "_s"], kvt[0:NS, TP, i * P:(i + 1) * P]).then_inc(S["kvout"], 16)
                else:
                    for b in range(NB):
                        sp.dma_start(o[nm + "_s"][b, PAST - NT:PAST, :],
                                     kvt[b * NT:(b + 1) * NT, TP, i * P:(i + 1) * P]).then_inc(S["winout"], 16)
            back("k", S["X_in"])
            sp.wait_ge(S["tm_done"], TT)
            for c4 in range(CC):
                if c4 == 3:
                    sp.wait_ge(S["X_ev"], 8)
                    chunk_rows("v", S["X_in"])
                    back("v", S["X_in"])
                    sp.wait_ge(S["hid_done"], 2)
                    sp.dma_start(w1s[:], a["cmp_w1_v"].rearrange("(k p) n -> p k n", p=P)).then_inc(S["w1_in"], 16)
                    sp.wait_ge(S["cv_done"], 1)
                for j in range(3):
                    sp.dma_start(wring[:, c4 % 3, 0:DC * 384].rearrange("p (c n) -> p c n", n=384)[:, :, j * P:(j + 1) * P],
                                 w_in[:, :, j * CONV + c4 * P:j * CONV + (c4 + 1) * P]).then_inc(S[f"wc{c4}"], 16)
            for nm in ("k_win", "v_win"):
                sp.dma_start(o[nm + "_s"][:, 0:PAST - NT, :], a["cache_" + nm][:, NT:PAST, :]).then_inc(S["winout"], 16)
            sp.wait_ge(S["hid_done"], 4)
            for lp in range(NPG):
                for name, d, arrived in (("cache_k_slc", kcache, "kc_in"), ("cache_v_slc", vcache, "vc_in")):
                    sp.dma_start(d[:, lp, :], a[name][bass.ds(page(lp), 1), :, :].rearrange("x p n -> p (x n)"))\
                        .then_inc(S[arrived], 16)
            sp.wait_ge(S["bl_out"], 16)
            for q in range(4):
                for n in range(NH):
                    r0 = 32 * q + NT * n
                    sp.dma_start(SM[r0:r0 + NT, :], bass.AP(tensor=bline.tensor, offset=n * P * BL + BREF - PAST,
                                                            ap=[[BL - 1, NT], [1, KEYS_S]])).then_inc(S["SM_in"], 16)
            sp.wait_ge(S["cv_ok"], CC)
            sp.wait_ge(S["cb_done"], 2)
            sp.wait_ge(S["cs_outd"], 16 * 2)
            for n in range(NH):
                sp.dma_start(M[:, n, :], bass.AP(tensor=bline.tensor, offset=n * P * BL + P - 1,
                                                 ap=[[BL - 1, P], [1, 512]])).then_inc(S["M_in"], 16)
            sp.wait_ge(S["kt_done"], 4)
            sp.dma_start(kcache[:], a["cache_k_win"].rearrange("b (g p) n -> p (b g) n", p=PAGE)).then_inc(S["kc_in"], 16)
            load_job(sp, 0, None)
            sp.wait_ge(S["ss_pv"], 4)
            sp.dma_start(vcache[:], a["cache_v_win"].rearrange("b (g p) n -> p (b g) n", p=PAGE)).then_inc(S["vc_in"], 16)
            sp.wait_ge(S["ss_pv"], 6)
            sp.dma_start(wout[:], a["w_out"].rearrange("(c p) n -> p c n", p=P)).then_inc(S["wout_in"], 16)
            sp.dma_start(gffn[:], bcast(a["norm_ffn"], D)).then_inc(S["wout_in"], 16)
            sp.wait_ge(S["u_soft"], 2 * NH * TP)
            sp.wait_ge(S["cm_sub"], TP)
            sp.dma_start(wr[:, :, 0:NG], a["w_router_group"].rearrange("(p c) n -> p c n", c=DC)).then_inc(S["wr_in"], 16)
            sp.dma_start(wr[:, :, NG:NG + NE], a["w_router_expert"].rearrange("(p c) n -> p c n", c=DC)).then_inc(S["wr_in"], 16)
            sp.dma_start(br[:, 0:NG], bcast(a["b_router_group"], NG)).then_inc(S["wr_in"], 16)
            sp.dma_start(br[:, NG:NG + NE], bcast(a["b_router_expert"], NE)).then_inc(S["wr_in"], 16)
            for t in range(TT):
                sp.wait_ge(S["hn_done"], t + 1)
                sp.dma_start(hn_d[t * P:t * P + rows(t), :], hnt[0:rows(t), :]).then_inc(S["hn_out"], 16)
            with sp.Fori(1, NE) as J:
                load_job(sp, J, J)
            sp.wait_ge(S["jei_ok"], 1)
            nov = sp.value_load(jei[0:1, MAXOV:MAXOV + 1], min_val=0, max_val=MAXOV)
            with sp.If(nov > 0):
                with sp.Fori(NE, nov + NE) as J:
                    e = sp.value_load(jei[0:1, bass.ds(J - NE, 1)], min_val=0, max_val=NE - 1)
                    load_job(sp, J, e)
            for t in range(TT):
                sp.wait_ge(S["f_o"], t + 1)
                to = o["y_prompt"][t * P:(t + 1) * P, :] if t < TP else o["y_sample"]
                sp.dma_start(to, yo[0:rows(t), t % 2, :]).then_inc(S[f"f_out{t % 2}"], 16)
            sp.wait_ge(S["kvout"], 16 * 8)
            sp.wait_ge(S["kcmp_out"], 16)
            sp.wait_ge(S["vcmp_out"], 16)
            sp.wait_ge(S["winout"], 16 * (2 * NB + 2))
            sp.wait_ge(S["cs_outd"], 16 * 2)
            sp.wait_ge(S["f_out0"], 16 * 3)
            sp.wait_ge(S["f_out1"], 16 * 2)

        @block.gpsimd
        def _(pool):
            pool.sem_inc(S["ysb_free"], 1)
            nc.gpsimd.memset(mixT[:, 6:8, 0:512], 0.0).then_inc(S["yz_ok"], 1)
            pool.wait_ge(S["yz_ok"], 1)
            for k in range(MAXOV * SLOTS // P):
                r0 = NE * SLOTS + k * P
                pool.dma_start(y_d[r0:r0 + P, :].rearrange("p (k n) -> p k n", k=2), mixT[:, 6:8, 0:512]).then_inc(S["yz_out"], 16)
            pool.wait_ge(S["yz_out"], 16 * (MAXOV * SLOTS // P))
            pool.wait_ge(S["z_ok"], 1)
            pool.dma_start(slot_d.rearrange("(s j) x -> s (j x)", s=SLOTS), zslot[:]).then_inc(S["z_out"], 16)
            pool.wait_ge(S["z_out"], 16)
            pool.wait_ge(S["dst_ok"], 1)
            for t in range(TT):
                for k in range(2):
                    pool.indirect_dma_start(out=slot_d, out_offset=bass.IndirectOffsetOnAxis(ap=dst[0:rows(t), k, t:t + 1], axis=0),
                                            in_=tok[0:rows(t), t:t + 1], in_offset=None).then_inc(S["sc_out"], 16)
            pool.wait_ge(S["sc_out"], 16 * 2 * TT)
            with nc.allow_non_contiguous_dma(reason="a slot index is one word"):
                pool.dma_start(sidx[:], slot_d.rearrange("(j s) x -> s (j x)", s=SLOTS)).then_inc(S["idx_in"], 16)
            pool.wait_ge(S["idx_in"], 16)
            pool.wait_ge(S["hn_out"], 16 * TT)

            def gather(J):
                pool.wait_ge(S["x_tr"], J)
                nc.gpsimd.tensor_copy(icur[:], sidx[:, J:J + 1] if isinstance(J, int) else sidx[:, bass.ds(J, 1)])\
                    .then_inc(S["ic_ok"], 1)
                pool.wait_ge(S["ic_ok"], J + 1)
                pool.sem_inc(S["passed"], 1)
                pool.indirect_dma_start(out=xg[0:SLOTS, :], out_offset=None, in_=hn_d,
                                        in_offset=bass.IndirectOffsetOnAxis(ap=icur[:, 0:1], axis=0)).then_inc(S["gath"], 16)

            def job(J, first):
                if not first:
                    pool.wait_ge(S["y_out"], J * 16)
                    pool.sem_inc(S["ysb_free"], 1)
                gather(J + 1)
                pool.wait_ge(S["y_ok"], J + 1)
                pool.dma_start(y_d[J * SLOTS:(J + 1) * SLOTS, :] if first else y_d[bass.ds(J * SLOTS, SLOTS), :],
                               ysb[0:SLOTS, :]).then_inc(S["y_out"], 16)

            gather(0)
            run_jobs(pool, job)
            n = total(pool)
            pool.wait_ge(S["y_out"], n * 16)
            pool.sem_inc(S["passed"], 1)
            for t in range(TT):
                if t >= 2:
                    pool.wait_ge(S["f_h2"], t - 1)
                for k in range(2):
                    pool.indirect_dma_start(out=yga[0:rows(t), t % 2, k, :], out_offset=None, in_=y_d,
                                            in_offset=bass.IndirectOffsetOnAxis(ap=dst[0:rows(t), k, t:t + 1], axis=0))\
                        .then_inc(S[f"ya{t % 2}"], 16)

        @block.scalar
        def _(act):
            A = nc.scalar.activation
            C = ACT.Copy
            act.dma_start(gmix[:], a["norm_mix"].rearrange("(p c) -> p c", c=DC)).then_inc(S["vec_in"], 16)
            act.dma_start(gple[:], a["norm_ple"].rearrange("(p c) -> p c", c=DC)).then_inc(S["vec_in"], 16)
            for hh in range(NKV):
                act.dma_start(gq[hh * HD:(hh + 1) * HD, :], a["q_norm"].rearrange("(p x) -> p x", x=1)).then_inc(S["vec_in"], 16)
                act.dma_start(gk0[hh * HD:(hh + 1) * HD, :], a["k_norm"][0, :].rearrange("(p x) -> p x", x=1)).then_inc(S["vec_in"], 16)
                for i in range(2):
                    act.dma_start(gk[:, i, hh * HD:(hh + 1) * HD], bcast(a["k_norm"][i + 1, :], HD)).then_inc(S["vec_in"], 16)
            act.dma_start(cmb[0:12, 0, :], a["conv_w"].rearrange("k (c p) -> (k c) p", p=P)).then_inc(S["rb_in"], 16)
            act.dma_start(tok[:], a["tok"]).then_inc(S["vec_in"], 16)
            act.dma_start(w2s[:], a["cmp_w2_k"].rearrange("(m p) n -> p m n", p=P)).then_inc(S["w2_in"], 16)
            act.dma_start(SM[0:NBUCK, 0:NH], a["rel_bias"]).then_inc(S["rb_in"], 16)
            act.dma_start(mixT[0:NBUCK + 1, 0:2, 0:320], a["buckets"].rearrange("b (k n) -> b k n", k=2)).then_inc(S["rb_in"], 16)
            act.dma_start(mixT[0:2 * NB, 2, 0:512], a["state_conv"]).then_inc(S["rb_in"], 16)
            sums = []

            def root_of(x, src, n):
                A(x, src, ACT.Sqrt, scale=1.0 / n, bias=eps[0:x.shape[0], 0:1]).then_inc(S["root_ok"], 1)

            def head_roots(r, n):
                sums.append(1)
                act.wait_ge(S["ss_sum"], len(sums))
                root_of(ss12[0:r, 0:n], ss12[0:r, 0:n], HD)

            act.wait_ge(S["eps_ok"], 1)
            for t in range(TT):
                act.wait_ge(S[f"x{t}_in"], 16)
                A(sq[0:rows(t), :], h[0:rows(t), t, :], ACT.Square, accum_out=ssq[0:rows(t), t:t + 1]).then_inc(S["sq_done"], 1)
                act.wait_ge(S["sq_done"], t + 1)
                root_of(rn[0:rows(t), t:t + 1], ssq[0:rows(t), t:t + 1], D)
            act.wait_ge(S["bl_ps"], 1)
            A(blrow[0:NH, :].rearrange("p (k n) -> p k n", k=2), ps[0:NH, 6:8, 0:320], C).then_inc(S["bl_sb"], 1)
            act.wait_ge(S["vec_in"], 16 * 11)
            for t in range(TT):
                r, b = rows(t), 3 * (t % 2)
                act.wait_ge(S["tm_done"], t + 1)
                if t >= 2:
                    act.wait_ge(S["tr_done"], t - 1)
                A(qn[0:r, t % 2, :].rearrange("p (g h d) -> p h g d", g=G, h=NKV),
                  ps[0:r, b, :].rearrange("p (h g d) -> p h g d", g=G, h=NKV), C)
                A(kvt[0:r, t, 0:512], ps[0:r, b + 1, :], C)
                A(kvt[0:r, t, 512:768], ps[0:r, b + 2, 0:256], C)
                A(gates[0:r, t, :], ps[0:r, b + 2, 256:280], C).then_inc(S["kv_copied"], 1)
                head_roots(r, 12)
                if t:
                    act.wait_ge(S["tr_done"], t)
                    A(qT[:, :, (t - 1) * P:t * P], ps[:, 6, :].rearrange("p (g n) -> p g n", g=G), C,
                      scale=gq[:, 0:1]).then_inc(S["tr_q"], 1)
            act.wait_ge(S["tr_done"], TT)
            A(qT[:, :, SEQ:N], ps[:, 6, :].rearrange("p (g n) -> p g n", g=G)[:, :, 0:NS], C,
              scale=gq[:, 0:1]).then_inc(S["tr_q"], 1)

            def hidden(i):
                act.wait_ge(S["hid_b"], i + 1)
                if i:
                    act.wait_ge(S["cb_done"], i)
                for m in range(2):
                    A(hidt[:, m, :], ps[:, 4 + m, 0:2 * XC], ACT.Gelu_apprx_tanh, bias=hb[:, m:m + 1]).then_inc(S["hid_gelu"], 1)

            def conv_xh(c4):
                act.wait_ge(S["cv_done"], c4 + 1)
                if c4:
                    act.wait_ge(S["cv_u"], c4)
                A(sq[:, 0:N].rearrange("p (k n) -> p k n", k=2), ps[:, 0:2, 0:N // 2], C).then_inc(S["cv_xh"], 1)

            hidden(0)
            head_roots(P, 2)
            head_roots(NCP, 2)
            act.wait_ge(S["cb_done"], 1)
            act.dma_start(w2s[:], a["cmp_w2_v"].rearrange("(m p) n -> p m n", p=P)).then_inc(S["w2_in"], 16)
            conv_xh(0)
            conv_xh(1)
            hidden(1)
            conv_xh(2)
            conv_xh(3)
            act.wait_ge(S["cs_out"], 1)
            act.dma_start(o["conv_p"], cs_out[0:2, :]).then_inc(S["cs_outd"], 16)
            act.dma_start(o["conv_s"], cs_out[2:18, :]).then_inc(S["cs_outd"], 16)
            act.wait_ge(S["kv_copied"], TT)
            A(gates[:], gates[:], ACT.Exp, scale=-1.0).then_inc(S["g_exp"], 1)
            for u in range(6):
                act.wait_ge(S["ss_soft"], u + 1)
                if u >= 2:
                    act.wait_ge(S["ss_tr"], u - 1)
                w = NCH if u < 2 else PAST + NS
                A(pr[:, u % 2, 0:w], sc[:, u % 2, 0:w], ACT.Exp, bias=st[:, u:u + 1], scale=-1.0,
                  accum_out=st[:, 8 + u:9 + u]).then_inc(S["ss_exp"], 1)
            for i in range(TP):
                nk = 8 * i + 7
                U = 2 * NH * i
                w = P * (i + 1)

                def exps(u):
                    act.wait_ge(S["u_soft"], u + 1)
                    if u >= 2:
                        act.wait_ge(S["u_tr"], u - 1)
                    A(pr[:, u % 2, 0:w], sc[:, u % 2, 0:w], ACT.Exp, bias=st[:, 16 + u % 4:17 + u % 4], scale=-1.0,
                      accum_out=st[:, 20 + u % 4:21 + u % 4]).then_inc(S["u_exp"], 1)

                act.wait_ge(S["cm_sub"], i + 1)
                A(cme[:, 0:NH * nk], cms[:, 0:NH * nk], ACT.Exp).then_inc(S["cm_exp"], 1)
                exps(U)
                exps(U + 1)
                act.wait_ge(S["cm_tr"], i + 1)
                A(cpT[0:nk, :, :].rearrange("p (b n) q -> p b (n q)", b=2), ps[0:nk, 6:8, :], C).then_inc(S["cm_pT"], 1)
                for k in range(2 * NH):
                    u = U + k
                    act.wait_ge(S["u_tr"], u + 1)
                    if u >= 2:
                        act.wait_ge(S["u_pv"], u - 1)
                    A(pT[:, u % 2, 0:w], ps[:, 2 + u % 2, 0:w], C).then_inc(S["u_pT"], 1)
                    if k + 2 < 2 * NH:
                        exps(u + 2)
            act.wait_ge(S["kvout"], 16 * 8)
            act.wait_ge(S["kcmp_out"], 16)
            act.wait_ge(S["vcmp_out"], 16)
            act.wait_ge(S["winout"], 16 * (2 * NB + 2))
            for t in range(TT):
                act.wait_ge(S["op_h"], t + 1)
                A(junk[0:rows(t), :], h[0:rows(t), t, :], ACT.Square, accum_out=ssq[0:rows(t), t:t + 1]).then_inc(S["hs_done"], 1)
                act.wait_ge(S["hs_done"], t + 1)
                root_of(rn[0:rows(t), t:t + 1], ssq[0:rows(t), t:t + 1], D)
            act.wait_ge(S["r_log"], 1)
            A(tg[:], tg[:], ACT.Exp).then_inc(S["r_exp"], 1)
            act.wait_ge(S["r_e2"], 1)
            A(rs[:, 5, :], rs[:, 4, :], ACT.Exp).then_inc(S["r_w2"], 1)
            act.wait_ge(S["op_done"], TT)
            act.wait_ge(S["r_done"], TT)
            act.wait_ge(S["hn_out"], 16 * TT)
            act.dma_start(wpg[:], a["w_ple_gate"].rearrange("(p c) n -> p c n", c=DC)).then_inc(S["wpg_in"], 16)
            act.dma_start(wple[:], a["w_ple"].rearrange("(p c) n -> p c n", c=2)).then_inc(S["wpg_in"], 16)
            act.dma_start(pin[:, 0:TP, :], a["p_prompt"].rearrange("(t p) n -> p t n", p=P)).then_inc(S["wpg_in"], 16)
            act.dma_start(pin[0:NS, TP, :], a["p_sample"]).then_inc(S["wpg_in"], 16)
            act.dma_start(bpg[:], bcast(a["b_ple_gate"], D)).then_inc(S["wpg_in"], 16)
            act.wait_ge(S["jei_ok"], 1)

            def high(J, k):
                act.wait_ge(S[f"raw{k}"], J * 16 + 16)
                act.wait_ge(S["used"], J * 6 + (k + 1))
                A(hiw[:, k % 3, :], raw[:, k, :], C).then_inc(S["hi_ok"], 1)

            def x_high(J):
                act.wait_ge(S["x_tr"], J + 1)
                A(xpack[:, :, 0:SLOTS], ps[:, 3, :].rearrange("p (c s) -> p c s", s=SLOTS), C).then_inc(S["x_hi"], 1)

            def y_low(J):
                act.wait_ge(S["used"], J * 6 + 3)
                A(ylo[0:SLOTS, :].rearrange("p (k n) -> p k n", k=2), ps[SLOTS:P, 5:7, :], C).then_inc(S["ylo_ok"], 1)

            def job(J, first):
                high(J, 0)
                high(J, 1)
                if not first:
                    y_low(J)
                high(J, 2)
                act.wait_ge(S["used"], J * 6 + 5)
                A(Sg[:, 0, :], ps[:, 0, :], C).then_inc(S["gu_copied"], 1)
                high(J, 3)
                high(J, 4)
                act.wait_ge(S["used"], J * 6 + 7)
                A(Sg[:, 1, :], ps[:, 1, :], C).then_inc(S["gu_copied"], 1)
                high(J, 5)
                act.wait_ge(S["gt_done"], J + 1)
                A(sg[:], ps[:, 2, 0:256], ACT.Silu).then_inc(S["silu_ok"], 1)
                x_high(J + 1)

            x_high(0)
            run_jobs(act, job)
            n = total(act)
            y_low(n)
            act.wait_ge(S["y_out"], n * 16)
            for t in range(TT):
                r = rows(t)
                act.wait_ge(S["f_tr"], 2 * t + 1)
                if t:
                    act.wait_ge(S["f_mm"], 2 * t)
                A(plT[:, :, 0:r], ps[:, 6, 0:2 * P].rearrange("p (c n) -> p c n", c=2)[:, :, 0:r], C).then_inc(S["f_plT"], 1)
                act.wait_ge(S["f_h2"], t + 1)
                if t:
                    act.wait_ge(S["f_o"], t)
                A(sgt[0:r, :], h[0:r, t, :], ACT.Square, accum_out=ssq[0:r, t:t + 1]).then_inc(S["f_sq"], 1)
                act.wait_ge(S["f_sq"], t + 1)
                root_of(rn[0:r, t:t + 1], ssq[0:r, t:t + 1], D)
                act.wait_ge(S["f_z"], t + 1)
                act.wait_ge(S["f_sq"], t + 1)
                A(sgt[0:r, :], h2n[0:r, :], ACT.Exp, scale=-1.0).then_inc(S["f_exp"], 1)

        @block.tensor
        def _(pe):
            T = nc.tensor.transpose

            def mm(out, l, r, start, stop, skip=False):
                return nc.tensor.matmul(out, l, r, start=start, stop=stop, skip_group_check=skip)

            pe.sem_inc(S["used"], 3)
            pe.wait_ge(S["cst_in"], 16)
            pe.wait_ge(S["rb_in"], 64)
            pe.wait_ge(S["rb_ok"], 1)
            for k in range(2):
                last = mm(ps[0:NH, 6 + k, 0:320], SM[0:NBUCK + 1, 0:NH], mixT[0:NBUCK + 1, k, 0:320], True, True)
            last.then_inc(S["bl_ps"], 1)
            T(ps[:, 5, 0:12], cmb[0:12, 0, :], eye(12))
            for c in range(CC):
                last = T(ps[:, 5, 16 + 16 * c:32 + 16 * c], mixT[0:2 * NB, 2, c * P:(c + 1) * P], eye(2 * NB))
            last.then_inc(S["cv_vec"], 1)

            def token_T(t, src, b, done):
                v = src.rearrange("r (p c) -> r p c", c=DC)
                for c in range(DC):
                    last = T(ps[:, b + c // 4, (c % 4) * P:(c % 4) * P + rows(t)], v[:, :, c], eye(rows(t)))
                last.then_inc(done, 1)

            for t in range(TT):
                pe.wait_ge(S["xn_done"], t + 1)
                if t >= 2:
                    pe.wait_ge(S["xT_ok"], t - 1)
                token_T(t, xn[0:rows(t), t % 2, :], 2 * (t % 2), S["xT_t"])

            def heads_T(t):
                r = rows(t)
                pe.wait_ge(S["tm_norm"], t + 1)
                if t:
                    pe.wait_ge(S["tr_q"], t)
                    pe.wait_ge(S["tr_k"], t)
                else:
                    pe.wait_ge(S["bl_sb"], 1)
                for g in range(G):
                    T(ps[:, 6, g * P:g * P + r], qn[0:r, t % 2, g * P:(g + 1) * P], eye(r))
                T(ps[:, 7, 0:r], kvt[0:r, t, KS:KS + P], eye(r))
                T(ps[:, 7, P:P + r], kvt[0:r, t, KW:KW + P], eye(r)).then_inc(S["tr_done"], 1)

            pe.wait_ge(S["xT_ok"], TT)
            pe.wait_ge(S["cv_vecc"], 1)
            for t in range(TT):
                r, b = rows(t), 3 * (t % 2)
                if t >= 2:
                    pe.wait_ge(S["kv_copied"], t - 1)
                for g, (c0, n) in enumerate(TM):
                    if t == 0 and g < 2:
                        pe.wait_ge(S[f"wq{g}"], 16 + 16 * g)
                    w = wring[:, g, 0:DC * n].rearrange("p (c n) -> p c n", n=n)
                    for c in range(DC):
                        last = mm(ps[0:r, b + g, 0:n], xT[:, c, t * P:t * P + r], w[:, c, :], c == 0, c == DC - 1)
                last.then_inc(S["tm_done"], 1)
                if t:
                    heads_T(t - 1)
            heads_T(TP)

            def compress_hidden(i, which):
                pe.wait_ge(S["X_in"], 16 * NKV * (NPG + 2) * (i + 1))
                for pp in range(8):
                    if pp >= 4:
                        pe.wait_ge(S["X_ev"], 8 * i + pp - 3)
                    for hh in range(NKV):
                        T(ps[:, pp % 4, hh * XC:hh * XC + NCH], X1[:, D * hh + P * pp:D * hh + P * (pp + 1)], eye(P))
                        last = T(ps[:, pp % 4, hh * XC + NCH:(hh + 1) * XC], X2[0:XC - NCH, D * hh + P * pp:D * hh + P * (pp + 1)],
                                 eye(XC - NCH))
                    last.then_inc(S["X_tr"], 1)
                pe.wait_ge(S["w1_in"], 16 * (i + 1))
                pe.wait_ge(S["X_ev"], 8 * i + 8)
                for m in range(2):
                    for k in range(16):
                        w = w1s[:, k, m * P:(m + 1) * P]
                        if k < 8:
                            last = mm(ps[:, 4 + m, 0:2 * XC], w, XT[:, k, :], k == 0, False)
                        else:
                            nxt = XT[:, k - 8, :].rearrange("p (g n) -> p g n", g=NKV)[:, :, 1:XC]
                            out = ps[:, 4 + m, 0:2 * XC].rearrange("p (g n) -> p g n", g=NKV)[:, :, 0:XC - 1]
                            last = mm(out, w, nxt, False, k == 15)
                    last.then_inc(S["hid_done"], 1)

            def compress_out(i, which):
                pe.wait_ge(S["hid_gelu"], 2 * i + 2)
                pe.wait_ge(S["w2_in"], 16 * (i + 1))
                if i:
                    pe.wait_ge(S["ct_ok"], 1)
                for hh in range(NKV):
                    for m in range(2):
                        mm(ps[:, 6, hh * HD:(hh + 1) * HD], hidt[:, m, hh * XC:hh * XC + NCH], w2s[:, m, :], m == 0, m == 1)
                for hh in range(NKV):
                    for m in range(2):
                        last = mm(ps[0:NCP, 7, hh * HD:(hh + 1) * HD], hidt[:, m, hh * XC + NCH:hh * XC + NCH + NCP],
                                  w2s[:, m, :], m == 0, m == 1)
                last.then_inc(S["cb_done"], 1)

            def conv(c4):
                pe.wait_ge(S[f"wc{c4}"], 48)
                if c4:
                    pe.wait_ge(S["cv_ok"], c4)
                w = wring[:, c4 % 3, 0:DC * 384].rearrange("p (c n) -> p c n", n=384)
                for j in range(3):
                    for half in range(2):
                        for c in range(DC):
                            last = mm(ps[:, 2 * j + half, 0:N // 2], w[:, c, j * P:(j + 1) * P],
                                      xT[:, c, half * (N // 2):(half + 1) * (N // 2)], c == 0, c == DC - 1)
                last.then_inc(S["cv_done"], 1)

            pe.wait_ge(S["kv_copied"], TT)
            pe.wait_ge(S["tr_q"], TT)
            pe.wait_ge(S["tr_k"], TT)
            compress_hidden(0, "k")
            compress_out(0, "k")
            pe.wait_ge(S["hid_gelu"], 2)
            conv(0)
            pe.wait_ge(S["cb_ok"], 1)
            T(ps[:, 6, 256:256 + NCH], kcb, eye(P))
            T(ps[:, 6, 384:384 + NCP], kcp[0:NCP, :], eye(NCP)).then_inc(S["ct_done"], 1)
            conv(1)
            pe.wait_ge(S["cv_ok"], 2)
            compress_hidden(1, "v")
            compress_out(1, "v")
            conv(2)
            conv(3)
            pe.wait_ge(S["cv_ok"], CC)
            pe.wait_ge(S["cb_ok"], 2)
            for c in range(CC):
                last = T(ps[0:18, 7, c * P:(c + 1) * P], cs_in[:, c, :], eye(P))
            last.then_inc(S["cs_ps"], 1)

            def qrows(rt):
                return Qbd[:, 4 * rt:4 * rt + 4, :].rearrange("p b r -> p (b r)")

            def keys_T(i, n):
                pe.wait_ge(S["kc_in"], n)
                for b in range(4):
                    if i:
                        pe.wait_ge(S["kt_ok"], 4)
                        pe.wait_ge(S["ss_done"], 4)
                    for j in range(4):
                        last = T(ps[:, b, j * P:(j + 1) * P], kcache[:, 4 * b + j, :], eye(P))
                    last.then_inc(S["kt_done"], 1)

            def ss_scores(u):
                bank, rt = 4 + u % 2, u % 2
                if u >= 2:
                    pe.wait_ge(S["ss_soft"], u - 1)
                if u < 2:
                    last = mm(ps[:, bank, 0:NCH], qrows(rt), kcbT[:], True, True)
                else:
                    newT = ksT if u < 4 else kwT
                    pe.wait_ge(S["kt_ok"], 4 if u < 4 else 8)
                    mm(ps[:, bank, PAST:PAST + NS], qrows(rt), newT[:, SEQ:N], True, True, True)
                    for q in range(4):
                        b = 4 * rt + q
                        last = nc.tensor.matmul(ps[32 * q:32 * q + 32, bank, 0:PAST], Qbd[:, b, :],
                                                kcT[:, 2 * b:2 * b + 2, :].rearrange("p g n -> p (g n)"),
                                                start=True, stop=True, skip_group_check=True)
                last.then_inc(S["ss_done"], 1)

            def ss_values(u):
                rt = u % 2
                pe.wait_ge(S["ss_exp"], u + 1)
                if u:
                    pe.wait_ge(S["ss_pT"], u)
                if u < 2:
                    T(ps[:, 6, 0:P], pr[:, rt, 0:NCH], eye(P)).then_inc(S["ss_tr"], 1)
                else:
                    for j in range(2):
                        T(ps[:, 6, j * P:(j + 1) * P], pr[:, rt, j * P:(j + 1) * P], eye(P))
                    T(ps[0:NS, 6, 2 * P:3 * P], pr[:, rt, PAST:PAST + NS], eye(P)).then_inc(S["ss_tr"], 1)
                pe.wait_ge(S["ss_pT"], u + 1)
                if u:
                    pe.wait_ge(S["ss_o"], u)
                else:
                    pe.wait_ge(S["s_qbd"], 2)
                po = ps[:, 7, 0:P]
                if u < 2:
                    last = mm(po, pT[:, 0, 0:P], vcb[:], True, True)
                else:
                    pe.wait_ge(S["vc_in"], 16 * (NPG if u < 4 else NPG + 1))
                    vn = kvt[0:NS, TP, (VS if u < 4 else VW):(VS if u < 4 else VW) + P]
                    mm(po, pT[0:NS, 0, 2 * P:3 * P], vn, True, False, True)
                    for q in range(4):
                        b = 4 * rt + q
                        for j in range(2):
                            last = mm(ps[32 * q:32 * q + 32, 7, 0:P], pT[:, 0, j * P + 32 * q:j * P + 32 * q + 32],
                                      vcache[:, 2 * b + j, :], False, j == 1, True)
                last.then_inc(S["ss_pv"], 1)

            pe.wait_ge(S["cv_ok"], CC)
            pe.wait_ge(S["cs_out"], 1)
            pe.wait_ge(S["s_qbd"], 1)
            pe.wait_ge(S["g_ok"], 1)
            for rt in range(2):
                mm(ps[:, 7, 32 * rt:32 * rt + 24], cst[0:NS, C_SEL + rt * P:C_SEL + (rt + 1) * P], gates[0:NS, TP, :],
                   True, True).then_inc(S["g_ps"], 1)
            ss_scores(0)
            ss_scores(1)
            keys_T(0, 16 * NPG)
            ss_values(0)
            ss_scores(2)
            ss_values(1)
            ss_scores(3)
            keys_T(1, 16 * NPG + 16)
            ss_values(2)
            ss_scores(4)
            ss_values(3)
            ss_scores(5)
            ss_values(4)
            ss_values(5)
            pe.wait_ge(S["ss_o"], 6)
            for rt in range(2):
                last = T(ps[:, 5, rt * P:(rt + 1) * P], osam[:, rt, :], eye(P))
            last.then_inc(S["so_ps"], 1)
            pe.wait_ge(S["so_ok"], 1)

            for i in range(TP):
                nk = 8 * i + 7
                U, w = 2 * NH * i, P * (i + 1)

                def scores(u):
                    n, kT = (u % (2 * NH)) // 2, (ksT, kwT)[u % 2]
                    p0 = HD * (n // G)
                    if u >= 2:
                        pe.wait_ge(S["u_soft"], u - 1)
                    mm(ps[:, u % 2, 0:w], qT[p0:p0 + HD, n % G, i * P:(i + 1) * P], kT[p0:p0 + HD, 0:w],
                       True, True).then_inc(S["u_s"], 1)

                for n in range(NH):
                    p0 = HD * (n // G)
                    last = mm(ps[:, 6 + n // G, (n % G) * nk:(n % G + 1) * nk], qT[p0:p0 + HD, n % G, i * P:(i + 1) * P],
                              kcpT[p0:p0 + HD, 0:nk], True, True)
                last.then_inc(S["cm_done"], 1)
                scores(U)
                scores(U + 1)
                pe.wait_ge(S["cm_p"], i + 1)
                if i:
                    pe.wait_ge(S["ot_ok"], i)
                for n in range(NH):
                    last = T(ps[0:nk, 6 + n // 4, (n % 4) * P:(n % 4 + 1) * P], cme[:, n * nk:(n + 1) * nk], eye(P))
                last.then_inc(S["cm_tr"], 1)
                pe.wait_ge(S["cm_pT"], i + 1)
                for n in range(NH):
                    last = mm(ps[:, 4, n * HD:(n + 1) * HD], cpT[0:nk, n, :], vcp[0:nk, HD * (n // G):HD * (n // G) + HD],
                              True, True)
                last.then_inc(S["cm_pv"], 1)
                pe.wait_ge(S["cm_o"], i + 1)
                for k in range(2 * NH):
                    u = U + k
                    pe.wait_ge(S["u_exp"], u + 1)
                    if u >= 2:
                        pe.wait_ge(S["u_pT"], u - 1)
                    for j in range(i + 1):
                        last = T(ps[:, 2 + u % 2, j * P:(j + 1) * P], pr[:, u % 2, j * P:(j + 1) * P], eye(P))
                    last.then_inc(S["u_tr"], 1)
                    if k + 2 < 2 * NH:
                        scores(u + 2)
                    pe.wait_ge(S["u_pT"], u + 1)
                    if u >= 2:
                        pe.wait_ge(S["u_o"], u - 1)
                    v0 = (VS, VW)[u % 2] + HD * (k // 2 // G)
                    for j in range(i + 1):
                        last = mm(ps[:, 4 + u % 2, 0:HD], pT[:, u % 2, j * P:(j + 1) * P],
                                  kvt[:, j, v0:v0 + HD], j == 0, j == i)
                    last.then_inc(S["u_pv"], 1)
                pe.wait_ge(S["u_o"], U + 2 * NH)
                for c in range(CC):
                    last = T(ps[:, 5, c * P:(c + 1) * P], oacc[:, c * P:(c + 1) * P], eye(P))
                last.then_inc(S["ot_ps"], 1)

            def route(t):
                r = rows(t)
                token_wait = S["ht_ok"]
                pe.wait_ge(token_wait, t + 1)
                for c in range(DC):
                    last = mm(ps[0:r, 6, (NG + NE) * t:(NG + NE) * (t + 1)], xT[:, c, t * P:t * P + r], wr[:, c, :],
                              c == 0, c == DC - 1)
                last.then_inc(S["r_done"], 1)

            def next_T(t):
                pe.wait_ge(S["hn_done"], t + 1)
                if t:
                    pe.wait_ge(S["ht_ok"], t)
                token_T(t, hnt[0:rows(t), :], 4, S["ht_done"])

            pe.wait_ge(S["wout_in"], 32)
            pe.wait_ge(S["ot_ok"], TP)
            for t in range(TT):
                r = rows(t)
                if t >= 2:
                    pe.wait_ge(S["op_h"], t - 1)
                for half in range(2):
                    for c in range(DC):
                        last = mm(ps[0:r, 2 * (t % 2) + half, :], mixT[:, c, t * P:t * P + r],
                                  wout[:, c, half * 512:(half + 1) * 512], c == 0, c == DC - 1)
                last.then_inc(S["op_done"], 1)
                if t == 1:
                    pe.wait_ge(S["wr_in"], 64)
                if t:
                    next_T(t - 1)
                    route(t - 1)
            next_T(TP)
            route(TP)
            pe.wait_ge(S["asn_ok"], 1)
            for t in range(TT):
                r = rows(t)
                for s in range(t):
                    mm(ps[0:r, 7, t * NE:(t + 1) * NE], cst[:, C_ONE:C_ONE + r], asn[:, s, :], s == 0, False)
                mm(ps[0:r, 7, t * NE:(t + 1) * NE], cst[0:r, C_TRI:C_TRI + r], asn[0:r, t, :], t == 0, True)
            for s in range(TT):
                r = rows(s)
                last = mm(ps[:, 7, TT * NE:(TT + 1) * NE], cst[0:r, C_ONE:C_ONE + P], asn[0:r, s, :], s == 0, s == TP)
            last.then_inc(S["pf_done"], 1)
            pe.wait_ge(S["jei_ok"], 1)

            def rows_T(J):
                pe.wait_ge(S["gath"], J * 16 + 16)
                pe.wait_ge(S["x_lo"], J)
                pe.sem_inc(S["passed"], 1)
                v = xg[0:SLOTS, :].rearrange("r (p c) -> r p c", c=DC)
                for c in range(DC):
                    last = T(ps[:, 3, c * SLOTS:(c + 1) * SLOTS], v[:, :, c], eye(SLOTS))
                last.then_inc(S["x_tr"], 1)

            def piece(J, k):
                pe.wait_ge(S["lo_ok"], J * 6 + (k + 1))
                hw, lw = hiw[:, k % 3, :], low[:, k % 3, :]
                if k < 4:
                    for j in range(4):
                        c = 4 * (k % 2) + j
                        for n, w in enumerate((hw, lw)):
                            last = mm(ps[:, k // 2, :], xpack[:, c, :], w[:, j * 512:(j + 1) * 512],
                                      c == 0 and n == 0, c == DC - 1 and n == 1)
                else:
                    for j in range(2):
                        c = 2 * (k % 2) + j
                        for half in range(2):
                            for n, w in enumerate((hw, lw)):
                                last = mm(ps[:, 5 + half, :], hpack[:, c, :], w[:, j * D + half * 512:j * D + (half + 1) * 512],
                                          c == 0 and n == 0, c == 3 and n == 1)
                last.then_inc(S["used"], 1)

            def job(J, first):
                pe.wait_ge(S["x_lo"], J + 1)
                pe.wait_ge(S["gu_copied"], J * 2)
                piece(J, 0)
                piece(J, 1)
                piece(J, 2)
                piece(J, 3)
                rows_T(J + 1)
                pe.wait_ge(S["gu_copied"], J * 2 + 2)
                pe.wait_ge(S["hT_ok"], J * 2)
                for i in range(2):
                    v = Sg[:, i, :].rearrange("r (p c) -> r p c", c=4)
                    for c in range(4):
                        last = mm(ps[:, 2, i * 256 + c * SLOTS:i * 256 + (c + 1) * SLOTS], v[:, :, c],
                                  cst[:, C_II:C_II + SLOTS], True, True)
                last.then_inc(S["gt_done"], 1)
                pe.wait_ge(S["h_ok"], J + 1)
                pe.wait_ge(S["y_ok"], J)
                piece(J, 4)
                piece(J, 5)

            rows_T(0)
            run_jobs(pe, job)
            pe.wait_ge(S["wpg_in"], 80)
            pe.wait_ge(S["y_out"], total(pe) * 16)
            for t in range(TT):
                r = rows(t)
                if t:
                    pe.wait_ge(S["f_plT"], t)
                v = pin[0:r, t, :].rearrange("r (p c) -> r p c", c=2)
                for c in range(2):
                    last = T(ps[:, 6, c * P:c * P + r], v[:, :, c], eye(r))
                last.then_inc(S["f_tr"], 1)
                pe.wait_ge(S["f_plT"], t + 1)
                if t:
                    pe.wait_ge(S["f_o"], t)
                for half in range(2):
                    for c in range(2):
                        last = mm(ps[0:r, 4 + half, :], plT[:, c, 0:r], wple[:, c, half * 512:(half + 1) * 512], c == 0, c == 1)
                last.then_inc(S["f_mm"], 1)
                pe.wait_ge(S["f_hn"], t + 1)
                token_T(t, h2n[0:r, :], 0, S["f_tr"])
                pe.wait_ge(S["f_hpT"], t + 1)
                for half in range(2):
                    for c in range(DC):
                        last = mm(ps[0:r, 2 + half, :], hpT[:, c, 0:r], wpg[:, c, half * 512:(half + 1) * 512], c == 0, c == DC - 1)
                last.then_inc(S["f_mm"], 1)

        @block.vector
        def _(dve):
            chain = Chain(dve, S["dve_chain"])
            V = nc.vector
            TTn, TS, STT = V.tensor_tensor, V.tensor_scalar, V.scalar_tensor_tensor

            roots = []

            def rms(x):
                roots.append(1)
                dve.wait_ge(S["root_ok"], len(roots))
                chain(V.reciprocal(x, x))

            def both(b, r=P):
                return ps[0:r, b:b + 2, :].rearrange("p k n -> p (k n)")

            V.memset(gates[:], 0.0)
            V.memset(eps[:], EPS).then_inc(S["eps_ok"], 1)
            dve.wait_ge(S["rb_in"], 64)
            V.memset(SM[NBUCK:NBUCK + 1, 0:NH], -BIG).then_inc(S["rb_ok"], 1)
            for t in range(TT):
                r = rows(t)
                rms(rn[0:r, t:t + 1])
                if t >= 2:
                    dve.wait_ge(S["xT_t"], t - 1)
                TS(xn[0:r, t % 2, :], h[0:r, t, :], rn[0:r, t:t + 1], None, ALU.mult).then_inc(S["xn_done"], 1)
                if t == 0:
                    dve.wait_ge(S["vec_in"], 16 * 11)
                    chain(TS(gq[:], gq[:], HD ** -0.5, None, ALU.mult))
                    dve.wait_ge(S["cv_vec"], 1)
                    V.tensor_copy(cwT[:], ps[:, 5, 0:12])
                    V.tensor_copy(upst[:], ps[:, 5, 16:80].rearrange("p (c n) -> p c n", c=CC)).then_inc(S["cv_vecc"], 1)
                if t:
                    token_cols(dve, S["xT_t"], t - 1, gmix, 2 * ((t - 1) % 2), S["xT_ok"])
            token_cols(dve, S["xT_t"], TP, gmix, 2 * (TP % 2), S["xT_ok"])

            dve.wait_ge(S["cv_vecc"], 1)
            V.memset(cmb[:], -BIG)
            V.memset(nmk[:], -BIG)
            V.memset(upp[:, 0:2], 0.0)
            chain(V.memset(Qbd[:], 0.0))

            for t in range(TT):
                r = rows(t)
                dve.wait_ge(S["kv_copied"], t + 1)
                q = qn[0:r, t % 2, :]
                kk = kvt[0:r, t, KS:KW + P].rearrange("p (i n) -> p i n", n=P)[:, 0:3:2, :]
                TTn(sq[0:r, 0:512], q, q, ALU.mult)
                chain(TTn(sq[0:r, 512:768].rearrange("p (i n) -> p i n", n=P), kk, kk, ALU.mult))
                V.reduce_sum(ss12[0:r, :], sq[0:r, 0:768].rearrange("p (k d) -> p k d", d=HD), axis=X).then_inc(S["ss_sum"], 1)
                rms(ss12[0:r, :])
                r8 = ss12[0:r, 0:NH].unsqueeze(2).broadcast_to([r, NH, HD])
                TTn(q.rearrange("p (k d) -> p k d", d=HD), q.rearrange("p (k d) -> p k d", d=HD), r8, ALU.mult)
                for i, c0 in enumerate((KS, KW)):
                    x = kvt[0:r, t, c0:c0 + P]
                    r2 = ss12[0:r, NH + 2 * i:NH + 2 * i + 2].unsqueeze(2).broadcast_to([r, NKV, HD])
                    x3 = x.rearrange("p (k d) -> p k d", d=HD)
                    chain(TTn(x3, x3, r2, ALU.mult))
                    last = TTn(x, x, gk[0:r, i, :], ALU.mult)
                last.then_inc(S["tm_norm"], 1)
                dve.wait_ge(S["tr_done"], t + 1)
                V.tensor_copy(ksT[:, t * P:t * P + r], ps[:, 7, 0:r])
                V.tensor_copy(kwT[:, t * P:t * P + r], ps[:, 7, P:P + r]).then_inc(S["tr_k"], 1)

            dve.wait_ge(S["tr_q"], TT)
            for hh in range(NKV):
                p0 = hh * HD
                last = V.tensor_copy(Qbd[p0:p0 + HD, :, 16 * hh:16 * hh + 16].rearrange("p b (g t) -> p b g t", g=G),
                                     qT[p0:p0 + HD, :, SEQ:N].rearrange("p g (b t) -> p b g t", b=NB))
            last.then_inc(S["s_qbd"], 1)

            def compress_dve(i):
                for pp in range(8):
                    dve.wait_ge(S["X_tr"], 8 * i + pp + 1)
                    if i and pp == 0:
                        dve.wait_ge(S["hid_done"], 2)
                    V.tensor_copy(XT[:, pp, :], ps[:, pp % 4, 0:2 * XC]).then_inc(S["X_ev"], 1)
                dve.wait_ge(S["hid_done"], 2 * i + 2)
                if i:
                    dve.wait_ge(S["hid_gelu"], 2)
                V.tensor_copy(hb[:], ps[:, 4:6, XC - 2]).then_inc(S["hid_b"], 1)

            def keys_norm():
                V.tensor_copy(kcb, ps[:, 6, 0:P])
                chain(V.tensor_copy(kcp[0:NCP, :], ps[0:NCP, 7, 0:P]))
                for x, r in ((kcb, P), (kcp, NCP)):
                    chain(TTn(nsq[0:r, :], x[0:r, :], x[0:r, :], ALU.mult))
                    V.reduce_sum(ss12[0:r, 0:2], nsq[0:r, :].rearrange("p (k d) -> p k d", d=HD), axis=X).then_inc(S["ss_sum"], 1)
                    rms(ss12[0:r, 0:2])
                    x3 = x[0:r, :].rearrange("p (k d) -> p k d", d=HD)
                    last = TTn(x3, x3, ss12[0:r, 0:2].unsqueeze(2).broadcast_to([r, NKV, HD]), ALU.mult)
                    if r == P:
                        chain(last)
                last.then_inc(S["cb_ok"], 1)

            def conv_dve(c4):
                dve.wait_ge(S["cv_xh"], c4 + 1)
                if c4 == 0:
                    dve.wait_ge(S["bl_out"], 16)
                NH2 = N // 2
                V.tensor_copy(ups[:, :, 0:2], upst[:, c4, :].rearrange("p (b k) -> p b k", k=2))
                TTn(upp[:, 2:2 + NH2], ps[:, 4, 0:NH2], sq[:, 0:NH2], ALU.mult)
                TTn(upp[:, 2 + NH2:2 + SEQ], ps[:, 5, 0:SEQ - NH2], sq[:, NH2:SEQ], ALU.mult)
                chain(TTn(ups[:, :, 2:6], ps[:, 5, SEQ - NH2:NH2].rearrange("p (b t) -> p b t", t=NT),
                          sq[:, SEQ:N].rearrange("p (b t) -> p b t", t=NT), ALU.mult))
                dve.sem_inc(S["cv_u"], 1)
                V.tensor_copy(cs_in[:, c4, 0:2], upp[:, SEQ:SEQ + 2])
                V.tensor_copy(cs_in[:, c4, 2:18].rearrange("p (b k) -> p b k", k=2), ups[:, :, NT:NT + 2])
                yp, ysm = mixT[:, c4, 0:SEQ], mixT[:, c4, SEQ:N].rearrange("p (b t) -> p b t", t=NT)
                TS(yp, upp[:, 0:SEQ], cwT[:, c4:c4 + 1], None, ALU.mult)
                chain(TS(ysm, ups[:, :, 0:NT], cwT[:, c4:c4 + 1], None, ALU.mult))
                for k in (1, 2):
                    w = cwT[:, CC * k + c4:CC * k + c4 + 1]
                    STT(yp, upp[:, k:k + SEQ], w, yp, ALU.mult, ALU.add)
                    chain(STT(ysm, ups[:, :, k:k + NT], w, ysm, ALU.mult, ALU.add))
                TTn(mixT[:, c4, 0:NH2], mixT[:, c4, 0:NH2], ps[:, 2, 0:NH2], ALU.mult)
                chain(TTn(mixT[:, c4, NH2:N], mixT[:, c4, NH2:N], ps[:, 3, 0:NH2], ALU.mult))
                dve.sem_inc(S["cv_ok"], 1)

            compress_dve(0)
            dve.wait_ge(S["cb_done"], 1)
            keys_norm()
            conv_dve(0)
            dve.wait_ge(S["ct_done"], 1)
            TS(kcbT[:], ps[:, 6, 256:256 + NCH], gk0[:, 0:1], None, ALU.mult)
            TS(kcpT[:, 0:NCP], ps[:, 6, 384:384 + NCP], gk0[:, 0:1], None, ALU.mult).then_inc(S["ct_ok"], 1)
            conv_dve(1)
            compress_dve(1)
            dve.wait_ge(S["cb_done"], 2)
            V.tensor_copy(vcb[:], ps[:, 6, 0:P])
            V.tensor_copy(vcp[0:NCP, :], ps[0:NCP, 7, 0:P]).then_inc(S["cb_ok"], 1)
            conv_dve(2)
            conv_dve(3)
            dve.wait_ge(S["SM_in"], 16 * 4 * NH)
            for b in range(NB):
                q0, rt = 32 * (b % 4), b // 4
                V.tensor_copy(cmb[q0:q0 + 32, rt, CS * b:CS * b + CS - 1],
                              SM[q0:q0 + 32, 2 * STRIDE - 1:2 * STRIDE - 1 + STRIDE * (CS - 2) + 1:STRIDE])
                V.tensor_copy(nmk[q0:q0 + 32, rt, NT * b:NT * b + NT], SM[q0:q0 + 32, PAST:PAST + NT])
            dve.wait_ge(S["cs_ps"], 1)
            chain(V.tensor_copy(cs_out[:], ps[0:18, 7, :]))
            dve.sem_inc(S["cs_out"], 1)

            def ss_soft(u):
                rt = u % 2
                dve.wait_ge(S["ss_done"], u + 1)
                if u >= 2:
                    dve.wait_ge(S["ss_exp"], u - 1)
                if u < 2:
                    V.tensor_tensor_reduce(sc[:, rt, 0:NCH], ps[:, 4 + rt, 0:NCH], cmb[:, rt, :], -1.0, BIG, ALU.add, ALU.min,
                                           st[:, u:u + 1]).then_inc(S["ss_soft"], 1)
                else:
                    w = PAST + NS
                    V.tensor_tensor_reduce(sc[:, rt, 0:PAST], ps[:, 4 + rt, 0:PAST], SM[:, 0:PAST], -1.0, BIG, ALU.add, ALU.min,
                                           st[:, u:u + 1])
                    chain(V.tensor_tensor_reduce(sc[:, rt, PAST:w], ps[:, 4 + rt, PAST:w], nmk[:, rt, :], -1.0, BIG, ALU.add,
                                                 ALU.min, st[:, 32 + u:33 + u]))
                    TTn(st[:, u:u + 1], st[:, u:u + 1], st[:, 32 + u:33 + u], ALU.min).then_inc(S["ss_soft"], 1)

            def ss_out(u):
                rt, br_ = u % 2, u // 2
                dve.wait_ge(S["ss_tr"], u + 1)
                if u:
                    dve.wait_ge(S["ss_pv"], u)
                if u < 2:
                    V.tensor_copy(pT[:, 0, 0:P], ps[:, 6, 0:P]).then_inc(S["ss_pT"], 1)
                else:
                    V.tensor_copy(pT[:, 0, 0:2 * P], ps[:, 6, 0:2 * P])
                    V.tensor_copy(pT[0:NS, 0, 2 * P:3 * P], ps[0:NS, 6, 2 * P:3 * P]).then_inc(S["ss_pT"], 1)
                chain(TS(st[:, 24:25], st[:, 8 + u:9 + u], 1e-30, None, ALU.max))
                chain(V.reciprocal(st[:, 24:25], st[:, 24:25]))
                chain(TTn(st[:, 24:25], st[:, 24:25], gs[:, rt, br_:br_ + 1], ALU.mult))
                chain(TS(st[:, 26:28], cst[:, C_HM:C_HM + NKV], st[:, 24:25], None, ALU.mult))
                dve.wait_ge(S["ss_pv"], u + 1)
                for hh in range(NKV):
                    if br_ == 0 and hh == 0:
                        chain(TS(osam[:, rt, 0:HD], ps[:, 7, 0:HD], st[:, 26:27], None, ALU.mult))
                    else:
                        chain(STT(osam[:, rt, 0:HD], ps[:, 7, hh * HD:(hh + 1) * HD], st[:, 26 + hh:27 + hh],
                                  osam[:, rt, 0:HD], ALU.mult, ALU.add))
                if br_ == NBR - 1:
                    chain(V.tensor_copy(osam[:, rt, HD:P], osam[:, rt, 0:HD]))
                dve.sem_inc(S["ss_o"], 1)

            dve.wait_ge(S["g_exp"], 1)
            chain(TS(gates[:], gates[:], 1.0, None, ALU.add))
            V.reciprocal(gates[:], gates[:]).then_inc(S["g_ok"], 1)
            for rt in range(2):
                dve.wait_ge(S["g_ps"], 2)
                chain(TTn(g24.rearrange("p (n k) -> p n k", k=NBR),
                          ps[:, 7, 32 * rt:32 * rt + 24].rearrange("p (n k) -> p n k", k=NBR),
                          cst[:, C_NM:C_NM + NH].unsqueeze(2).broadcast_to([P, NH, NBR]), ALU.mult))
                chain(V.reduce_sum(gs[:, rt, :], g24.rearrange("p (n k) -> p k n", k=NBR), axis=X))
            dve.sem_inc(S["s_qbd"], 1)
            ss_soft(0)
            ss_soft(1)
            for b in range(4):
                dve.wait_ge(S["kt_done"], b + 1)
                V.tensor_copy(kcT[:, 4 * b:4 * b + 4, :].rearrange("p g n -> p (g n)"), ps[:, b, :]).then_inc(S["kt_ok"], 1)
            ss_out(0)
            ss_soft(2)
            ss_out(1)
            ss_soft(3)
            for b in range(4):
                dve.wait_ge(S["kt_done"], b + 5)
                dve.wait_ge(S["ss_done"], 4)
                V.tensor_copy(kcT[:, 4 * b:4 * b + 4, :].rearrange("p g n -> p (g n)"), ps[:, b, :]).then_inc(S["kt_ok"], 1)
            ss_out(2)
            ss_soft(4)
            ss_out(3)
            ss_soft(5)
            ss_out(4)
            ss_out(5)
            dve.wait_ge(S["so_ps"], 1)
            dve.wait_ge(S["yz_out"], 16 * (MAXOV * SLOTS // P))
            for n in range(NH):
                p0 = HD * (n % 2)
                last = V.tensor_copy(
                    mixT[p0:p0 + HD, CC + n // 2, SEQ:N].rearrange("p (b t) -> p b t", t=NT),
                    ps[p0:p0 + HD, 5, 0:2 * P].rearrange("p (b n t) -> p b n t", n=NH, t=NT)[:, :, n, :])
            last.then_inc(S["so_ok"], 1)

            dve.wait_ge(S["M_in"], 16 * NH)
            for i in range(TP):
                nk = 8 * i + 7
                U, w = 2 * NH * i, P * (i + 1)
                x0 = 512 - P * (i + 1)

                def soft(u):
                    n = (u % (2 * NH)) // 2
                    dve.wait_ge(S["u_s"], u + 1)
                    if u >= 2:
                        dve.wait_ge(S["u_exp"], u - 1)
                    V.tensor_tensor_reduce(sc[:, u % 2, 0:w], ps[:, u % 2, 0:w], M[:, n, x0:512], -1.0, BIG, ALU.add, ALU.min,
                                           st[:, 16 + u % 4:17 + u % 4]).then_inc(S["u_soft"], 1)

                c3 = cms[:, 0:NH * nk].rearrange("p (h n) -> p h n", h=NH)
                e3 = cme[:, 0:NH * nk].rearrange("p (h n) -> p h n", h=NH)
                off = x0 + 2 * STRIDE - 1
                dve.wait_ge(S["cm_done"], i + 1)
                chain(TTn(c3.rearrange("p (b g) n -> p b g n", b=NKV),
                          ps[:, 6:8, 0:G * nk].rearrange("p b (g n) -> p b g n", g=G),
                          M[:, :, off:off + STRIDE * (nk - 1) + 1:STRIDE].rearrange("p (b g) n -> p b g n", b=NKV), ALU.add))
                chain(V.tensor_reduce(st[:, 32:40], c3, X, ALU.max))
                chain(TS(st[:, 32:40], st[:, 32:40], -0.1 * BIG, None, ALU.max))
                TTn(c3, c3, st[:, 32:40].unsqueeze(2).broadcast_to([P, NH, nk]), ALU.subtract).then_inc(S["cm_sub"], 1)
                soft(U)
                soft(U + 1)
                dve.wait_ge(S["cm_exp"], i + 1)
                gt = gates[:, i, :].rearrange("p (h k) -> p h k", k=NBR)
                chain(V.reduce_sum(st[:, 32:40], e3, axis=X))
                chain(TS(st[:, 32:40], st[:, 32:40], 1e-30, None, ALU.max))
                chain(V.reciprocal(st[:, 32:40], st[:, 32:40]))
                chain(TTn(st[:, 32:40], st[:, 32:40], gt[:, :, 0], ALU.mult))
                TTn(e3, e3, st[:, 32:40].unsqueeze(2).broadcast_to([P, NH, nk]), ALU.mult).then_inc(S["cm_p"], 1)
                dve.wait_ge(S["cm_pv"], i + 1)
                if i:
                    dve.wait_ge(S["ot_ps"], i)
                chain(V.tensor_copy(oacc[:], ps[:, 4, :]))
                dve.sem_inc(S["cm_o"], 1)
                for k in range(2 * NH):
                    u, n = U + k, k // 2
                    if k + 2 < 2 * NH:
                        soft(u + 2)
                    dve.wait_ge(S["u_exp"], u + 1)
                    coef = st[:, 28 + u % 4:29 + u % 4]
                    chain(TS(coef, st[:, 20 + u % 4:21 + u % 4], 1e-30, None, ALU.max))
                    chain(V.reciprocal(coef, coef))
                    chain(TTn(coef, coef, gates[:, i, NBR * n + 1 + k % 2:NBR * n + 2 + k % 2], ALU.mult))
                    dve.wait_ge(S["u_pv"], u + 1)
                    if k % 2:
                        dve.wait_ge(S["u_o"], u)
                    STT(oacc[:, n * HD:(n + 1) * HD], ps[:, 4 + u % 2, 0:HD], coef,
                        oacc[:, n * HD:(n + 1) * HD], ALU.mult, ALU.add).then_inc(S["u_o"], 1)
                dve.wait_ge(S["ot_ps"], i + 1)
                V.tensor_copy(mixT[:, CC:DC, i * P:(i + 1) * P], ps[:, 5, :].rearrange("p (c n) -> p c n", c=CC))\
                    .then_inc(S["ot_ok"], 1)

            dve.wait_ge(S["wout_in"], 32)
            for t in range(TT):
                r = rows(t)
                dve.wait_ge(S["op_done"], t + 1)
                TTn(h[0:r, t, :], h[0:r, t, :], both(2 * (t % 2), r), ALU.add).then_inc(S["op_h"], 1)
                if t:
                    token_cols(dve, S["ht_done"], t - 1, None, 4, S["ht_ok"])
                rms(rn[0:r, t:t + 1])
                if t:
                    dve.wait_ge(S["hn_out"], 16 * t)
                STT(hnt[0:r, :], h[0:r, t, :], rn[0:r, t:t + 1], gffn[0:r, :], ALU.mult, ALU.mult).then_inc(S["hn_done"], 1)
            token_cols(dve, S["ht_done"], TP, None, 4, S["ht_ok"])

            dve.wait_ge(S["wr_in"], 64)
            V.memset(zslot[:], 0).then_inc(S["z_ok"], 1)
            chain(V.memset(lg[:], 0.0))
            dve.wait_ge(S["r_done"], TT)
            W = NG + NE
            for t in range(TT):
                r = rows(t)
                chain(TTn(lg[0:r, t, :], ps[0:r, 6, W * t:W * (t + 1)], br[0:r, :], ALU.add))

            def spread(x, n):
                return x.unsqueeze(2).broadcast_to([P, TT, n])

            def first_max(hot, x, m, n, tmp):
                chain(V.tensor_reduce(m, x, X, ALU.max))
                chain(TTn(tmp, x, spread(m, n), ALU.is_ge))
                desc = cst[:, C_DESC:C_DESC + n].unsqueeze(1).broadcast_to([P, TT, n])
                chain(TTn(tmp, tmp, desc, ALU.mult))
                chain(V.tensor_reduce(rs[:, 7, :], tmp, X, ALU.max))
                chain(TTn(hot, tmp, spread(rs[:, 7, :], n), ALU.is_equal))

            lgg = lg[:, :, 0:NG]
            first_max(og[:], lgg, rs[:, 0, :], NG, tg[:])
            TTn(tg[:], lgg, spread(rs[:, 0, :], NG), ALU.subtract).then_inc(S["r_log"], 1)
            chain(TS(og[:], og[:], 1.0, BIG, ALU.subtract, ALU.mult))
            for t in range(TT):
                chain(TTn(le[:, t, :].rearrange("p (g e) -> p g e", e=EG), lg[:, t, NG:W].rearrange("p (g e) -> p g e", e=EG),
                          og[:, t, :].unsqueeze(2).broadcast_to([P, NG, EG]), ALU.add))
            first_max(oh1[:], le[:], rs[:, 1, :], NE, t32[:])
            chain(TS(t32[:], oh1[:], -3.0 * BIG, None, ALU.mult))
            chain(TTn(le[:], le[:], t32[:], ALU.add))
            first_max(oh2[:], le[:], rs[:, 2, :], NE, t32[:])
            TTn(asn[:], oh1[:], oh2[:], ALU.add).then_inc(S["asn_ok"], 1)
            TTn(rs[:, 4, :], rs[:, 2, :], rs[:, 1, :], ALU.subtract).then_inc(S["r_e2"], 1)
            dve.wait_ge(S["r_exp"], 1)
            chain(V.reduce_sum(rs[:, 3, :], tg[:], axis=X))
            dve.wait_ge(S["r_w2"], 1)
            chain(TS(rs[:, 6, :], rs[:, 5, :], 1.0, None, ALU.add))
            chain(TTn(rs[:, 6, :], rs[:, 6, :], rs[:, 3, :], ALU.mult))
            chain(V.reciprocal(wts[:, 0, :], rs[:, 6, :]))
            chain(TTn(wts[:, 1, :], wts[:, 0, :], rs[:, 5, :], ALU.mult))
            dve.wait_ge(S["pf_done"], 1)
            cnt, nov, end, beg = (ovs[:, k, :] for k in range(4))
            chain(V.tensor_copy(cnt, ps[:, 7, TT * NE:(TT + 1) * NE]))
            chain(TS(nov, cnt, float(SLOTS), None, ALU.is_gt))
            for k in range(2, OVMAX + 1):
                chain(STT(nov, cnt, float(SLOTS * k), nov, ALU.is_gt, ALU.add))
            chain(V.tensor_tensor_scan(end, cst[:, C_ONE:C_ONE + NE], nov, 0.0, ALU.mult, ALU.add))
            chain(TTn(beg, end, nov, ALU.subtract))
            jv = cst[:, C_EID:C_EID + MAXOV].unsqueeze(2).broadcast_to([P, MAXOV, NE])
            ev = cst[:, C_EID:C_EID + NE].unsqueeze(1).broadcast_to([P, MAXOV, NE])
            chain(TTn(jex[:], jv, beg.unsqueeze(1).broadcast_to([P, MAXOV, NE]), ALU.is_ge))
            chain(TTn(jey[:], jv, end.unsqueeze(1).broadcast_to([P, MAXOV, NE]), ALU.is_lt))
            chain(TTn(jex[:], jex[:], jey[:], ALU.mult))
            chain(TTn(jex[:], jex[:], ev, ALU.mult))
            chain(V.reduce_sum(jef[:, 0:MAXOV], jex[:], axis=X))
            chain(V.tensor_copy(jef[:, MAXOV:MAXOV + 1], end[:, NE - 1:NE]))
            V.tensor_copy(jei[:], jef[:]).then_inc(S["jei_ok"], 1)
            chain(TS(beg, beg, float(SLOTS), float(SLOTS * (NE - 1)), ALU.mult, ALU.add))
            chain(STT(beg, cst[:, C_EID:C_EID + NE], -float(SLOTS), beg, ALU.mult, ALU.add))
            chain(V.memset(slot[:], 0.0))
            chain(V.memset(t32[:], 0.0))
            for t in range(TT):
                r = rows(t)
                V.tensor_copy(slot[0:r, t, :], ps[0:r, 7, t * NE:(t + 1) * NE])
                chain(STT(t32[0:r, t, :], ps[0:r, 7, t * NE:(t + 1) * NE], float(SLOTS), beg[0:r, :], ALU.is_ge, ALU.mult))
                chain(TTn(slot[0:r, t, :], slot[0:r, t, :], t32[0:r, t, :], ALU.add))
                chain(STT(slot[0:r, t, :], cst[0:r, C_EID:C_EID + NE], float(SLOTS), slot[0:r, t, :], ALU.mult, ALU.add))
            for k, oh in enumerate((oh1, oh2)):
                chain(TTn(t32[:], oh[:], slot[:], ALU.mult))
                chain(V.reduce_sum(rs[:, 6 + k, :], t32[:], axis=X))
            chain(V.tensor_copy(dst[:], rs[:, 6:8, :]))
            dve.sem_inc(S["dst_ok"], 1)

            def low_part(J, k):
                dve.wait_ge(S["hi_ok"], J * 6 + (k + 1))
                TTn(low[:, k % 3, :], raw[:, k, :], hiw[:, k % 3, :].bitcast(F32), ALU.subtract).then_inc(S["lo_ok"], 1)

            def x_low(J):
                dve.wait_ge(S["x_hi"], J + 1)
                TTn(xpack[:, :, SLOTS:2 * SLOTS], ps[:, 3, :].rearrange("p (c s) -> p c s", s=SLOTS),
                    xpack[:, :, 0:SLOTS].bitcast(F32), ALU.subtract).then_inc(S["x_lo"], 1)

            def y_add(J):
                dve.wait_ge(S["ylo_ok"], J)
                dve.wait_ge(S["ysb_free"], J)
                TTn(ysb[0:SLOTS, :], both(5, SLOTS), ylo[0:SLOTS, :], ALU.add).then_inc(S["y_ok"], 1)

            def job(J, first):
                low_part(J, 0)
                low_part(J, 1)
                if not first:
                    y_add(J)
                for k in range(2, 6):
                    low_part(J, k)
                dve.wait_ge(S["silu_ok"], J + 1)
                dve.wait_ge(S["used"], J * 6 + 3)
                TTn(hT32[:].rearrange("p c s -> p (c s)"), sg[:], ps[:, 2, 256:512], ALU.mult).then_inc(S["hT_ok"], 1)
                dve.wait_ge(S["hT_ok"], J * 2 + 1)
                V.tensor_copy(hpack[:, :, 0:SLOTS], hT32[:]).then_inc(S["hT_ok"], 1)
                dve.wait_ge(S["hT_ok"], J * 2 + 2)
                TTn(hpack[:, :, SLOTS:2 * SLOTS], hT32[:], hpack[:, :, 0:SLOTS].bitcast(F32), ALU.subtract).then_inc(S["h_ok"], 1)
                x_low(J + 1)

            x_low(0)
            run_jobs(dve, job)
            y_add(total(dve))

            dve.wait_ge(S["wpg_in"], 80)
            for t in range(TT):
                r = rows(t)
                dve.wait_ge(S[f"ya{t % 2}"], 32 * (t // 2 + 1))
                chain(STT(h[0:r, t, :], yga[0:r, t % 2, 0, :], wts[0:r, 0, t:t + 1], h[0:r, t, :], ALU.mult, ALU.add))
                STT(h[0:r, t, :], yga[0:r, t % 2, 1, :], wts[0:r, 1, t:t + 1], h[0:r, t, :], ALU.mult, ALU.add)\
                    .then_inc(S["f_h2"], 1)
                rms(rn[0:r, t:t + 1])
                TS(h2n[0:r, :], h[0:r, t, :], rn[0:r, t:t + 1], None, ALU.mult).then_inc(S["f_hn"], 1)
                dve.wait_ge(S["f_tr"], 2 * t + 2)
                TTn(hpT[:, :, 0:r], ps[:, 0:2, :].rearrange("p k (c n) -> p (k c) n", n=P)[:, :, 0:r],
                    gple[:].unsqueeze(2).broadcast_to([P, DC, r]), ALU.mult).then_inc(S["f_hpT"], 1)
                dve.wait_ge(S["f_mm"], 2 * t + 2)
                TTn(h2n[0:r, :], both(2, r), bpg[0:r, :], ALU.add).then_inc(S["f_z"], 1)
                dve.wait_ge(S["f_exp"], t + 1)
                chain(TS(sgt[0:r, :], sgt[0:r, :], 1.0, None, ALU.add))
                chain(V.reciprocal(sgt[0:r, :], sgt[0:r, :]))
                chain(TTn(sgt[0:r, :], both(4, r), sgt[0:r, :], ALU.mult))
                if t >= 2:
                    dve.wait_ge(S[f"f_out{t % 2}"], 16 * (t // 2))
                TTn(yo[0:r, t % 2, :], h[0:r, t, :], sgt[0:r, :], ALU.add).then_inc(S["f_o"], 1)


def kernel(**inputs):
    import concourse.bacc as _bacc
    from concourse.bass_utils import run_bass_kernel_spmd as _run

    nc = _bacc.Bacc("TRN2", target_bir_lowering=False, num_devices=1)
    consts, buckets, tok = constants()
    shapes = {
        "x_prompt": (SEQ, D), "x_sample": (NS, D), "p_prompt": (SEQ, PLE), "p_sample": (NS, PLE),
        "state_conv": (NB * 2, CONV), "page_table": (NB, PAST // PAGE), "conv_w": (3, CONV),
        "q_norm": (HD,), "k_norm": (NBR, HD), "norm_mix": (D,), "norm_ffn": (D,), "norm_ple": (D,), "b_ple_gate": (D,),
        "b_router_group": (NG,), "b_router_expert": (NE,), "rel_bias": (NBUCK, NH),
        "cache_k_win": (NB, PAST, P), "cache_v_win": (NB, PAST, P),
    }
    arrays, a, o = {}, {}, {}

    def put(name, x):
        arrays[f"in_{name}"] = x
        a[name] = nc.dram_tensor(f"in_{name}", x.shape, mybir.dt.from_np(x.dtype), kind="ExternalInput").ap()

    for name, x in inputs.items():
        x = np.ascontiguousarray(x)
        if name in shapes:
            x = x.reshape(shapes[name])
        elif name.startswith("cache_"):
            x = x.reshape(x.shape[1], PAGE, P)
        else:
            x = x.reshape(x.shape[1:])
        put(name, x)
    put("consts", consts)
    put("buckets", buckets)
    put("tok", tok)
    kv = ("k_cmp", "v_cmp", "k_slc", "v_slc", "k_win", "v_win")
    outs = [("y_prompt", (SEQ, D), (1, SEQ, D)), ("y_sample", (NS, D), (NB, NT, D))]
    outs += [(n + "_p", (SEQ, P), (1, 1, SEQ, NKV, HD)) for n in kv]
    outs += [("conv_p", (2, CONV), (1, 1, 2, CONV))]
    outs += [(n + "_s", (NS, P), (1, NB, NT, NKV, HD)) for n in kv[:4]]
    outs += [(n + "_s", (NB, PAST, P), (1, NB, PAST, NKV, HD)) for n in kv[4:]]
    outs += [("conv_s", (NB * 2, CONV), (1, NB, 2, CONV))]
    for name, shape, _ in outs:
        o[name] = nc.dram_tensor(f"out_{name}", shape, F32, kind="ExternalOutput").ap()
    build(nc, a, o)
    r = _run(nc, [arrays], core_ids=[0])
    return tuple(r.results[0][f"out_{name}"].reshape(full) for name, _, full in outs)
```

```python
from contextlib import ExitStack

import numpy as np
import concourse.bass as bass
from concourse import mybir

F32 = mybir.dt.float32
F32R = mybir.dt.float32r
I32 = mybir.dt.int32
U32 = mybir.dt.uint32
ALU = mybir.AluOpType
ACT = mybir.ActivationFunctionType
X = mybir.AxisListType.X

P = 128
D = 1024
DC = D // P
SEQ, NB, NT = 512, 8, 4
NS = NB * NT
N = SEQ + NS
TP = SEQ // P
TT = TP + 1
CONV, HD, NH, NKV = 512, 64, 8, 2
G = NH // NKV
CC = CONV // P
PAST, PAGE = 256, 128
NPG = NB * PAST // PAGE
STRIDE = 16
NCP = SEQ // STRIDE - 1
CS = PAST // STRIDE
NCH = NB * CS
XC = NCH + SEQ // STRIDE + 2
CH = 256
NBR = 3
NE, NG, DE = 32, 4, 512
EG = NE // NG
SLOTS = 64
MAXOV = (2 * N - 1) // SLOTS
JOBS = NE + MAXOV + 1
OVMAX = (N - 1) // SLOTS
PLE = 256
EPS = 1e-6
BIG = 1e30
NBUCK = 32
BREF = 511
BL = 640
KEYS_S = PAST + NT
KC, VC, KS, VS, KW, VW = [i * P for i in range(6)]

C_ID, C_TRI, C_ONE, C_II, C_DESC, C_EID, C_NM, C_HM, C_SEL, C_END = np.cumsum(
    [0, P, P, P, SLOTS, NE, NE, NH, NKV, 2 * P]).tolist()


def rows(t):
    return P if t < TP else NS


def constants():
    c = np.zeros((P, C_END), np.float32)
    i = np.arange(P)
    c[:, C_ID:C_TRI] = np.eye(P)
    c[:, C_TRI:C_ONE] = i[:, None] < i[None, :]
    c[:, C_ONE:C_II] = 1.0
    c[:, C_II:C_DESC] = (i[:, None] % SLOTS) == np.arange(SLOTS)[None, :]
    c[:, C_DESC:C_EID] = NE - np.arange(NE)
    c[:, C_EID:C_NM] = np.arange(NE)
    head = (i % 32) // NT
    c[:, C_NM:C_HM] = head[:, None] == np.arange(NH)
    c[:, C_HM:C_SEL] = (head // G)[:, None] == np.arange(NKV)
    for rt in range(2):
        tok = (rt * 4 + i // 32) * NT + i % NT
        c[:NS, C_SEL + rt * P:C_SEL + (rt + 1) * P] = np.arange(NS)[:, None] == tok[None, :]
    dist = BREF - np.arange(BL)
    n = np.maximum(dist, 0)
    exact = NBUCK // 2
    nf = np.maximum(n, 1).astype(np.float32)
    large = exact + (np.log(nf / np.float32(exact)) / np.float32(np.log(128 / exact))
                     * np.float32(NBUCK - exact)).astype(np.int32)
    bucket = np.where(n < exact, n, np.minimum(large, NBUCK - 1))
    b = np.zeros((NBUCK + 1, BL), np.float32)
    b[bucket, np.arange(BL)] = 1.0
    b[NBUCK] = dist < 0
    tok = np.zeros((P, TT), np.int32)
    for t in range(TT):
        tok[:, t] = t * P + i
    tok[NS:, TP] = 0
    return c, b, tok


class Chain:

    def __init__(self, eng, sem):
        self.eng, self.sem, self.n = eng, sem, 0

    def __call__(self, ins):
        self.n += 1
        ins.then_inc(self.sem, 1)
        self.eng.wait_ge(self.sem, self.n)


SEMS = """
M_in SM_in X_ev X_in X_tr asn_ok bl_out bl_ps bl_sb cb_done cb_ok cm_done cm_exp cm_o cm_p cm_pT
cm_pv cm_sub cm_tr cs_out cs_outd cs_ps cst_in ct_done ct_ok cv_done cv_ok cv_u cv_vec cv_vecc cv_xh
dst_ok dve_chain eps_ok f_h2 f_hn f_hpT f_mm f_o f_out0 f_out1 f_pl f_ple f_sig f_tr f_z g_exp g_ok
g_ps gath gt_done gu_copied hT_ok h_ok hi_ok hid_b hid_done hid_gelu hn_done hn_out ht_done ht_ok
ic_ok idx_in jei_ok kc_in kcmp_out kt_done kt_ok kv_copied kvout lo_ok op_done op_h ot_ok ot_ps
passed pf_done ple_in pt_in r_done r_e2 r_exp r_log raw0 raw1 raw2 raw3 raw4 raw5 rb_in rb_ok
root_ok s_qbd sc_out silu_ok so_ok so_ps sq_done ss_done ss_exp ss_o ss_pT ss_pv ss_soft ss_sum
ss_tr tm_done tm_norm tr_done tr_k tr_q u_exp u_o u_pT u_pv u_s u_soft u_tr used vc_in vcmp_out
vec_in w1_in w2_in wc0 wc1 wc2 wc3 winout wout_in wpg_in wq0 wq1 wr_in x0_in x1_in x2_in x3_in x4_in
xT_ok xT_t x_hi x_lo x_tr xn_done y_ok y_out ya0 ya1 ya2 ylo_ok ysb_free yz_ok yz_out z_ok z_out
"""


def bcast(ap, n):
    return bass.AP(tensor=ap.tensor, offset=ap.offset, ap=[[0, P], [1, n]])


def build(nc, a, o):
    ctx = ExitStack()
    with ctx:
        base, K = 16512, 1024

        def at(name, shape, off, dt=F32):
            return nc.alloc_sbuf_tensor_at(name, shape, dt, offset=base + int(off))

        def run_of(start):
            cur = [int(start)]

            def place(name, shape, dt=F32):
                off = cur[0]
                cur[0] += -(-int(np.prod(shape[1:])) * 4 // 32) * 32
                return at(name, shape, off, dt)
            return place, cur

        wring = at("wring", [P, 3, DC * 512], 0)
        raw = at("raw", [P, 6, 2048], 0)
        h = at("h", [P, TT, D], 48 * K)
        xT = at("xT", [P, DC, N], 68 * K)
        hiw = at("hiw", [P, 6, 2048], 92 * K, F32R)
        low = at("low", [P, 6, 2048], 140 * K, F32R)
        mixT = at("mixT", [P, DC, N], 86 * K)
        blrow = at("blrow", [P, BL], 96 * K)
        kvt = at("kvt", [P, TT, 6 * P], 103.5 * K)
        junk = at("junk", [P, D], 104 * K)
        qT = at("qT", [P, G, N], 118.5 * K)
        ksT = at("ksT", [P, N], 127 * K)
        kwT = at("kwT", [P, N], 129.25 * K)
        M = at("M", [P, NH, 512], 131.5 * K)
        xn = at("xn", [P, 2, D], 131.5 * K)
        hidt = at("hidt", [P, 2, 2 * XC], 131.5 * K)
        sq = at("sq", [P, D], 139.5 * K)
        qn = at("qn", [P, 2, 512], 143.5 * K)
        RB = 147.5 * K
        X1 = at("X1", [P, 2048], RB)
        X2 = at("X2", [P, 2048], RB + 8 * K)
        w1s = at("w1s", [P, 16, CH], RB + 16 * K)
        XT = at("XT", [P, 8, 2 * XC], RB + 32 * K)
        kcache = at("kcache", [P, NPG, P], RB)
        vcache = at("vcache", [P, NPG, P], RB + 8 * K)
        kcT = at("kcT", [P, NPG, P], RB + 16 * K)
        wout = at("wout", [P, DC, D], RB)
        gffn = at("gffn", [P, D], RB + 32 * K)
        hnt = at("hnt", [P, D], RB + 36 * K)
        cpT = at("cpT", [P, NH, P], RB + 36 * K)
        upp = at("upp", [P, SEQ + 2], 134.5 * K)
        ups = at("ups", [P, NB, 2 + NT], 136.75 * K)
        nsq = at("nsq", [P, P], 137 * K)
        cs_out = at("cs_out", [18, CONV], 143.5 * K)
        cs_in = at("cs_in", [P, CC, 2 + 2 * NB], 145.5 * K)
        sc = at("sc", [P, 2, 512], 68 * K)
        pr = at("pr", [P, 2, 512], 72 * K)
        pT = at("pT", [P, 2, 512], 76 * K)
        oacc = at("oacc", [P, 512], 80 * K)
        cms = at("cms", [P, 256], 82 * K)
        cme = at("cme", [P, 256], 83 * K)
        rsmall, rcur = run_of(134 * K)
        wr = rsmall("wr", [P, DC, NG + NE])
        br = rsmall("br", [P, NG + NE])
        lg = rsmall("lg", [P, TT, NG + NE])
        og = rsmall("og", [P, TT, NG])
        tg = rsmall("tg", [P, TT, NG])
        le = rsmall("le", [P, TT, NE])
        t32 = rsmall("t32", [P, TT, NE])
        oh1 = rsmall("oh1", [P, TT, NE])
        oh2 = rsmall("oh2", [P, TT, NE])
        asn = rsmall("asn", [P, TT, NE])
        slot = rsmall("slot", [P, TT, NE])
        ovs = rsmall("ovs", [P, 4, NE])
        rs = rsmall("rs", [P, 8, TT])
        jex = rsmall("jex", [P, MAXOV, NE])
        jey = rsmall("jey", [P, MAXOV, NE])
        jef = rsmall("jef", [P, JOBS])
        zslot = rsmall("zslot", [SLOTS, JOBS], I32)
        assert rcur[0] <= RB
        xg = at("xg", [P, D], 68 * K)
        xpack = at("xpack", [P, DC, 2 * SLOTS], 72 * K, F32R)
        Sg = at("Sg", [P, 2, 512], 76 * K)
        sg = at("sg", [P, 256], 80 * K)
        hT32 = at("hT32", [P, 4, SLOTS], 81 * K)
        hpack = at("hpack", [P, 4, 2 * SLOTS], 82 * K, F32R)
        ylo = at("ylo", [P, D], 84 * K)
        ysb = at("ysb", [P, D], 88 * K)
        wpg = at("wpg", [P, DC, D], 0)
        wple = at("wple", [P, 2, D], 32 * K)
        bpg = at("bpg", [P, D], 40 * K)
        yga = at("yga", [P, 3, 2, D], 68 * K)
        plo = at("plo", [P, TT, D], 124 * K)
        plT = at("plT", [P, 2, P], 144 * K)
        pin = at("pin", [P, TT, PLE], 148 * K)
        h2n = at("h2n", [P, 2, D], 157 * K)
        hpT = at("hpT", [P, 2, DC, P], 165 * K)
        sgt = at("sgt", [P, 2, D], 173 * K)
        junk2 = at("junk2", [P, D], 181 * K)
        small, scur = run_of(190.5 * K)
        cst = small("cst", [P, C_END])
        gk = small("gk", [P, 2, P])
        gmix = small("gmix", [P, DC])
        gple = small("gple", [P, DC])
        gq = small("gq", [P, 1])
        gk0 = small("gk0", [P, 1])
        cwT = small("cwT", [P, 12])
        ssq = small("ssq", [P, TT])
        rn = small("rn", [P, TT])
        ss12 = small("ss12", [P, 12])
        gates = small("gates", [P, TT, 24])
        w2s = small("w2s", [P, 2, HD])
        eps = small("eps", [P, 1])
        hb = small("hb", [P, 2])
        vcb = small("vcb", [P, P])
        vcp = small("vcp", [P, P])
        kcbT = small("kcbT", [P, NCH])
        kcpT = small("kcpT", [P, 32])
        Qbd = small("Qbd", [P, NB, 32])
        SM = small("SM", [P, KEYS_S])
        cmb = small("cmb", [P, 2, NCH])
        nmk = small("nmk", [P, 2, NS])
        st = small("st", [P, 40])
        gs = small("gs", [P, 2, NBR])
        tok = small("tok", [P, TT], I32)
        osam = small("osam", [P, 2, P])
        kcb, kcp, g24 = osam[:, 0, :], osam[:, 1, :], osam[:, 1, 0:24]
        upst = small("upst", [P, CC, 2 * NB])
        wts = small("wts", [P, 2, TT])
        dst = small("dst", [P, 2, TT], I32)
        jtab = small("jtab", [P, JOBS], I32)
        pti = small("pti", [P, NPG], I32)
        sidx = small("sidx", [SLOTS, JOBS], I32)
        icur = small("icur", [SLOTS, 1], I32)
        assert scur[0] <= 229360 - base, scur[0]

        ps = ctx.enter_context(nc.psum_tensor("ps", [P, 8, 512], F32))
        bline = nc.dram_tensor("biaslines", (NH, P, BL), F32).ap()
        hn_d = nc.dram_tensor("hn_rows", (N, D), F32).ap()
        y_d = nc.dram_tensor("expert_rows", ((JOBS - 1) * SLOTS, D), F32).ap()
        slot_d = nc.dram_tensor("slot_token", (JOBS * SLOTS, 1), I32).ap()

        S = {n: ctx.enter_context(nc.semaphore(n)) for n in SEMS.split()}
        block = ctx.enter_context(nc.Block())

        def eye(n):
            return cst[0:n, C_ID:C_ID + n]

        kv_out = list(enumerate(("k_cmp", "v_cmp", "k_slc", "v_slc", "k_win", "v_win")))
        w_in = a["w_in"].rearrange("(p c) n -> p c n", c=DC)
        TM = [(3 * CONV, 512), (3 * CONV + 512, 512), (3 * CONV + 1024, 280)]
        WGU = [a[f"w_exp_{x}"].rearrange("e (p k c) n -> e p k (c n)", k=2, c=4) for x in ("gate", "up")]
        WD = a["w_exp_down"].rearrange("e (p k c) n -> e p k (c n)", k=2, c=2)
        PIECES = [(WGU[0], 0, 0), (WGU[0], 1, 0), (WD, 0, 1), (WD, 1, 1), (WGU[1], 0, 0), (WGU[1], 1, 0)]
        G0, G1, D0, D1, U0, U1 = range(6)

        def load_piece(sp, J, i, e, first=False):
            src, half, _ = PIECES[i]
            if first:
                part = src[0, :, half, :]
            else:
                sp.wait_ge(S["lo_ok"], J * 6 + (i - 5))
                part = src[bass.ds(e, 1), :, half, :].rearrange("e p n -> p (e n)")
            sp.dma_start(raw[:, i, :], part).then_inc(S[f"raw{i}"], 16)

        def load_round(sp, J, e, before):
            for i in range(6):
                load_piece(sp, J, i, before if PIECES[i][2] else e)

        def arrival(J, i):
            return (J + (1 - PIECES[i][2])) * 16

        def rounds(eng, work):
            work(0, first=True)
            work(1, second=True)
            with eng.Fori(2, NE) as J:
                work(J)
            nov = eng.value_load(jtab[0:1, JOBS - 1:JOBS], min_val=0, max_val=MAXOV)
            with eng.If(nov > 0):
                with eng.Fori(NE, nov + NE) as J:
                    work(J)
            n = total(eng)
            work(n, last=True)
            return n

        def total(eng):
            return eng.value_load(jtab[0:1, JOBS - 1:JOBS], min_val=0, max_val=MAXOV) + NE

        def token_cols(dve, done, t, gain, b, ok):
            r = rows(t)
            dve.wait_ge(done, t + 1)
            src = ps[:, b:b + 2, :].rearrange("p k (c n) -> p (k c) n", n=P)[:, :, 0:r]
            to = xT[:, :, t * P:t * P + r]
            if gain is None:
                nc.vector.tensor_copy(to, src).then_inc(ok, 1)
            else:
                nc.vector.tensor_tensor(to, src, gain[:].unsqueeze(2).broadcast_to([P, DC, r]), ALU.mult).then_inc(ok, 1)

        @block.sync
        def _(sp):
            sp.dma_start(cst[:], a["consts"]).then_inc(S["cst_in"], 16)
            for t in range(TP):
                sp.dma_start(h[:, t, :], a["x_prompt"][t * P:(t + 1) * P, :]).then_inc(S[f"x{t}_in"], 16)
            sp.dma_start(h[0:NS, TP, :], a["x_sample"]).then_inc(S[f"x{TP}_in"], 16)
            for g, (c0, n) in enumerate(TM):
                sp.dma_start(wring[:, g, 0:DC * n].rearrange("p (c n) -> p c n", n=n),
                             w_in[:, :, c0:c0 + n]).then_inc(S[f"wq{min(g, 1)}"], 16)
            sp.dma_start(pti[0:1, :], a["page_table"].rearrange("(x b) n -> x (b n)", x=1)).then_inc(S["pt_in"], 16)
            sp.wait_ge(S["pt_in"], 16)

            def page(lp):
                return sp.value_load(pti[0:1, lp:lp + 1], min_val=0, max_val=a["cache_k_cmp"].shape[0] - 1)

            def chunk_rows(which, arrived):
                src = a[f"cache_{which}_cmp"].rearrange("g (c r) n -> g c (r n)", r=STRIDE)
                for lp in range(NPG):
                    pg = page(lp)
                    for hh in range(NKV):
                        sp.dma_start(X1[8 * lp:8 * lp + 8, D * hh:D * (hh + 1)].rearrange("c (r d) -> c r d", d=HD),
                                     src[bass.ds(pg, 1), :, :].rearrange("x c (r g d) -> (x c) r g d", g=NKV, d=HD)[:, :, hh, :])\
                            .then_inc(arrived, 16)
                r0 = SEQ // STRIDE
                for hh in range(NKV):
                    sp.dma_start(X2[r0:r0 + 2, :].rearrange("b (g r d) -> b r g d", g=NKV, d=HD)[:, :, hh, :],
                                 a[f"cmp_pe_{which}"].rearrange("(b r) d -> b r d", b=2)).then_inc(arrived, 16)

            def back(which, arrived):
                sp.wait_ge(S[f"{which}cmp_out"], 16)
                for hh in range(NKV):
                    sp.dma_start(X2[0:SEQ // STRIDE, D * hh:D * (hh + 1)].rearrange("c (r d) -> c r d", d=HD),
                                 o[f"{which}_cmp_p"].rearrange("(c r) (g d) -> c r g d", r=STRIDE, g=NKV)[:, :, hh, :])\
                        .then_inc(arrived, 16)

            sp.dma_start(w1s[:], a["cmp_w1_k"].rearrange("(k p) n -> p k n", p=P)).then_inc(S["w1_in"], 16)
            chunk_rows("k", S["X_in"])
            sp.wait_ge(S["bl_sb"], 1)
            sp.dma_start(bline, blrow[0:NH, :].unsqueeze(1).broadcast_to([NH, P, BL])).then_inc(S["bl_out"], 16)
            sp.wait_ge(S["tm_norm"], TT)
            for i, nm in kv_out:
                done = S["kcmp_out"] if i == 0 else S["vcmp_out"] if i == 1 else S["kvout"]
                sp.dma_start(o[nm + "_p"].rearrange("(t p) c -> p t c", p=P),
                             kvt[:, 0:TP, i * P:(i + 1) * P]).then_inc(done, 16)
                if i < 4:
                    sp.dma_start(o[nm + "_s"], kvt[0:NS, TP, i * P:(i + 1) * P]).then_inc(S["kvout"], 16)
                else:
                    for b in range(NB):
                        sp.dma_start(o[nm + "_s"][b, PAST - NT:PAST, :],
                                     kvt[b * NT:(b + 1) * NT, TP, i * P:(i + 1) * P]).then_inc(S["winout"], 16)
            back("k", S["X_in"])
            sp.wait_ge(S["tm_done"], TT)
            for c4 in range(CC):
                if c4 == 3:
                    sp.wait_ge(S["X_ev"], 8)
                    chunk_rows("v", S["X_in"])
                    back("v", S["X_in"])
                    sp.wait_ge(S["hid_done"], 2)
                    sp.dma_start(w1s[:], a["cmp_w1_v"].rearrange("(k p) n -> p k n", p=P)).then_inc(S["w1_in"], 16)
                    sp.wait_ge(S["cv_done"], 1)
                for j in range(3):
                    sp.dma_start(wring[:, c4 % 3, 0:DC * 384].rearrange("p (c n) -> p c n", n=384)[:, :, j * P:(j + 1) * P],
                                 w_in[:, :, j * CONV + c4 * P:j * CONV + (c4 + 1) * P]).then_inc(S[f"wc{c4}"], 16)
            for nm in ("k_win", "v_win"):
                sp.dma_start(o[nm + "_s"][:, 0:PAST - NT, :], a["cache_" + nm][:, NT:PAST, :]).then_inc(S["winout"], 16)
            sp.wait_ge(S["hid_done"], 4)
            for lp in range(NPG):
                for name, d, arrived in (("cache_k_slc", kcache, "kc_in"), ("cache_v_slc", vcache, "vc_in")):
                    sp.dma_start(d[:, lp, :], a[name][bass.ds(page(lp), 1), :, :].rearrange("x p n -> p (x n)"))\
                        .then_inc(S[arrived], 16)
            sp.wait_ge(S["bl_out"], 16)
            for q in range(4):
                for n in range(NH):
                    r0 = 32 * q + NT * n
                    sp.dma_start(SM[r0:r0 + NT, :], bass.AP(tensor=bline.tensor, offset=n * P * BL + BREF - PAST,
                                                            ap=[[BL - 1, NT], [1, KEYS_S]])).then_inc(S["SM_in"], 16)
            sp.wait_ge(S["cv_ok"], CC)
            sp.wait_ge(S["cb_done"], 2)
            sp.wait_ge(S["cs_outd"], 16 * 2)
            for n in range(NH):
                sp.dma_start(M[:, n, :], bass.AP(tensor=bline.tensor, offset=n * P * BL + P - 1,
                                                 ap=[[BL - 1, P], [1, 512]])).then_inc(S["M_in"], 16)
            sp.wait_ge(S["kt_done"], 4)
            sp.dma_start(kcache[:], a["cache_k_win"].rearrange("b (g p) n -> p (b g) n", p=PAGE)).then_inc(S["kc_in"], 16)
            for i in (G0, G1, U0, U1):
                load_piece(sp, 0, i, 0, first=True)
            sp.wait_ge(S["ss_pv"], 4)
            sp.dma_start(vcache[:], a["cache_v_win"].rearrange("b (g p) n -> p (b g) n", p=PAGE)).then_inc(S["vc_in"], 16)
            sp.wait_ge(S["ss_pv"], 6)
            sp.dma_start(wout[:], a["w_out"].rearrange("(c p) n -> p c n", p=P)).then_inc(S["wout_in"], 16)
            sp.dma_start(gffn[:], bcast(a["norm_ffn"], D)).then_inc(S["wout_in"], 16)
            sp.wait_ge(S["u_soft"], 2 * NH * TP)
            sp.wait_ge(S["cm_sub"], TP)
            sp.dma_start(wr[:, :, 0:NG], a["w_router_group"].rearrange("(p c) n -> p c n", c=DC)).then_inc(S["wr_in"], 16)
            sp.dma_start(wr[:, :, NG:NG + NE], a["w_router_expert"].rearrange("(p c) n -> p c n", c=DC)).then_inc(S["wr_in"], 16)
            sp.dma_start(br[:, 0:NG], bcast(a["b_router_group"], NG)).then_inc(S["wr_in"], 16)
            sp.dma_start(br[:, NG:NG + NE], bcast(a["b_router_expert"], NE)).then_inc(S["wr_in"], 16)
            for t in range(TT):
                sp.wait_ge(S["hn_done"], t + 1)
                sp.dma_start(hn_d[t * P:t * P + rows(t), :], hnt[0:rows(t), :]).then_inc(S["hn_out"], 16)
            with sp.Fori(1, NE) as J:
                load_round(sp, J, J, J - 1)
            sp.wait_ge(S["jei_ok"], 1)

            def expert(J):
                return sp.value_load(jtab[0:1, bass.ds(J, 1)], min_val=0, max_val=NE - 1)

            nov = sp.value_load(jtab[0:1, JOBS - 1:JOBS], min_val=0, max_val=MAXOV)
            with sp.If(nov > 0):
                with sp.Fori(NE, nov + NE) as J:
                    load_round(sp, J, expert(J), expert(J - 1))
            n = total(sp)
            e = expert(n - 1)
            for i in (D0, D1):
                load_piece(sp, n, i, e)
            sp.wait_ge(S["lo_ok"], n * 6)
            sp.dma_start(wple[:], a["w_ple"].rearrange("(p c) n -> p c n", c=2)).then_inc(S["ple_in"], 16)
            sp.wait_ge(S["used"], n * 6 + 6)
            sp.dma_start(pin[:, 0:TP, :], a["p_prompt"].rearrange("(t p) n -> p t n", p=P)).then_inc(S["ple_in"], 16)
            sp.dma_start(pin[0:NS, TP, :], a["p_sample"]).then_inc(S["ple_in"], 16)
            w = a["w_ple_gate"].rearrange("(p c) n -> p c n", c=DC)
            sp.dma_start(wpg[:, 0:4, :], w[:, 0:4, :]).then_inc(S["wpg_in"], 16)
            sp.dma_start(bpg[:], bcast(a["b_ple_gate"], D)).then_inc(S["wpg_in"], 16)
            sp.wait_ge(S["lo_ok"], n * 6 + 4)
            sp.dma_start(wpg[:, 4:8, :], w[:, 4:8, :]).then_inc(S["wpg_in"], 16)
            for t in range(TT):
                sp.wait_ge(S["f_o"], t + 1)
                to = o["y_prompt"][t * P:(t + 1) * P, :] if t < TP else o["y_sample"]
                sp.dma_start(to, sgt[0:rows(t), t % 2, :]).then_inc(S[f"f_out{t % 2}"], 16)
            sp.wait_ge(S["kvout"], 16 * 8)
            sp.wait_ge(S["kcmp_out"], 16)
            sp.wait_ge(S["vcmp_out"], 16)
            sp.wait_ge(S["winout"], 16 * (2 * NB + 2))
            sp.wait_ge(S["cs_outd"], 16 * 2)
            sp.wait_ge(S["f_out0"], 16 * 3)
            sp.wait_ge(S["f_out1"], 16 * 2)

        @block.gpsimd
        def _(pool):
            pool.sem_inc(S["ysb_free"], 1)
            nc.gpsimd.memset(mixT[:, 6:8, 0:512], 0.0).then_inc(S["yz_ok"], 1)
            pool.wait_ge(S["yz_ok"], 1)
            for k in range(MAXOV * SLOTS // P):
                r0 = NE * SLOTS + k * P
                pool.dma_start(y_d[r0:r0 + P, :].rearrange("p (k n) -> p k n", k=2), mixT[:, 6:8, 0:512]).then_inc(S["yz_out"], 16)
            pool.wait_ge(S["yz_out"], 16 * (MAXOV * SLOTS // P))
            pool.wait_ge(S["z_ok"], 1)
            pool.dma_start(slot_d.rearrange("(s j) x -> s (j x)", s=SLOTS), zslot[:]).then_inc(S["z_out"], 16)
            pool.wait_ge(S["z_out"], 16)
            pool.wait_ge(S["dst_ok"], 1)
            for t in range(TT):
                for k in range(2):
                    pool.indirect_dma_start(out=slot_d, out_offset=bass.IndirectOffsetOnAxis(ap=dst[0:rows(t), k, t:t + 1], axis=0),
                                            in_=tok[0:rows(t), t:t + 1], in_offset=None).then_inc(S["sc_out"], 16)
            pool.wait_ge(S["sc_out"], 16 * 2 * TT)
            with nc.allow_non_contiguous_dma(reason="a slot index is one word"):
                pool.dma_start(sidx[:], slot_d.rearrange("(j s) x -> s (j x)", s=SLOTS)).then_inc(S["idx_in"], 16)
            pool.wait_ge(S["idx_in"], 16)
            pool.wait_ge(S["hn_out"], 16 * TT)

            def gather(J):
                pool.wait_ge(S["x_tr"], J)
                nc.gpsimd.tensor_copy(icur[:], sidx[:, J:J + 1] if isinstance(J, int) else sidx[:, bass.ds(J, 1)])\
                    .then_inc(S["ic_ok"], 1)
                pool.wait_ge(S["ic_ok"], J + 1)
                pool.sem_inc(S["passed"], 1)
                pool.indirect_dma_start(out=xg[0:SLOTS, :], out_offset=None, in_=hn_d,
                                        in_offset=bass.IndirectOffsetOnAxis(ap=icur[:, 0:1], axis=0)).then_inc(S["gath"], 16)

            def work(J, first=False, second=False, last=False):
                if not last:
                    gather(J + 1)
                if not (first or second):
                    rows_leave(J)

            def rows_leave(J):
                pool.wait_ge(S["y_ok"], J)
                pool.dma_start(y_d[bass.ds(J * SLOTS - 2 * SLOTS, SLOTS), :], ysb[0:SLOTS, :]).then_inc(S["y_out"], 16)
                pool.wait_ge(S["y_out"], J * 16 - 16)
                pool.sem_inc(S["ysb_free"], 1)

            gather(0)
            n = rounds(pool, work)
            rows_leave(n + 1)
            for t in range(TT):
                if t >= 3:
                    pool.wait_ge(S["f_h2"], t - 2)
                for k in range(2):
                    pool.indirect_dma_start(out=yga[0:rows(t), t % 3, k, :], out_offset=None, in_=y_d,
                                            in_offset=bass.IndirectOffsetOnAxis(ap=dst[0:rows(t), k, t:t + 1], axis=0))\
                        .then_inc(S[f"ya{t % 3}"], 16)

        @block.scalar
        def _(act):
            A = nc.scalar.activation
            C = ACT.Copy
            act.dma_start(gmix[:], a["norm_mix"].rearrange("(p c) -> p c", c=DC)).then_inc(S["vec_in"], 16)
            act.dma_start(gple[:], a["norm_ple"].rearrange("(p c) -> p c", c=DC)).then_inc(S["vec_in"], 16)
            for hh in range(NKV):
                act.dma_start(gq[hh * HD:(hh + 1) * HD, :], a["q_norm"].rearrange("(p x) -> p x", x=1)).then_inc(S["vec_in"], 16)
                act.dma_start(gk0[hh * HD:(hh + 1) * HD, :], a["k_norm"][0, :].rearrange("(p x) -> p x", x=1)).then_inc(S["vec_in"], 16)
                for i in range(2):
                    act.dma_start(gk[:, i, hh * HD:(hh + 1) * HD], bcast(a["k_norm"][i + 1, :], HD)).then_inc(S["vec_in"], 16)
            act.dma_start(cmb[0:12, 0, :], a["conv_w"].rearrange("k (c p) -> (k c) p", p=P)).then_inc(S["rb_in"], 16)
            act.dma_start(tok[:], a["tok"]).then_inc(S["vec_in"], 16)
            act.dma_start(w2s[:], a["cmp_w2_k"].rearrange("(m p) n -> p m n", p=P)).then_inc(S["w2_in"], 16)
            act.dma_start(SM[0:NBUCK, 0:NH], a["rel_bias"]).then_inc(S["rb_in"], 16)
            act.dma_start(mixT[0:NBUCK + 1, 0:2, 0:320], a["buckets"].rearrange("b (k n) -> b k n", k=2)).then_inc(S["rb_in"], 16)
            act.dma_start(mixT[0:2 * NB, 2, 0:512], a["state_conv"]).then_inc(S["rb_in"], 16)
            sums = []

            def root_of(x, src, n):
                A(x, src, ACT.Sqrt, scale=1.0 / n, bias=eps[0:x.shape[0], 0:1]).then_inc(S["root_ok"], 1)

            def head_roots(r, n):
                sums.append(1)
                act.wait_ge(S["ss_sum"], len(sums))
                root_of(ss12[0:r, 0:n], ss12[0:r, 0:n], HD)

            act.wait_ge(S["eps_ok"], 1)
            for t in range(TT):
                act.wait_ge(S[f"x{t}_in"], 16)
                A(sq[0:rows(t), :], h[0:rows(t), t, :], ACT.Square, accum_out=ssq[0:rows(t), t:t + 1]).then_inc(S["sq_done"], 1)
                act.wait_ge(S["sq_done"], t + 1)
                root_of(rn[0:rows(t), t:t + 1], ssq[0:rows(t), t:t + 1], D)
            act.wait_ge(S["bl_ps"], 1)
            A(blrow[0:NH, :].rearrange("p (k n) -> p k n", k=2), ps[0:NH, 6:8, 0:320], C).then_inc(S["bl_sb"], 1)
            act.wait_ge(S["vec_in"], 16 * 11)
            for t in range(TT):
                r, b = rows(t), 3 * (t % 2)
                act.wait_ge(S["tm_done"], t + 1)
                if t >= 2:
                    act.wait_ge(S["tr_done"], t - 1)
                A(qn[0:r, t % 2, :].rearrange("p (g h d) -> p h g d", g=G, h=NKV),
                  ps[0:r, b, :].rearrange("p (h g d) -> p h g d", g=G, h=NKV), C)
                A(kvt[0:r, t, 0:512], ps[0:r, b + 1, :], C)
                A(kvt[0:r, t, 512:768], ps[0:r, b + 2, 0:256], C)
                A(gates[0:r, t, :], ps[0:r, b + 2, 256:280], C).then_inc(S["kv_copied"], 1)
                head_roots(r, 12)
                if t:
                    act.wait_ge(S["tr_done"], t)
                    A(qT[:, :, (t - 1) * P:t * P], ps[:, 6, :].rearrange("p (g n) -> p g n", g=G), C,
                      scale=gq[:, 0:1]).then_inc(S["tr_q"], 1)
            act.wait_ge(S["tr_done"], TT)
            A(qT[:, :, SEQ:N], ps[:, 6, :].rearrange("p (g n) -> p g n", g=G)[:, :, 0:NS], C,
              scale=gq[:, 0:1]).then_inc(S["tr_q"], 1)

            def hidden(i):
                act.wait_ge(S["hid_b"], i + 1)
                if i:
                    act.wait_ge(S["cb_done"], i)
                for m in range(2):
                    A(hidt[:, m, :], ps[:, 4 + m, 0:2 * XC], ACT.Gelu_apprx_tanh, bias=hb[:, m:m + 1]).then_inc(S["hid_gelu"], 1)

            def conv_xh(c4):
                act.wait_ge(S["cv_done"], c4 + 1)
                if c4:
                    act.wait_ge(S["cv_u"], c4)
                A(sq[:, 0:N].rearrange("p (k n) -> p k n", k=2), ps[:, 0:2, 0:N // 2], C).then_inc(S["cv_xh"], 1)

            hidden(0)
            head_roots(P, 2)
            head_roots(NCP, 2)
            act.wait_ge(S["cb_done"], 1)
            act.dma_start(w2s[:], a["cmp_w2_v"].rearrange("(m p) n -> p m n", p=P)).then_inc(S["w2_in"], 16)
            conv_xh(0)
            conv_xh(1)
            hidden(1)
            conv_xh(2)
            conv_xh(3)
            act.wait_ge(S["cs_out"], 1)
            act.dma_start(o["conv_p"], cs_out[0:2, :]).then_inc(S["cs_outd"], 16)
            act.dma_start(o["conv_s"], cs_out[2:18, :]).then_inc(S["cs_outd"], 16)
            act.wait_ge(S["kv_copied"], TT)
            A(gates[:], gates[:], ACT.Exp, scale=-1.0).then_inc(S["g_exp"], 1)
            for u in range(6):
                act.wait_ge(S["ss_soft"], u + 1)
                if u >= 2:
                    act.wait_ge(S["ss_tr"], u - 1)
                w = NCH if u < 2 else PAST + NS
                A(pr[:, u % 2, 0:w], sc[:, u % 2, 0:w], ACT.Exp, bias=st[:, u:u + 1], scale=-1.0,
                  accum_out=st[:, 8 + u:9 + u]).then_inc(S["ss_exp"], 1)
            for i in range(TP):
                nk = 8 * i + 7
                U = 2 * NH * i
                w = P * (i + 1)

                def exps(u):
                    act.wait_ge(S["u_soft"], u + 1)
                    if u >= 2:
                        act.wait_ge(S["u_tr"], u - 1)
                    A(pr[:, u % 2, 0:w], sc[:, u % 2, 0:w], ACT.Exp, bias=st[:, 16 + u % 4:17 + u % 4], scale=-1.0,
                      accum_out=st[:, 20 + u % 4:21 + u % 4]).then_inc(S["u_exp"], 1)

                act.wait_ge(S["cm_sub"], i + 1)
                A(cme[:, 0:NH * nk], cms[:, 0:NH * nk], ACT.Exp).then_inc(S["cm_exp"], 1)
                exps(U)
                exps(U + 1)
                act.wait_ge(S["cm_tr"], i + 1)
                A(cpT[0:nk, :, :].rearrange("p (b n) q -> p b (n q)", b=2), ps[0:nk, 6:8, :], C).then_inc(S["cm_pT"], 1)
                for k in range(2 * NH):
                    u = U + k
                    act.wait_ge(S["u_tr"], u + 1)
                    if u >= 2:
                        act.wait_ge(S["u_pv"], u - 1)
                    A(pT[:, u % 2, 0:w], ps[:, 2 + u % 2, 0:w], C).then_inc(S["u_pT"], 1)
                    if k + 2 < 2 * NH:
                        exps(u + 2)
            act.wait_ge(S["kvout"], 16 * 8)
            act.wait_ge(S["kcmp_out"], 16)
            act.wait_ge(S["vcmp_out"], 16)
            act.wait_ge(S["winout"], 16 * (2 * NB + 2))
            for t in range(TT):
                act.wait_ge(S["op_h"], t + 1)
                A(junk[0:rows(t), :], h[0:rows(t), t, :], ACT.Square, accum_out=ssq[0:rows(t), t:t + 1]).then_inc(S["sq_done"], 1)
                act.wait_ge(S["sq_done"], TT + t + 1)
                root_of(rn[0:rows(t), t:t + 1], ssq[0:rows(t), t:t + 1], D)
            act.wait_ge(S["r_log"], 1)
            A(tg[:], tg[:], ACT.Exp).then_inc(S["r_exp"], 1)
            act.wait_ge(S["r_e2"], 1)
            A(rs[:, 5, :], rs[:, 4, :], ACT.Exp).then_inc(S["r_exp"], 1)
            act.wait_ge(S["op_done"], TT)
            act.wait_ge(S["dst_ok"], 1)
            act.wait_ge(S["z_out"], 16)
            act.wait_ge(S["hn_out"], 16 * TT)

            A(sg[:, 0:1], eps[:], ACT.Silu)

            def high(J, i):
                act.wait_ge(S[f"raw{i}"], arrival(J, i))
                act.wait_ge(S["used"], J * 6 + (i + 1))
                A(hiw[:, i, :], raw[:, i, :], C).then_inc(S["hi_ok"], 1)

            def none_high(n):
                act.wait_ge(S["hi_ok"], n)
                act.sem_inc(S["hi_ok"], 2)

            def work(J, first=False, second=False, last=False):
                if last:
                    none_high(J * 6)
                else:
                    high(J, G0)
                    act.wait_ge(S["x_tr"], J + 1)
                    A(xpack[:, :, 0:SLOTS], ps[:, 3, :].rearrange("p (c s) -> p c s", s=SLOTS), C).then_inc(S["x_hi"], 1)
                if not first:
                    act.wait_ge(S["used"], J * 6 + 6)
                    A(Sg[:, 1, :], ps[:, 1, :], C).then_inc(S["gu_copied"], 1)
                if not last:
                    high(J, G1)
                if not (first or second):
                    rows_low(J)
                if first:
                    none_high(2)
                else:
                    act.wait_ge(S["gt_done"], J)
                    A(sg[:], ps[:, 2, 0:256], ACT.Silu).then_inc(S["silu_ok"], 1)
                    high(J, D0)
                    high(J, D1)
                if not last:
                    high(J, U0)
                    act.wait_ge(S["used"], J * 6 + 8)
                    A(Sg[:, 0, :], ps[:, 0, :], C).then_inc(S["gu_copied"], 1)
                    high(J, U1)
            def rows_low(J):
                act.wait_ge(S["used"], J * 6 + 4)
                act.wait_ge(S["y_ok"], J - 1)
                A(ylo[0:SLOTS, :].rearrange("p (k n) -> p k n", k=2), ps[SLOTS:P, 5:7, :], C).then_inc(S["ylo_ok"], 1)

            n = rounds(act, work)
            rows_low(n + 1)
            for t in range(TT):
                r = rows(t)
                act.wait_ge(S["f_ple"], 2 * t + 1)
                A(plT[:, :, 0:r], ps[:, 7, 0:2 * P].rearrange("p (c n) -> p c n", c=2)[:, :, 0:r], C).then_inc(S["f_pl"], 1)
                act.wait_ge(S["f_ple"], 2 * t + 2)
                b = 3 * (t % 2)
                A(plo[0:r, t, :].rearrange("p (k n) -> p k n", k=2), ps[0:r, b:b + 2, :], C).then_inc(S["f_pl"], 1)
            for t in range(TT):
                r = rows(t)
                act.wait_ge(S["f_h2"], t + 1)
                A(junk2[0:r, :], h[0:r, t, :], ACT.Square, accum_out=ssq[0:r, t:t + 1]).then_inc(S["sq_done"], 1)
                act.wait_ge(S["sq_done"], 2 * TT + t + 1)
                root_of(rn[0:r, t:t + 1], ssq[0:r, t:t + 1], D)
            for t in range(TT):
                r = rows(t)
                act.wait_ge(S["f_z"], t + 1)
                A(sgt[0:r, t % 2, :], sgt[0:r, t % 2, :], ACT.Sigmoid).then_inc(S["f_sig"], 1)

        @block.tensor
        def _(pe):
            T = nc.tensor.transpose

            def mm(out, l, r, start, stop, skip=False):
                return nc.tensor.matmul(out, l, r, start=start, stop=stop, skip_group_check=skip)

            pe.sem_inc(S["used"], 6)
            pe.wait_ge(S["cst_in"], 16)
            pe.wait_ge(S["rb_in"], 64)
            pe.wait_ge(S["rb_ok"], 1)
            for k in range(2):
                last = mm(ps[0:NH, 6 + k, 0:320], SM[0:NBUCK + 1, 0:NH], mixT[0:NBUCK + 1, k, 0:320], True, True)
            last.then_inc(S["bl_ps"], 1)
            T(ps[:, 5, 0:12], cmb[0:12, 0, :], eye(12))
            for c in range(CC):
                last = T(ps[:, 5, 16 + 16 * c:32 + 16 * c], mixT[0:2 * NB, 2, c * P:(c + 1) * P], eye(2 * NB))
            last.then_inc(S["cv_vec"], 1)

            def token_T(t, src, b, done):
                v = src.rearrange("r (p c) -> r p c", c=DC)
                for c in range(DC):
                    last = T(ps[:, b + c // 4, (c % 4) * P:(c % 4) * P + rows(t)], v[:, :, c], eye(rows(t)))
                last.then_inc(done, 1)

            for t in range(TT):
                pe.wait_ge(S["xn_done"], t + 1)
                if t >= 2:
                    pe.wait_ge(S["xT_ok"], t - 1)
                token_T(t, xn[0:rows(t), t % 2, :], 2 * (t % 2), S["xT_t"])

            def heads_T(t):
                r = rows(t)
                pe.wait_ge(S["tm_norm"], t + 1)
                if t:
                    pe.wait_ge(S["tr_q"], t)
                    pe.wait_ge(S["tr_k"], t)
                else:
                    pe.wait_ge(S["bl_sb"], 1)
                for g in range(G):
                    T(ps[:, 6, g * P:g * P + r], qn[0:r, t % 2, g * P:(g + 1) * P], eye(r))
                T(ps[:, 7, 0:r], kvt[0:r, t, KS:KS + P], eye(r))
                T(ps[:, 7, P:P + r], kvt[0:r, t, KW:KW + P], eye(r)).then_inc(S["tr_done"], 1)

            pe.wait_ge(S["xT_ok"], TT)
            pe.wait_ge(S["cv_vecc"], 1)
            for t in range(TT):
                r, b = rows(t), 3 * (t % 2)
                if t >= 2:
                    pe.wait_ge(S["kv_copied"], t - 1)
                for g, (c0, n) in enumerate(TM):
                    if t == 0 and g < 2:
                        pe.wait_ge(S[f"wq{g}"], 16 + 16 * g)
                    w = wring[:, g, 0:DC * n].rearrange("p (c n) -> p c n", n=n)
                    for c in range(DC):
                        last = mm(ps[0:r, b + g, 0:n], xT[:, c, t * P:t * P + r], w[:, c, :], c == 0, c == DC - 1)
                last.then_inc(S["tm_done"], 1)
                if t:
                    heads_T(t - 1)
            heads_T(TP)

            def compress_hidden(i, which):
                pe.wait_ge(S["X_in"], 16 * NKV * (NPG + 2) * (i + 1))
                for pp in range(8):
                    if pp >= 4:
                        pe.wait_ge(S["X_ev"], 8 * i + pp - 3)
                    for hh in range(NKV):
                        T(ps[:, pp % 4, hh * XC:hh * XC + NCH], X1[:, D * hh + P * pp:D * hh + P * (pp + 1)], eye(P))
                        last = T(ps[:, pp % 4, hh * XC + NCH:(hh + 1) * XC], X2[0:XC - NCH, D * hh + P * pp:D * hh + P * (pp + 1)],
                                 eye(XC - NCH))
                    last.then_inc(S["X_tr"], 1)
                pe.wait_ge(S["w1_in"], 16 * (i + 1))
                pe.wait_ge(S["X_ev"], 8 * i + 8)
                for m in range(2):
                    for k in range(16):
                        w = w1s[:, k, m * P:(m + 1) * P]
                        if k < 8:
                            last = mm(ps[:, 4 + m, 0:2 * XC], w, XT[:, k, :], k == 0, False)
                        else:
                            nxt = XT[:, k - 8, :].rearrange("p (g n) -> p g n", g=NKV)[:, :, 1:XC]
                            out = ps[:, 4 + m, 0:2 * XC].rearrange("p (g n) -> p g n", g=NKV)[:, :, 0:XC - 1]
                            last = mm(out, w, nxt, False, k == 15)
                    last.then_inc(S["hid_done"], 1)

            def compress_out(i, which):
                pe.wait_ge(S["hid_gelu"], 2 * i + 2)
                pe.wait_ge(S["w2_in"], 16 * (i + 1))
                if i:
                    pe.wait_ge(S["ct_ok"], 1)
                for hh in range(NKV):
                    for m in range(2):
                        mm(ps[:, 6, hh * HD:(hh + 1) * HD], hidt[:, m, hh * XC:hh * XC + NCH], w2s[:, m, :], m == 0, m == 1)
                for hh in range(NKV):
                    for m in range(2):
                        last = mm(ps[0:NCP, 7, hh * HD:(hh + 1) * HD], hidt[:, m, hh * XC + NCH:hh * XC + NCH + NCP],
                                  w2s[:, m, :], m == 0, m == 1)
                last.then_inc(S["cb_done"], 1)

            def conv(c4):
                pe.wait_ge(S[f"wc{c4}"], 48)
                if c4:
                    pe.wait_ge(S["cv_ok"], c4)
                w = wring[:, c4 % 3, 0:DC * 384].rearrange("p (c n) -> p c n", n=384)
                for j in range(3):
                    for half in range(2):
                        for c in range(DC):
                            last = mm(ps[:, 2 * j + half, 0:N // 2], w[:, c, j * P:(j + 1) * P],
                                      xT[:, c, half * (N // 2):(half + 1) * (N // 2)], c == 0, c == DC - 1)
                last.then_inc(S["cv_done"], 1)

            pe.wait_ge(S["kv_copied"], TT)
            pe.wait_ge(S["tr_q"], TT)
            pe.wait_ge(S["tr_k"], TT)
            compress_hidden(0, "k")
            compress_out(0, "k")
            pe.wait_ge(S["hid_gelu"], 2)
            conv(0)
            pe.wait_ge(S["cb_ok"], 1)
            T(ps[:, 6, 256:256 + NCH], kcb, eye(P))
            T(ps[:, 6, 384:384 + NCP], kcp[0:NCP, :], eye(NCP)).then_inc(S["ct_done"], 1)
            conv(1)
            pe.wait_ge(S["cv_ok"], 2)
            compress_hidden(1, "v")
            compress_out(1, "v")
            conv(2)
            conv(3)
            pe.wait_ge(S["cv_ok"], CC)
            pe.wait_ge(S["cb_ok"], 2)
            for c in range(CC):
                last = T(ps[0:18, 7, c * P:(c + 1) * P], cs_in[:, c, :], eye(P))
            last.then_inc(S["cs_ps"], 1)

            def qrows(rt):
                return Qbd[:, 4 * rt:4 * rt + 4, :].rearrange("p b r -> p (b r)")

            def keys_T(i, n):
                pe.wait_ge(S["kc_in"], n)
                for b in range(4):
                    if i:
                        pe.wait_ge(S["kt_ok"], 4)
                        pe.wait_ge(S["ss_done"], 4)
                    for j in range(4):
                        last = T(ps[:, b, j * P:(j + 1) * P], kcache[:, 4 * b + j, :], eye(P))
                    last.then_inc(S["kt_done"], 1)

            def ss_scores(u):
                bank, rt = 4 + u % 2, u % 2
                if u >= 2:
                    pe.wait_ge(S["ss_soft"], u - 1)
                if u < 2:
                    last = mm(ps[:, bank, 0:NCH], qrows(rt), kcbT[:], True, True)
                else:
                    newT = ksT if u < 4 else kwT
                    pe.wait_ge(S["kt_ok"], 4 if u < 4 else 8)
                    mm(ps[:, bank, PAST:PAST + NS], qrows(rt), newT[:, SEQ:N], True, True, True)
                    for q in range(4):
                        b = 4 * rt + q
                        last = nc.tensor.matmul(ps[32 * q:32 * q + 32, bank, 0:PAST], Qbd[:, b, :],
                                                kcT[:, 2 * b:2 * b + 2, :].rearrange("p g n -> p (g n)"),
                                                start=True, stop=True, skip_group_check=True)
                last.then_inc(S["ss_done"], 1)

            def ss_values(u):
                rt = u % 2
                pe.wait_ge(S["ss_exp"], u + 1)
                if u:
                    pe.wait_ge(S["ss_pT"], u)
                if u < 2:
                    T(ps[:, 6, 0:P], pr[:, rt, 0:NCH], eye(P)).then_inc(S["ss_tr"], 1)
                else:
                    for j in range(2):
                        T(ps[:, 6, j * P:(j + 1) * P], pr[:, rt, j * P:(j + 1) * P], eye(P))
                    T(ps[0:NS, 6, 2 * P:3 * P], pr[:, rt, PAST:PAST + NS], eye(P)).then_inc(S["ss_tr"], 1)
                pe.wait_ge(S["ss_pT"], u + 1)
                if u:
                    pe.wait_ge(S["ss_o"], u)
                else:
                    pe.wait_ge(S["s_qbd"], 2)
                po = ps[:, 7, 0:P]
                if u < 2:
                    last = mm(po, pT[:, 0, 0:P], vcb[:], True, True)
                else:
                    pe.wait_ge(S["vc_in"], 16 * (NPG if u < 4 else NPG + 1))
                    vn = kvt[0:NS, TP, (VS if u < 4 else VW):(VS if u < 4 else VW) + P]
                    mm(po, pT[0:NS, 0, 2 * P:3 * P], vn, True, False, True)
                    for q in range(4):
                        b = 4 * rt + q
                        for j in range(2):
                            last = mm(ps[32 * q:32 * q + 32, 7, 0:P], pT[:, 0, j * P + 32 * q:j * P + 32 * q + 32],
                                      vcache[:, 2 * b + j, :], False, j == 1, True)
                last.then_inc(S["ss_pv"], 1)

            pe.wait_ge(S["cv_ok"], CC)
            pe.wait_ge(S["cs_out"], 1)
            pe.wait_ge(S["s_qbd"], 1)
            pe.wait_ge(S["g_ok"], 1)
            for rt in range(2):
                mm(ps[:, 7, 32 * rt:32 * rt + 24], cst[0:NS, C_SEL + rt * P:C_SEL + (rt + 1) * P], gates[0:NS, TP, :],
                   True, True).then_inc(S["g_ps"], 1)
            ss_scores(0)
            ss_scores(1)
            keys_T(0, 16 * NPG)
            ss_values(0)
            ss_scores(2)
            ss_values(1)
            ss_scores(3)
            keys_T(1, 16 * NPG + 16)
            ss_values(2)
            ss_scores(4)
            ss_values(3)
            ss_scores(5)
            ss_values(4)
            ss_values(5)
            pe.wait_ge(S["ss_o"], 6)
            for rt in range(2):
                last = T(ps[:, 5, rt * P:(rt + 1) * P], osam[:, rt, :], eye(P))
            last.then_inc(S["so_ps"], 1)
            pe.wait_ge(S["so_ok"], 1)

            for i in range(TP):
                nk = 8 * i + 7
                U, w = 2 * NH * i, P * (i + 1)

                def scores(u):
                    n, kT = (u % (2 * NH)) // 2, (ksT, kwT)[u % 2]
                    p0 = HD * (n // G)
                    if u >= 2:
                        pe.wait_ge(S["u_soft"], u - 1)
                    mm(ps[:, u % 2, 0:w], qT[p0:p0 + HD, n % G, i * P:(i + 1) * P], kT[p0:p0 + HD, 0:w],
                       True, True).then_inc(S["u_s"], 1)

                for n in range(NH):
                    p0 = HD * (n // G)
                    last = mm(ps[:, 6 + n // G, (n % G) * nk:(n % G + 1) * nk], qT[p0:p0 + HD, n % G, i * P:(i + 1) * P],
                              kcpT[p0:p0 + HD, 0:nk], True, True)
                last.then_inc(S["cm_done"], 1)
                scores(U)
                scores(U + 1)
                pe.wait_ge(S["cm_p"], i + 1)
                if i:
                    pe.wait_ge(S["ot_ok"], i)
                for n in range(NH):
                    last = T(ps[0:nk, 6 + n // 4, (n % 4) * P:(n % 4 + 1) * P], cme[:, n * nk:(n + 1) * nk], eye(P))
                last.then_inc(S["cm_tr"], 1)
                pe.wait_ge(S["cm_pT"], i + 1)
                for n in range(NH):
                    last = mm(ps[:, 4, n * HD:(n + 1) * HD], cpT[0:nk, n, :], vcp[0:nk, HD * (n // G):HD * (n // G) + HD],
                              True, True)
                last.then_inc(S["cm_pv"], 1)
                pe.wait_ge(S["cm_o"], i + 1)
                for k in range(2 * NH):
                    u = U + k
                    pe.wait_ge(S["u_exp"], u + 1)
                    if u >= 2:
                        pe.wait_ge(S["u_pT"], u - 1)
                    for j in range(i + 1):
                        last = T(ps[:, 2 + u % 2, j * P:(j + 1) * P], pr[:, u % 2, j * P:(j + 1) * P], eye(P))
                    last.then_inc(S["u_tr"], 1)
                    if k + 2 < 2 * NH:
                        scores(u + 2)
                    pe.wait_ge(S["u_pT"], u + 1)
                    if u >= 2:
                        pe.wait_ge(S["u_o"], u - 1)
                    v0 = (VS, VW)[u % 2] + HD * (k // 2 // G)
                    for j in range(i + 1):
                        last = mm(ps[:, 4 + u % 2, 0:HD], pT[:, u % 2, j * P:(j + 1) * P],
                                  kvt[:, j, v0:v0 + HD], j == 0, j == i)
                    last.then_inc(S["u_pv"], 1)
                pe.wait_ge(S["u_o"], U + 2 * NH)
                for c in range(CC):
                    last = T(ps[:, 5, c * P:(c + 1) * P], oacc[:, c * P:(c + 1) * P], eye(P))
                last.then_inc(S["ot_ps"], 1)

            def route(t):
                r = rows(t)
                token_wait = S["ht_ok"]
                pe.wait_ge(token_wait, t + 1)
                for c in range(DC):
                    last = mm(ps[0:r, 6, (NG + NE) * t:(NG + NE) * (t + 1)], xT[:, c, t * P:t * P + r], wr[:, c, :],
                              c == 0, c == DC - 1)
                last.then_inc(S["r_done"], 1)

            def next_T(t):
                pe.wait_ge(S["hn_done"], t + 1)
                if t:
                    pe.wait_ge(S["ht_ok"], t)
                token_T(t, hnt[0:rows(t), :], 4, S["ht_done"])

            pe.wait_ge(S["wout_in"], 32)
            pe.wait_ge(S["ot_ok"], TP)
            for t in range(TT):
                r = rows(t)
                if t >= 2:
                    pe.wait_ge(S["op_h"], t - 1)
                for half in range(2):
                    for c in range(DC):
                        last = mm(ps[0:r, 2 * (t % 2) + half, :], mixT[:, c, t * P:t * P + r],
                                  wout[:, c, half * 512:(half + 1) * 512], c == 0, c == DC - 1)
                last.then_inc(S["op_done"], 1)
                if t == 1:
                    pe.wait_ge(S["wr_in"], 64)
                if t:
                    next_T(t - 1)
                    route(t - 1)
            next_T(TP)
            route(TP)
            pe.wait_ge(S["asn_ok"], 1)
            for t in range(TT):
                r = rows(t)
                for s in range(t):
                    mm(ps[0:r, 7, t * NE:(t + 1) * NE], cst[:, C_ONE:C_ONE + r], asn[:, s, :], s == 0, False)
                mm(ps[0:r, 7, t * NE:(t + 1) * NE], cst[0:r, C_TRI:C_TRI + r], asn[0:r, t, :], t == 0, True)
            for s in range(TT):
                r = rows(s)
                last = mm(ps[:, 7, TT * NE:(TT + 1) * NE], cst[0:r, C_ONE:C_ONE + P], asn[0:r, s, :], s == 0, s == TP)
            last.then_inc(S["pf_done"], 1)
            pe.wait_ge(S["jei_ok"], 1)

            def rows_T(J):
                pe.wait_ge(S["gath"], J * 16 + 16)
                pe.wait_ge(S["x_lo"], J)
                pe.sem_inc(S["passed"], 1)
                v = xg[0:SLOTS, :].rearrange("r (p c) -> r p c", c=DC)
                for c in range(DC):
                    last = T(ps[:, 3, c * SLOTS:(c + 1) * SLOTS], v[:, :, c], eye(SLOTS))
                last.then_inc(S["x_tr"], 1)

            def piece(J, i):
                pe.wait_ge(S["lo_ok"], J * 6 + (i + 1))
                half = PIECES[i][1]
                if i in (D0, D1):
                    for j in range(2):
                        c = 2 * half + j
                        for n in range(2):
                            for w in (hiw, low):
                                last = mm(ps[:, 5 + n, :], hpack[:, c, :], w[:, i, j * D + n * 512:j * D + (n + 1) * 512],
                                          c == 0 and w is hiw, c == 3 and w is low)
                else:
                    for j in range(4):
                        c = 4 * half + j
                        for w in (hiw, low):
                            last = mm(ps[:, i // U0, :], xpack[:, c, :], w[:, i, j * 512:(j + 1) * 512],
                                      c == 0 and w is hiw, c == DC - 1 and w is low)
                last.then_inc(S["used"], 1)

            def none_used(n):
                pe.wait_ge(S["used"], n)
                pe.sem_inc(S["used"], 2)

            def work(J, first=False, second=False, last=False):
                if last:
                    none_used(J * 6 + 6)
                else:
                    pe.wait_ge(S["x_lo"], J + 1)
                    piece(J, G0)
                if not first:
                    pe.wait_ge(S["gu_copied"], J * 2)
                    pe.wait_ge(S["hT_ok"], J * 2 - 1)
                    for k in range(2):
                        v = Sg[:, k, :].rearrange("r (p c) -> r p c", c=4)
                        for c in range(4):
                            last_mm = mm(ps[:, 2, k * 256 + c * SLOTS:k * 256 + (c + 1) * SLOTS], v[:, :, c],
                                         cst[:, C_II:C_II + SLOTS], True, True)
                    last_mm.then_inc(S["gt_done"], 1)
                if not last:
                    piece(J, G1)
                if first:
                    none_used(8)
                else:
                    pe.wait_ge(S["h_ok"], J)
                    pe.wait_ge(S["y_ok"], J)
                    piece(J, D0)
                    piece(J, D1)
                if not last:
                    piece(J, U0)
                    piece(J, U1)
                    rows_T(J + 1)

            rows_T(0)
            rounds(pe, work)
            pe.wait_ge(S["ple_in"], 48)
            for t in range(TT):
                r, b = rows(t), 3 * (t % 2)
                v = pin[0:r, t, :].rearrange("r (p c) -> r p c", c=2)
                if t:
                    pe.wait_ge(S["f_pl"], 2 * t)
                for c in range(2):
                    last = T(ps[:, 7, c * P:c * P + r], v[:, :, c], eye(r))
                last.then_inc(S["f_ple"], 1)
                pe.wait_ge(S["f_pl"], 2 * t + 1)
                for half in range(2):
                    for c in range(2):
                        last = mm(ps[0:r, b + half, :], plT[:, c, 0:r], wple[:, c, half * 512:(half + 1) * 512], c == 0, c == 1)
                last.then_inc(S["f_ple"], 1)

            def normed_T(t):
                pe.wait_ge(S["f_hn"], t + 1)
                if t >= 2:
                    pe.wait_ge(S["f_hpT"], t - 1)
                token_T(t, h2n[0:rows(t), t % 2, :], 2 * (t % 2), S["f_tr"])

            pe.wait_ge(S["wpg_in"], 48)
            pe.wait_ge(S["f_pl"], 2 * TT)
            normed_T(0)
            normed_T(1)
            for t in range(TT):
                r, b = rows(t), 4 + 2 * (t % 2)
                pe.wait_ge(S["f_hpT"], t + 1)
                if t >= 2:
                    pe.wait_ge(S["f_z"], t - 1)
                for half in range(2):
                    for c in range(DC):
                        last = mm(ps[0:r, b + half, :], hpT[:, t % 2, c, 0:r], wpg[:, c, half * 512:(half + 1) * 512],
                                  c == 0, c == DC - 1)
                last.then_inc(S["f_mm"], 1)
                if t + 2 < TT:
                    normed_T(t + 2)

        @block.vector
        def _(dve):
            chain = Chain(dve, S["dve_chain"])
            V = nc.vector
            TTn, TS, STT = V.tensor_tensor, V.tensor_scalar, V.scalar_tensor_tensor

            roots = []

            def rms(x):
                roots.append(1)
                dve.wait_ge(S["root_ok"], len(roots))
                chain(V.reciprocal(x, x))

            def both(b, r=P):
                return ps[0:r, b:b + 2, :].rearrange("p k n -> p (k n)")

            V.memset(gates[:], 0.0)
            V.memset(eps[:], EPS).then_inc(S["eps_ok"], 1)
            dve.wait_ge(S["rb_in"], 64)
            V.memset(SM[NBUCK:NBUCK + 1, 0:NH], -BIG).then_inc(S["rb_ok"], 1)
            for t in range(TT):
                r = rows(t)
                rms(rn[0:r, t:t + 1])
                if t >= 2:
                    dve.wait_ge(S["xT_t"], t - 1)
                TS(xn[0:r, t % 2, :], h[0:r, t, :], rn[0:r, t:t + 1], None, ALU.mult).then_inc(S["xn_done"], 1)
                if t == 0:
                    dve.wait_ge(S["vec_in"], 16 * 11)
                    chain(TS(gq[:], gq[:], HD ** -0.5, None, ALU.mult))
                    dve.wait_ge(S["cv_vec"], 1)
                    V.tensor_copy(cwT[:], ps[:, 5, 0:12])
                    V.tensor_copy(upst[:], ps[:, 5, 16:80].rearrange("p (c n) -> p c n", c=CC)).then_inc(S["cv_vecc"], 1)
                if t:
                    token_cols(dve, S["xT_t"], t - 1, gmix, 2 * ((t - 1) % 2), S["xT_ok"])
            token_cols(dve, S["xT_t"], TP, gmix, 2 * (TP % 2), S["xT_ok"])

            dve.wait_ge(S["cv_vecc"], 1)
            V.memset(cmb[:], -BIG)
            V.memset(nmk[:], -BIG)
            V.memset(upp[:, 0:2], 0.0)
            chain(V.memset(Qbd[:], 0.0))

            for t in range(TT):
                r = rows(t)
                dve.wait_ge(S["kv_copied"], t + 1)
                q = qn[0:r, t % 2, :]
                kk = kvt[0:r, t, KS:KW + P].rearrange("p (i n) -> p i n", n=P)[:, 0:3:2, :]
                TTn(sq[0:r, 0:512], q, q, ALU.mult)
                chain(TTn(sq[0:r, 512:768].rearrange("p (i n) -> p i n", n=P), kk, kk, ALU.mult))
                V.reduce_sum(ss12[0:r, :], sq[0:r, 0:768].rearrange("p (k d) -> p k d", d=HD), axis=X).then_inc(S["ss_sum"], 1)
                rms(ss12[0:r, :])
                r8 = ss12[0:r, 0:NH].unsqueeze(2).broadcast_to([r, NH, HD])
                TTn(q.rearrange("p (k d) -> p k d", d=HD), q.rearrange("p (k d) -> p k d", d=HD), r8, ALU.mult)
                for i, c0 in enumerate((KS, KW)):
                    x = kvt[0:r, t, c0:c0 + P]
                    r2 = ss12[0:r, NH + 2 * i:NH + 2 * i + 2].unsqueeze(2).broadcast_to([r, NKV, HD])
                    x3 = x.rearrange("p (k d) -> p k d", d=HD)
                    chain(TTn(x3, x3, r2, ALU.mult))
                    last = TTn(x, x, gk[0:r, i, :], ALU.mult)
                last.then_inc(S["tm_norm"], 1)
                dve.wait_ge(S["tr_done"], t + 1)
                V.tensor_copy(ksT[:, t * P:t * P + r], ps[:, 7, 0:r])
                V.tensor_copy(kwT[:, t * P:t * P + r], ps[:, 7, P:P + r]).then_inc(S["tr_k"], 1)

            dve.wait_ge(S["tr_q"], TT)
            for hh in range(NKV):
                p0 = hh * HD
                last = V.tensor_copy(Qbd[p0:p0 + HD, :, 16 * hh:16 * hh + 16].rearrange("p b (g t) -> p b g t", g=G),
                                     qT[p0:p0 + HD, :, SEQ:N].rearrange("p g (b t) -> p b g t", b=NB))
            last.then_inc(S["s_qbd"], 1)

            def compress_dve(i):
                for pp in range(8):
                    dve.wait_ge(S["X_tr"], 8 * i + pp + 1)
                    if i and pp == 0:
                        dve.wait_ge(S["hid_done"], 2)
                    V.tensor_copy(XT[:, pp, :], ps[:, pp % 4, 0:2 * XC]).then_inc(S["X_ev"], 1)
                dve.wait_ge(S["hid_done"], 2 * i + 2)
                if i:
                    dve.wait_ge(S["hid_gelu"], 2)
                V.tensor_copy(hb[:], ps[:, 4:6, XC - 2]).then_inc(S["hid_b"], 1)

            def keys_norm():
                V.tensor_copy(kcb, ps[:, 6, 0:P])
                chain(V.tensor_copy(kcp[0:NCP, :], ps[0:NCP, 7, 0:P]))
                for x, r in ((kcb, P), (kcp, NCP)):
                    chain(TTn(nsq[0:r, :], x[0:r, :], x[0:r, :], ALU.mult))
                    V.reduce_sum(ss12[0:r, 0:2], nsq[0:r, :].rearrange("p (k d) -> p k d", d=HD), axis=X).then_inc(S["ss_sum"], 1)
                    rms(ss12[0:r, 0:2])
                    x3 = x[0:r, :].rearrange("p (k d) -> p k d", d=HD)
                    last = TTn(x3, x3, ss12[0:r, 0:2].unsqueeze(2).broadcast_to([r, NKV, HD]), ALU.mult)
                    if r == P:
                        chain(last)
                last.then_inc(S["cb_ok"], 1)

            def conv_dve(c4):
                dve.wait_ge(S["cv_xh"], c4 + 1)
                if c4 == 0:
                    dve.wait_ge(S["bl_out"], 16)
                NH2 = N // 2
                V.tensor_copy(ups[:, :, 0:2], upst[:, c4, :].rearrange("p (b k) -> p b k", k=2))
                TTn(upp[:, 2:2 + NH2], ps[:, 4, 0:NH2], sq[:, 0:NH2], ALU.mult)
                TTn(upp[:, 2 + NH2:2 + SEQ], ps[:, 5, 0:SEQ - NH2], sq[:, NH2:SEQ], ALU.mult)
                chain(TTn(ups[:, :, 2:6], ps[:, 5, SEQ - NH2:NH2].rearrange("p (b t) -> p b t", t=NT),
                          sq[:, SEQ:N].rearrange("p (b t) -> p b t", t=NT), ALU.mult))
                dve.sem_inc(S["cv_u"], 1)
                V.tensor_copy(cs_in[:, c4, 0:2], upp[:, SEQ:SEQ + 2])
                V.tensor_copy(cs_in[:, c4, 2:18].rearrange("p (b k) -> p b k", k=2), ups[:, :, NT:NT + 2])
                yp, ysm = mixT[:, c4, 0:SEQ], mixT[:, c4, SEQ:N].rearrange("p (b t) -> p b t", t=NT)
                TS(yp, upp[:, 0:SEQ], cwT[:, c4:c4 + 1], None, ALU.mult)
                chain(TS(ysm, ups[:, :, 0:NT], cwT[:, c4:c4 + 1], None, ALU.mult))
                for k in (1, 2):
                    w = cwT[:, CC * k + c4:CC * k + c4 + 1]
                    STT(yp, upp[:, k:k + SEQ], w, yp, ALU.mult, ALU.add)
                    chain(STT(ysm, ups[:, :, k:k + NT], w, ysm, ALU.mult, ALU.add))
                TTn(mixT[:, c4, 0:NH2], mixT[:, c4, 0:NH2], ps[:, 2, 0:NH2], ALU.mult)
                chain(TTn(mixT[:, c4, NH2:N], mixT[:, c4, NH2:N], ps[:, 3, 0:NH2], ALU.mult))
                dve.sem_inc(S["cv_ok"], 1)

            compress_dve(0)
            dve.wait_ge(S["cb_done"], 1)
            keys_norm()
            conv_dve(0)
            dve.wait_ge(S["ct_done"], 1)
            TS(kcbT[:], ps[:, 6, 256:256 + NCH], gk0[:, 0:1], None, ALU.mult)
            TS(kcpT[:, 0:NCP], ps[:, 6, 384:384 + NCP], gk0[:, 0:1], None, ALU.mult).then_inc(S["ct_ok"], 1)
            conv_dve(1)
            compress_dve(1)
            dve.wait_ge(S["cb_done"], 2)
            V.tensor_copy(vcb[:], ps[:, 6, 0:P])
            V.tensor_copy(vcp[0:NCP, :], ps[0:NCP, 7, 0:P]).then_inc(S["cb_ok"], 1)
            conv_dve(2)
            conv_dve(3)
            dve.wait_ge(S["SM_in"], 16 * 4 * NH)
            for b in range(NB):
                q0, rt = 32 * (b % 4), b // 4
                V.tensor_copy(cmb[q0:q0 + 32, rt, CS * b:CS * b + CS - 1],
                              SM[q0:q0 + 32, 2 * STRIDE - 1:2 * STRIDE - 1 + STRIDE * (CS - 2) + 1:STRIDE])
                V.tensor_copy(nmk[q0:q0 + 32, rt, NT * b:NT * b + NT], SM[q0:q0 + 32, PAST:PAST + NT])
            dve.wait_ge(S["cs_ps"], 1)
            chain(V.tensor_copy(cs_out[:], ps[0:18, 7, :]))
            dve.sem_inc(S["cs_out"], 1)

            def ss_soft(u):
                rt = u % 2
                dve.wait_ge(S["ss_done"], u + 1)
                if u >= 2:
                    dve.wait_ge(S["ss_exp"], u - 1)
                if u < 2:
                    V.tensor_tensor_reduce(sc[:, rt, 0:NCH], ps[:, 4 + rt, 0:NCH], cmb[:, rt, :], -1.0, BIG, ALU.add, ALU.min,
                                           st[:, u:u + 1]).then_inc(S["ss_soft"], 1)
                else:
                    w = PAST + NS
                    V.tensor_tensor_reduce(sc[:, rt, 0:PAST], ps[:, 4 + rt, 0:PAST], SM[:, 0:PAST], -1.0, BIG, ALU.add, ALU.min,
                                           st[:, u:u + 1])
                    chain(V.tensor_tensor_reduce(sc[:, rt, PAST:w], ps[:, 4 + rt, PAST:w], nmk[:, rt, :], -1.0, BIG, ALU.add,
                                                 ALU.min, st[:, 32 + u:33 + u]))
                    TTn(st[:, u:u + 1], st[:, u:u + 1], st[:, 32 + u:33 + u], ALU.min).then_inc(S["ss_soft"], 1)

            def ss_out(u):
                rt, br_ = u % 2, u // 2
                dve.wait_ge(S["ss_tr"], u + 1)
                if u:
                    dve.wait_ge(S["ss_pv"], u)
                if u < 2:
                    V.tensor_copy(pT[:, 0, 0:P], ps[:, 6, 0:P]).then_inc(S["ss_pT"], 1)
                else:
                    V.tensor_copy(pT[:, 0, 0:2 * P], ps[:, 6, 0:2 * P])
                    V.tensor_copy(pT[0:NS, 0, 2 * P:3 * P], ps[0:NS, 6, 2 * P:3 * P]).then_inc(S["ss_pT"], 1)
                chain(TS(st[:, 24:25], st[:, 8 + u:9 + u], 1e-30, None, ALU.max))
                chain(V.reciprocal(st[:, 24:25], st[:, 24:25]))
                chain(TTn(st[:, 24:25], st[:, 24:25], gs[:, rt, br_:br_ + 1], ALU.mult))
                chain(TS(st[:, 26:28], cst[:, C_HM:C_HM + NKV], st[:, 24:25], None, ALU.mult))
                dve.wait_ge(S["ss_pv"], u + 1)
                for hh in range(NKV):
                    if br_ == 0 and hh == 0:
                        chain(TS(osam[:, rt, 0:HD], ps[:, 7, 0:HD], st[:, 26:27], None, ALU.mult))
                    else:
                        chain(STT(osam[:, rt, 0:HD], ps[:, 7, hh * HD:(hh + 1) * HD], st[:, 26 + hh:27 + hh],
                                  osam[:, rt, 0:HD], ALU.mult, ALU.add))
                if br_ == NBR - 1:
                    chain(V.tensor_copy(osam[:, rt, HD:P], osam[:, rt, 0:HD]))
                dve.sem_inc(S["ss_o"], 1)

            dve.wait_ge(S["g_exp"], 1)
            chain(TS(gates[:], gates[:], 1.0, None, ALU.add))
            V.reciprocal(gates[:], gates[:]).then_inc(S["g_ok"], 1)
            for rt in range(2):
                dve.wait_ge(S["g_ps"], 2)
                chain(TTn(g24.rearrange("p (n k) -> p n k", k=NBR),
                          ps[:, 7, 32 * rt:32 * rt + 24].rearrange("p (n k) -> p n k", k=NBR),
                          cst[:, C_NM:C_NM + NH].unsqueeze(2).broadcast_to([P, NH, NBR]), ALU.mult))
                chain(V.reduce_sum(gs[:, rt, :], g24.rearrange("p (n k) -> p k n", k=NBR), axis=X))
            dve.sem_inc(S["s_qbd"], 1)
            ss_soft(0)
            ss_soft(1)
            for b in range(4):
                dve.wait_ge(S["kt_done"], b + 1)
                V.tensor_copy(kcT[:, 4 * b:4 * b + 4, :].rearrange("p g n -> p (g n)"), ps[:, b, :]).then_inc(S["kt_ok"], 1)
            ss_out(0)
            ss_soft(2)
            ss_out(1)
            ss_soft(3)
            for b in range(4):
                dve.wait_ge(S["kt_done"], b + 5)
                dve.wait_ge(S["ss_done"], 4)
                V.tensor_copy(kcT[:, 4 * b:4 * b + 4, :].rearrange("p g n -> p (g n)"), ps[:, b, :]).then_inc(S["kt_ok"], 1)
            ss_out(2)
            ss_soft(4)
            ss_out(3)
            ss_soft(5)
            ss_out(4)
            ss_out(5)
            dve.wait_ge(S["so_ps"], 1)
            dve.wait_ge(S["yz_out"], 16 * (MAXOV * SLOTS // P))
            for n in range(NH):
                p0 = HD * (n % 2)
                last = V.tensor_copy(
                    mixT[p0:p0 + HD, CC + n // 2, SEQ:N].rearrange("p (b t) -> p b t", t=NT),
                    ps[p0:p0 + HD, 5, 0:2 * P].rearrange("p (b n t) -> p b n t", n=NH, t=NT)[:, :, n, :])
            last.then_inc(S["so_ok"], 1)

            dve.wait_ge(S["M_in"], 16 * NH)
            for i in range(TP):
                nk = 8 * i + 7
                U, w = 2 * NH * i, P * (i + 1)
                x0 = 512 - P * (i + 1)

                def soft(u):
                    n = (u % (2 * NH)) // 2
                    dve.wait_ge(S["u_s"], u + 1)
                    if u >= 2:
                        dve.wait_ge(S["u_exp"], u - 1)
                    V.tensor_tensor_reduce(sc[:, u % 2, 0:w], ps[:, u % 2, 0:w], M[:, n, x0:512], -1.0, BIG, ALU.add, ALU.min,
                                           st[:, 16 + u % 4:17 + u % 4]).then_inc(S["u_soft"], 1)

                c3 = cms[:, 0:NH * nk].rearrange("p (h n) -> p h n", h=NH)
                e3 = cme[:, 0:NH * nk].rearrange("p (h n) -> p h n", h=NH)
                off = x0 + 2 * STRIDE - 1
                dve.wait_ge(S["cm_done"], i + 1)
                chain(TTn(c3.rearrange("p (b g) n -> p b g n", b=NKV),
                          ps[:, 6:8, 0:G * nk].rearrange("p b (g n) -> p b g n", g=G),
                          M[:, :, off:off + STRIDE * (nk - 1) + 1:STRIDE].rearrange("p (b g) n -> p b g n", b=NKV), ALU.add))
                chain(V.tensor_reduce(st[:, 32:40], c3, X, ALU.max))
                chain(TS(st[:, 32:40], st[:, 32:40], -0.1 * BIG, None, ALU.max))
                TTn(c3, c3, st[:, 32:40].unsqueeze(2).broadcast_to([P, NH, nk]), ALU.subtract).then_inc(S["cm_sub"], 1)
                soft(U)
                soft(U + 1)
                dve.wait_ge(S["cm_exp"], i + 1)
                gt = gates[:, i, :].rearrange("p (h k) -> p h k", k=NBR)
                chain(V.reduce_sum(st[:, 32:40], e3, axis=X))
                chain(TS(st[:, 32:40], st[:, 32:40], 1e-30, None, ALU.max))
                chain(V.reciprocal(st[:, 32:40], st[:, 32:40]))
                chain(TTn(st[:, 32:40], st[:, 32:40], gt[:, :, 0], ALU.mult))
                TTn(e3, e3, st[:, 32:40].unsqueeze(2).broadcast_to([P, NH, nk]), ALU.mult).then_inc(S["cm_p"], 1)
                dve.wait_ge(S["cm_pv"], i + 1)
                if i:
                    dve.wait_ge(S["ot_ps"], i)
                chain(V.tensor_copy(oacc[:], ps[:, 4, :]))
                dve.sem_inc(S["cm_o"], 1)
                for k in range(2 * NH):
                    u, n = U + k, k // 2
                    if k + 2 < 2 * NH:
                        soft(u + 2)
                    dve.wait_ge(S["u_exp"], u + 1)
                    coef = st[:, 28 + u % 4:29 + u % 4]
                    chain(TS(coef, st[:, 20 + u % 4:21 + u % 4], 1e-30, None, ALU.max))
                    chain(V.reciprocal(coef, coef))
                    chain(TTn(coef, coef, gates[:, i, NBR * n + 1 + k % 2:NBR * n + 2 + k % 2], ALU.mult))
                    dve.wait_ge(S["u_pv"], u + 1)
                    if k % 2:
                        dve.wait_ge(S["u_o"], u)
                    STT(oacc[:, n * HD:(n + 1) * HD], ps[:, 4 + u % 2, 0:HD], coef,
                        oacc[:, n * HD:(n + 1) * HD], ALU.mult, ALU.add).then_inc(S["u_o"], 1)
                dve.wait_ge(S["ot_ps"], i + 1)
                V.tensor_copy(mixT[:, CC:DC, i * P:(i + 1) * P], ps[:, 5, :].rearrange("p (c n) -> p c n", c=CC))\
                    .then_inc(S["ot_ok"], 1)

            dve.wait_ge(S["wout_in"], 32)
            for t in range(TT):
                r = rows(t)
                dve.wait_ge(S["op_done"], t + 1)
                TTn(h[0:r, t, :], h[0:r, t, :], both(2 * (t % 2), r), ALU.add).then_inc(S["op_h"], 1)
                if t:
                    token_cols(dve, S["ht_done"], t - 1, None, 4, S["ht_ok"])
                rms(rn[0:r, t:t + 1])
                if t:
                    dve.wait_ge(S["hn_out"], 16 * t)
                STT(hnt[0:r, :], h[0:r, t, :], rn[0:r, t:t + 1], gffn[0:r, :], ALU.mult, ALU.mult).then_inc(S["hn_done"], 1)
            token_cols(dve, S["ht_done"], TP, None, 4, S["ht_ok"])

            dve.wait_ge(S["wr_in"], 64)
            V.memset(zslot[:], 0).then_inc(S["z_ok"], 1)
            chain(V.memset(lg[:], 0.0))
            dve.wait_ge(S["r_done"], TT)
            W = NG + NE
            for t in range(TT):
                r = rows(t)
                chain(TTn(lg[0:r, t, :], ps[0:r, 6, W * t:W * (t + 1)], br[0:r, :], ALU.add))

            def spread(x, n):
                return x.unsqueeze(2).broadcast_to([P, TT, n])

            def first_max(hot, x, m, n, tmp):
                chain(V.tensor_reduce(m, x, X, ALU.max))
                chain(TTn(tmp, x, spread(m, n), ALU.is_ge))
                desc = cst[:, C_DESC:C_DESC + n].unsqueeze(1).broadcast_to([P, TT, n])
                chain(TTn(tmp, tmp, desc, ALU.mult))
                chain(V.tensor_reduce(rs[:, 7, :], tmp, X, ALU.max))
                chain(TTn(hot, tmp, spread(rs[:, 7, :], n), ALU.is_equal))

            lgg = lg[:, :, 0:NG]
            first_max(og[:], lgg, rs[:, 0, :], NG, tg[:])
            TTn(tg[:], lgg, spread(rs[:, 0, :], NG), ALU.subtract).then_inc(S["r_log"], 1)
            chain(TS(og[:], og[:], 1.0, BIG, ALU.subtract, ALU.mult))
            for t in range(TT):
                chain(TTn(le[:, t, :].rearrange("p (g e) -> p g e", e=EG), lg[:, t, NG:W].rearrange("p (g e) -> p g e", e=EG),
                          og[:, t, :].unsqueeze(2).broadcast_to([P, NG, EG]), ALU.add))
            first_max(oh1[:], le[:], rs[:, 1, :], NE, t32[:])
            chain(TS(t32[:], oh1[:], -3.0 * BIG, None, ALU.mult))
            chain(TTn(le[:], le[:], t32[:], ALU.add))
            first_max(oh2[:], le[:], rs[:, 2, :], NE, t32[:])
            TTn(asn[:], oh1[:], oh2[:], ALU.add).then_inc(S["asn_ok"], 1)
            TTn(rs[:, 4, :], rs[:, 2, :], rs[:, 1, :], ALU.subtract).then_inc(S["r_e2"], 1)
            dve.wait_ge(S["r_exp"], 1)
            chain(V.reduce_sum(rs[:, 3, :], tg[:], axis=X))
            dve.wait_ge(S["r_exp"], 2)
            chain(TS(rs[:, 6, :], rs[:, 5, :], 1.0, None, ALU.add))
            chain(TTn(rs[:, 6, :], rs[:, 6, :], rs[:, 3, :], ALU.mult))
            chain(V.reciprocal(wts[:, 0, :], rs[:, 6, :]))
            chain(TTn(wts[:, 1, :], wts[:, 0, :], rs[:, 5, :], ALU.mult))
            dve.wait_ge(S["pf_done"], 1)
            cnt, nov, end, beg = (ovs[:, k, :] for k in range(4))
            chain(V.tensor_copy(cnt, ps[:, 7, TT * NE:(TT + 1) * NE]))
            chain(TS(nov, cnt, float(SLOTS), None, ALU.is_gt))
            for k in range(2, OVMAX + 1):
                chain(STT(nov, cnt, float(SLOTS * k), nov, ALU.is_gt, ALU.add))
            chain(V.tensor_tensor_scan(end, cst[:, C_ONE:C_ONE + NE], nov, 0.0, ALU.mult, ALU.add))
            chain(TTn(beg, end, nov, ALU.subtract))
            jv = cst[:, C_EID:C_EID + MAXOV].unsqueeze(2).broadcast_to([P, MAXOV, NE])
            ev = cst[:, C_EID:C_EID + NE].unsqueeze(1).broadcast_to([P, MAXOV, NE])
            chain(TTn(jex[:], jv, beg.unsqueeze(1).broadcast_to([P, MAXOV, NE]), ALU.is_ge))
            chain(TTn(jey[:], jv, end.unsqueeze(1).broadcast_to([P, MAXOV, NE]), ALU.is_lt))
            chain(TTn(jex[:], jex[:], jey[:], ALU.mult))
            chain(TTn(jex[:], jex[:], ev, ALU.mult))
            chain(V.reduce_sum(jef[:, NE:JOBS - 1], jex[:], axis=X))
            V.tensor_copy(jef[:, 0:NE], cst[:, C_EID:C_EID + NE])
            chain(V.tensor_copy(jef[:, JOBS - 1:JOBS], end[:, NE - 1:NE]))
            V.tensor_copy(jtab[:], jef[:]).then_inc(S["jei_ok"], 1)
            chain(TS(beg, beg, float(SLOTS), float(SLOTS * (NE - 1)), ALU.mult, ALU.add))
            chain(STT(beg, cst[:, C_EID:C_EID + NE], -float(SLOTS), beg, ALU.mult, ALU.add))
            chain(V.memset(slot[:], 0.0))
            chain(V.memset(t32[:], 0.0))
            for t in range(TT):
                r = rows(t)
                V.tensor_copy(slot[0:r, t, :], ps[0:r, 7, t * NE:(t + 1) * NE])
                chain(STT(t32[0:r, t, :], ps[0:r, 7, t * NE:(t + 1) * NE], float(SLOTS), beg[0:r, :], ALU.is_ge, ALU.mult))
                chain(TTn(slot[0:r, t, :], slot[0:r, t, :], t32[0:r, t, :], ALU.add))
                chain(STT(slot[0:r, t, :], cst[0:r, C_EID:C_EID + NE], float(SLOTS), slot[0:r, t, :], ALU.mult, ALU.add))
            for k, oh in enumerate((oh1, oh2)):
                chain(TTn(t32[:], oh[:], slot[:], ALU.mult))
                chain(V.reduce_sum(rs[:, 6 + k, :], t32[:], axis=X))
            chain(V.tensor_copy(dst[:], rs[:, 6:8, :]))
            dve.sem_inc(S["dst_ok"], 1)

            dve.wait_ge(S["z_out"], 16)
            dve.wait_ge(S["hn_out"], 16 * TT)

            def low_part(J, i):
                dve.wait_ge(S["hi_ok"], J * 6 + (i + 1))
                TTn(low[:, i, :], raw[:, i, :], hiw[:, i, :].bitcast(F32), ALU.subtract).then_inc(S["lo_ok"], 1)

            def none_low(n):
                dve.wait_ge(S["lo_ok"], n)
                dve.sem_inc(S["lo_ok"], 2)

            def work(J, first=False, second=False, last=False):
                if last:
                    none_low(J * 6)
                else:
                    low_part(J, G0)
                    dve.wait_ge(S["x_hi"], J + 1)
                    TTn(xpack[:, :, SLOTS:2 * SLOTS], ps[:, 3, :].rearrange("p (c s) -> p c s", s=SLOTS),
                        xpack[:, :, 0:SLOTS].bitcast(F32), ALU.subtract).then_inc(S["x_lo"], 1)
                    low_part(J, G1)
                if first:
                    none_low(2)
                else:
                    dve.wait_ge(S["silu_ok"], J)
                    dve.wait_ge(S["used"], J * 6 + 4)
                    TTn(hT32[:].rearrange("p c s -> p (c s)"), sg[:], ps[:, 2, 256:512], ALU.mult).then_inc(S["hT_ok"], 1)
                    dve.wait_ge(S["hT_ok"], J * 2)
                    V.tensor_copy(hpack[:, :, 0:SLOTS], hT32[:]).then_inc(S["hT_ok"], 1)
                    dve.wait_ge(S["hT_ok"], J * 2 + 1)
                    TTn(hpack[:, :, SLOTS:2 * SLOTS], hT32[:], hpack[:, :, 0:SLOTS].bitcast(F32), ALU.subtract)\
                        .then_inc(S["h_ok"], 1)
                    if not second:
                        rows_out(J)
                    low_part(J, D0)
                    low_part(J, D1)
                if not last:
                    low_part(J, U0)
                    low_part(J, U1)

            def rows_out(J):
                dve.wait_ge(S["ylo_ok"], J - 1)
                dve.wait_ge(S["ysb_free"], J - 1)
                TTn(ysb[0:SLOTS, :], both(5, SLOTS), ylo[0:SLOTS, :], ALU.add).then_inc(S["y_ok"], 1)

            dve.sem_inc(S["hT_ok"], 1)
            dve.sem_inc(S["y_ok"], 1)
            n = rounds(dve, work)
            rows_out(n + 1)

            def weigh(t):
                r = rows(t)
                dve.wait_ge(S[f"ya{t % 3}"], 32 * (t // 3 + 1))
                chain(STT(h[0:r, t, :], yga[0:r, t % 3, 0, :], wts[0:r, 0, t:t + 1], h[0:r, t, :], ALU.mult, ALU.add))
                STT(h[0:r, t, :], yga[0:r, t % 3, 1, :], wts[0:r, 1, t:t + 1], h[0:r, t, :], ALU.mult, ALU.add)\
                    .then_inc(S["f_h2"], 1)

            def normed(t):
                r = rows(t)
                rms(rn[0:r, t:t + 1])
                if t >= 2:
                    dve.wait_ge(S["f_tr"], t - 1)
                TS(h2n[0:r, t % 2, :], h[0:r, t, :], rn[0:r, t:t + 1], None, ALU.mult).then_inc(S["f_hn"], 1)

            def columns(t):
                r, b = rows(t), 2 * (t % 2)
                dve.wait_ge(S["f_tr"], t + 1)
                if t >= 2:
                    dve.wait_ge(S["f_mm"], t - 1)
                TTn(hpT[:, t % 2, :, 0:r], ps[:, b:b + 2, :].rearrange("p k (c n) -> p (k c) n", n=P)[:, :, 0:r],
                    gple[:].unsqueeze(2).broadcast_to([P, DC, r]), ALU.mult).then_inc(S["f_hpT"], 1)

            for t in range(2):
                weigh(t)
                normed(t)
                columns(t)
            weigh(2)
            normed(2)
            weigh(3)
            weigh(4)
            for t in range(TT):
                r, b = rows(t), 4 + 2 * (t % 2)
                gate = sgt[0:r, t % 2, :]
                if t >= 2:
                    dve.wait_ge(S[f"f_out{t % 2}"], 16 * (t // 2))
                dve.wait_ge(S["f_mm"], t + 1)
                TTn(gate, both(b, r), bpg[0:r, :], ALU.add).then_inc(S["f_z"], 1)
                if t + 3 < TT:
                    normed(t + 3)
                if t + 2 < TT:
                    columns(t + 2)
                dve.wait_ge(S["f_sig"], t + 1)
                chain(TTn(gate, gate, plo[0:r, t, :], ALU.mult))
                TTn(gate, gate, h[0:r, t, :], ALU.add).then_inc(S["f_o"], 1)


def kernel(**inputs):
    import concourse.bacc as _bacc
    from concourse.bass_utils import run_bass_kernel_spmd as _run

    nc = _bacc.Bacc("TRN2", target_bir_lowering=False, num_devices=1)
    consts, buckets, tok = constants()
    shapes = {
        "x_prompt": (SEQ, D), "x_sample": (NS, D), "p_prompt": (SEQ, PLE), "p_sample": (NS, PLE),
        "state_conv": (NB * 2, CONV), "page_table": (NB, PAST // PAGE), "conv_w": (3, CONV),
        "q_norm": (HD,), "k_norm": (NBR, HD), "norm_mix": (D,), "norm_ffn": (D,), "norm_ple": (D,), "b_ple_gate": (D,),
        "b_router_group": (NG,), "b_router_expert": (NE,), "rel_bias": (NBUCK, NH),
        "cache_k_win": (NB, PAST, P), "cache_v_win": (NB, PAST, P),
    }
    arrays, a, o = {}, {}, {}

    def put(name, x):
        arrays[f"in_{name}"] = x
        a[name] = nc.dram_tensor(f"in_{name}", x.shape, mybir.dt.from_np(x.dtype), kind="ExternalInput").ap()

    for name, x in inputs.items():
        x = np.ascontiguousarray(x)
        if name in shapes:
            x = x.reshape(shapes[name])
        elif name.startswith("cache_"):
            x = x.reshape(x.shape[1], PAGE, P)
        else:
            x = x.reshape(x.shape[1:])
        put(name, x)
    put("consts", consts)
    put("buckets", buckets)
    put("tok", tok)
    kv = ("k_cmp", "v_cmp", "k_slc", "v_slc", "k_win", "v_win")
    outs = [("y_prompt", (SEQ, D), (1, SEQ, D)), ("y_sample", (NS, D), (NB, NT, D))]
    outs += [(n + "_p", (SEQ, P), (1, 1, SEQ, NKV, HD)) for n in kv]
    outs += [("conv_p", (2, CONV), (1, 1, 2, CONV))]
    outs += [(n + "_s", (NS, P), (1, NB, NT, NKV, HD)) for n in kv[:4]]
    outs += [(n + "_s", (NB, PAST, P), (1, NB, PAST, NKV, HD)) for n in kv[4:]]
    outs += [("conv_s", (NB * 2, CONV), (1, NB, 2, CONV))]
    for name, shape, _ in outs:
        o[name] = nc.dram_tensor(f"out_{name}", shape, F32, kind="ExternalOutput").ap()
    build(nc, a, o)
    r = _run(nc, [arrays], core_ids=[0])
    return tuple(r.results[0][f"out_{name}"].reshape(full) for name, _, full in outs)
```

```python
from contextlib import ExitStack

import numpy as np
import concourse.bass as bass
from concourse import mybir

F32 = mybir.dt.float32
F32R = mybir.dt.float32r
I32 = mybir.dt.int32
ALU = mybir.AluOpType
ACT = mybir.ActivationFunctionType
X = mybir.AxisListType.X

P = 128
D = 1024
DC = D // P
SEQ, NB, NT = 512, 8, 4
NS = NB * NT
N = SEQ + NS
TP = SEQ // P
TT = TP + 1
CONV, HD, NH, NKV = 512, 64, 8, 2
G = NH // NKV
CC = CONV // P
PAST, PAGE = 256, 128
NPG = NB * PAST // PAGE
STRIDE = 16
NCP = SEQ // STRIDE - 1
CS = PAST // STRIDE
NCH = NB * CS
XC = NCH + SEQ // STRIDE + 2
CH = 256
NBR = 3
NE, NG, DE = 32, 4, 512
EG = NE // NG
SLOTS = 64
MAXOV = (2 * N - 1) // SLOTS
JOBS = NE + MAXOV + 1
OVMAX = (N - 1) // SLOTS
PLE = 256
EPS = 1e-6
BIG = 1e30
NBUCK = 32
BREF = 511
BL = 640
KEYS_S = PAST + NT
KC, VC, KS, VS, KW, VW = [i * P for i in range(6)]

C_ID, C_TRI, C_ONE, C_II, C_DESC, C_EID, C_NM, C_HM, C_SEL, C_END = np.cumsum(
    [0, P, P, P, SLOTS, NE, NE, NH, NKV, 2 * P]).tolist()


def rows(t):
    return P if t < TP else NS


def constants():
    c = np.zeros((P, C_END), np.float32)
    i = np.arange(P)
    c[:, C_ID:C_TRI] = np.eye(P)
    c[:, C_TRI:C_ONE] = i[:, None] < i[None, :]
    c[:, C_ONE:C_II] = 1.0
    c[:, C_II:C_DESC] = (i[:, None] % SLOTS) == np.arange(SLOTS)[None, :]
    c[:, C_DESC:C_EID] = NE - np.arange(NE)
    c[:, C_EID:C_NM] = np.arange(NE)
    head = (i % 32) // NT
    c[:, C_NM:C_HM] = head[:, None] == np.arange(NH)
    c[:, C_HM:C_SEL] = (head // G)[:, None] == np.arange(NKV)
    for rt in range(2):
        tok = (rt * 4 + i // 32) * NT + i % NT
        c[:NS, C_SEL + rt * P:C_SEL + (rt + 1) * P] = np.arange(NS)[:, None] == tok[None, :]
    dist = BREF - np.arange(BL)
    n = np.maximum(dist, 0)
    exact = NBUCK // 2
    nf = np.maximum(n, 1).astype(np.float32)
    large = exact + (np.log(nf / np.float32(exact)) / np.float32(np.log(128 / exact))
                     * np.float32(NBUCK - exact)).astype(np.int32)
    bucket = np.where(n < exact, n, np.minimum(large, NBUCK - 1))
    b = np.zeros((NBUCK + 1, BL), np.float32)
    b[bucket, np.arange(BL)] = 1.0
    b[NBUCK] = dist < 0
    tok = np.zeros((P, TT), np.int32)
    for t in range(TT):
        tok[:, t] = t * P + i
    tok[NS:, TP] = 0
    return c, b, tok


class Chain:

    def __init__(self, eng, sem):
        self.eng, self.sem, self.n = eng, sem, 0

    def __call__(self, ins):
        self.n += 1
        ins.then_inc(self.sem, 1)
        self.eng.wait_ge(self.sem, self.n)


SEMS = """
M_in SM_in X_ev X_in X_tr asn_ok bl_out bl_ps bl_sb cb_done cb_ok cm_done cm_exp cm_o cm_p cm_pT
cm_pv cm_sub cm_tr cs_out cs_outd cs_ps cst_in ct_done ct_ok cv_done cv_ok cv_u cv_vec cv_vecc cv_xh
dst_ok dve_chain eps_ok f_h2 f_hn f_hpT f_mm f_o f_out0 f_out1 f_pl f_ple f_sig f_tr f_z g_exp g_ok
g_ps gath gt_done gu_copied hT_ok h_ok hi_ok hid_b hid_done hid_gelu hn_done hn_out ht_done ht_ok
ic_ok idx_in jei_ok kc_in kcmp_out kt_done kt_ok kv_copied kvout lo_ok op_done op_h ot_ok ot_ps
passed pf_done ple_in pt_in r_done r_e2 r_exp r_log raw0 raw1 raw2 raw3 raw4 raw5 rb_in rb_ok
root_ok s_qbd sc_out silu_ok so_ok so_ps sq_done ss_done ss_exp ss_o ss_pT ss_pv ss_soft ss_sum
ss_tr tm_done tm_norm tr_done tr_k tr_q u_exp u_o u_pT u_pv u_s u_soft u_tr used vc_in vcmp_out
vec_in w1_in w2_in wc0 wc1 wc2 wc3 winout wout_in wpg_in wq0 wq1 wr_in x0_in x1_in x2_in x3_in x4_in
xT_ok xT_t x_hi x_lo x_tr xn_done y_ok y_out ya0 ya1 ya2 ylo_ok ysb_free yz_ok yz_out z_ok z_out
"""


def bcast(ap, n):
    return bass.AP(tensor=ap.tensor, offset=ap.offset, ap=[[0, P], [1, n]])


def build(nc, a, o):
    ctx = ExitStack()
    with ctx:
        base, K = 16512, 1024

        def at(name, shape, off, dt=F32):
            return nc.alloc_sbuf_tensor_at(name, shape, dt, offset=base + int(off))

        def run_of(start):
            cur = [int(start)]

            def place(name, shape, dt=F32):
                off = cur[0]
                cur[0] += -(-int(np.prod(shape[1:])) * 4 // 32) * 32
                return at(name, shape, off, dt)
            return place, cur

        wring = at("wring", [P, 3, DC * 512], 0)
        raw = at("raw", [P, 6, 2048], 0)
        qz = at("qz", [P, NH, SEQ], 16 * K)
        h = at("h", [P, TT, D], 48 * K)
        xT = at("xT", [P, DC, N], 68 * K)
        hiw = at("hiw", [P, 6, 2048], 92 * K, F32R)
        low = at("low", [P, 6, 2048], 140 * K, F32R)
        mixT = at("mixT", [P, DC, N], 86 * K)
        blrow = at("blrow", [P, BL], 96 * K)
        kvt = at("kvt", [P, TT, 6 * P], 103.5 * K)
        junk = at("junk", [P, D], 104 * K)
        qT = at("qT", [P, G, N], 118.5 * K)
        ksT = at("ksT", [P, N], 127 * K)
        kwT = at("kwT", [P, N], 129.25 * K)
        M = at("M", [P, NH, 512], 131.5 * K)
        xn = at("xn", [P, 2, D], 131.5 * K)
        hidt = at("hidt", [P, 2, 2 * XC], 131.5 * K)
        sq = at("sq", [P, D], 139.5 * K)
        qn = at("qn", [P, 2, 512], 143.5 * K)
        RB = 147.5 * K
        X1 = at("X1", [P, 2048], RB)
        X2 = at("X2", [P, 2048], RB + 8 * K)
        w1s = at("w1s", [P, 16, CH], RB + 16 * K)
        XT = at("XT", [P, 8, 2 * XC], RB + 32 * K)
        kcache = at("kcache", [P, NPG, P], RB)
        vcache = at("vcache", [P, NPG, P], RB + 8 * K)
        kcT = at("kcT", [P, NPG, P], RB + 16 * K)
        wout = at("wout", [P, DC, D], RB)
        gffn = at("gffn", [P, D], RB + 32 * K)
        hnt = at("hnt", [P, D], RB + 36 * K)
        cpT = at("cpT", [P, NH, P], RB + 36 * K)
        upp = at("upp", [P, SEQ + 2], 134.5 * K)
        ups = at("ups", [P, NB, 2 + NT], 136.75 * K)
        nsq = at("nsq", [P, P], 137 * K)
        cs_out = at("cs_out", [18, CONV], 143.5 * K)
        cs_in = at("cs_in", [P, CC, 2 + 2 * NB], 145.5 * K)
        sc = at("sc", [P, 2, 512], 68 * K)
        pr = at("pr", [P, 2, 512], 72 * K)
        pT = at("pT", [P, 2, 512], 76 * K)
        oacc = at("oacc", [P, 512], 80 * K)
        cms = at("cms", [P, 256], 82 * K)
        cme = at("cme", [P, 256], 83 * K)
        wr = at("wr", [P, DC, NG + NE], 118.5 * K)
        br = at("br", [P, NG + NE], 120 * K)
        rsmall, rcur = run_of(108 * K)
        lg = rsmall("lg", [P, TT, NG + NE])
        og = rsmall("og", [P, TT, NG])
        tg = rsmall("tg", [P, TT, NG])
        le = rsmall("le", [P, TT, NE])
        t32 = rsmall("t32", [P, TT, NE])
        oh1 = rsmall("oh1", [P, TT, NE])
        oh2 = rsmall("oh2", [P, TT, NE])
        asn = rsmall("asn", [P, TT, NE])
        slot = rsmall("slot", [P, TT, NE])
        ovs = rsmall("ovs", [P, 4, NE])
        cum = rsmall("cum", [P, TT, NE])
        rs = rsmall("rs", [P, 8, TT])
        e64 = rsmall("e64", [P, NE])
        jex = rsmall("jex", [P, MAXOV, NE])
        jey = rsmall("jey", [P, MAXOV, NE])
        jef = rsmall("jef", [P, JOBS])
        zslot = rsmall("zslot", [SLOTS, JOBS], I32)
        assert rcur[0] <= 118.5 * K
        xg = at("xg", [P, D], 68 * K)
        xpack = at("xpack", [P, DC, 2 * SLOTS], 72 * K, F32R)
        Sg = at("Sg", [P, 2, 512], 76 * K)
        sg = at("sg", [P, 256], 80 * K)
        hT32 = at("hT32", [P, 4, SLOTS], 81 * K)
        hpack = at("hpack", [P, 4, 2 * SLOTS], 82 * K, F32R)
        ylo = at("ylo", [P, D], 84 * K)
        ysb = at("ysb", [P, D], 88 * K)
        wpg = at("wpg", [P, DC, D], 0)
        wple = at("wple", [P, 2, D], 32 * K)
        bpg = at("bpg", [P, D], 40 * K)
        yga = at("yga", [P, 3, 2, D], 68 * K)
        plo = at("plo", [P, TT, D], 124 * K)
        pin = at("pin", [P, TT, PLE], 144 * K)
        plT = at("plT", [P, 2, N], 149 * K)
        h2n = at("h2n", [P, 2, D], 157 * K)
        hpT = at("hpT", [P, 2, DC, P], 165 * K)
        sgt = at("sgt", [P, 2, D], 173 * K)
        junk2 = at("junk2", [P, D], 181 * K)
        vwin = at("vwin", [P, NPG, P], 40 * K)
        small, scur = run_of(190.5 * K)
        cst = small("cst", [P, C_END])
        gk = small("gk", [P, 2, P])
        gmix = small("gmix", [P, DC])
        gple = small("gple", [P, DC])
        gq = small("gq", [P, 1])
        gk0 = small("gk0", [P, 1])
        cwT = small("cwT", [P, 12])
        ssq = small("ssq", [P, TT])
        rn = small("rn", [P, TT])
        ss12 = small("ss12", [P, 12])
        gates = small("gates", [P, TT, 24])
        w2s = small("w2s", [P, 2, HD])
        eps = small("eps", [P, 1])
        hb = small("hb", [P, 2])
        vcb = small("vcb", [P, P])
        vcp = small("vcp", [P, P])
        kcbT = small("kcbT", [P, NCH])
        kcpT = small("kcpT", [P, 32])
        Qbd = small("Qbd", [P, NB, 32])
        SM = small("SM", [P, KEYS_S])
        cmb = small("cmb", [P, 2, NCH])
        nmk = small("nmk", [P, 2, NS])
        st = small("st", [P, 40])
        gs = small("gs", [P, 2, NBR])
        tok = small("tok", [P, TT], I32)
        osam = small("osam", [P, 2, P])
        kcb, kcp, g24 = osam[:, 0, :], osam[:, 1, :], osam[:, 1, 0:24]
        upst = small("upst", [P, CC, 2 * NB])
        wts = small("wts", [P, 2, TT])
        dst = small("dst", [P, 2, TT], I32)
        jtab = small("jtab", [P, JOBS], I32)
        pti = small("pti", [P, NPG], I32)
        sidx = small("sidx", [SLOTS, JOBS], I32)
        icur = small("icur", [SLOTS, 1], I32)
        assert scur[0] <= 229360 - base, scur[0]

        ps = ctx.enter_context(nc.psum_tensor("ps", [P, 8, 512], F32))
        bline = nc.dram_tensor("biaslines", (NH, P, BL), F32).ap()
        hn_d = nc.dram_tensor("hn_rows", (N, D), F32).ap()
        y_d = nc.dram_tensor("expert_rows", ((JOBS - 1) * SLOTS, D), F32).ap()
        slot_d = nc.dram_tensor("slot_token", (JOBS * SLOTS, 1), I32).ap()

        S = {n: ctx.enter_context(nc.semaphore(n)) for n in SEMS.split()}
        block = ctx.enter_context(nc.Block())

        def eye(n):
            return cst[0:n, C_ID:C_ID + n]

        kv_out = list(enumerate(("k_cmp", "v_cmp", "k_slc", "v_slc", "k_win", "v_win")))
        w_in = a["w_in"].rearrange("(p c) n -> p c n", c=DC)
        TM = [(3 * CONV, 512), (3 * CONV + 512, 512), (3 * CONV + 1024, 280)]
        WGU = [a[f"w_exp_{x}"].rearrange("e (p k c) n -> e p k (c n)", k=2, c=4) for x in ("gate", "up")]
        WD = a["w_exp_down"].rearrange("e (p k c) n -> e p k (c n)", k=2, c=2)
        PIECES = [(WGU[0], 0, 0), (WGU[0], 1, 0), (WD, 0, 1), (WD, 1, 1), (WGU[1], 0, 0), (WGU[1], 1, 0)]
        G0, G1, D0, D1, U0, U1 = range(6)

        def load_piece(sp, J, i, e, first=False):
            src, half, _ = PIECES[i]
            if first:
                part = src[0, :, half, :]
            else:
                sp.wait_ge(S["lo_ok"], J * 6 + (i - 5))
                part = src[bass.ds(e, 1), :, half, :].rearrange("e p n -> p (e n)")
            sp.dma_start(raw[:, i, :], part).then_inc(S[f"raw{i}"], 16)

        def load_round(sp, J, e, before):
            for i in range(6):
                load_piece(sp, J, i, before if PIECES[i][2] else e)

        def arrival(J, i):
            return (J + (1 - PIECES[i][2])) * 16

        def rounds(eng, work):
            work(0, first=True)
            work(1, second=True)
            with eng.Fori(2, NE) as J:
                work(J)
            nov = eng.value_load(jtab[0:1, JOBS - 1:JOBS], min_val=0, max_val=MAXOV)
            with eng.If(nov > 0):
                with eng.Fori(NE, nov + NE) as J:
                    work(J)
            n = total(eng)
            work(n, last=True)
            return n

        def total(eng):
            return eng.value_load(jtab[0:1, JOBS - 1:JOBS], min_val=0, max_val=MAXOV) + NE

        def token_cols(dve, done, t, gain, b, ok):
            r = rows(t)
            dve.wait_ge(done, t + 1)
            src = ps[:, b:b + 2, :].rearrange("p k (c n) -> p (k c) n", n=P)[:, :, 0:r]
            to = xT[:, :, t * P:t * P + r]
            if gain is None:
                nc.vector.tensor_copy(to, src).then_inc(ok, 1)
            else:
                nc.vector.tensor_tensor(to, src, gain[:].unsqueeze(2).broadcast_to([P, DC, r]), ALU.mult).then_inc(ok, 1)

        UNITS = TP * NH * 2

        def width(u):
            return P * (u // (2 * NH) + 1)

        def blocks(i):
            return P // STRIDE * (i + 1) - 1

        @block.sync
        def _(sp):
            sp.dma_start(cst[:], a["consts"]).then_inc(S["cst_in"], 16)
            for t in range(TP):
                sp.dma_start(h[:, t, :], a["x_prompt"][t * P:(t + 1) * P, :]).then_inc(S[f"x{t}_in"], 16)
            sp.dma_start(h[0:NS, TP, :], a["x_sample"]).then_inc(S[f"x{TP}_in"], 16)
            for g, (c0, n) in enumerate(TM):
                sp.dma_start(wring[:, g, 0:DC * n].rearrange("p (c n) -> p c n", n=n),
                             w_in[:, :, c0:c0 + n]).then_inc(S[f"wq{min(g, 1)}"], 16)
            sp.dma_start(pti[0:1, :], a["page_table"].rearrange("(x b) n -> x (b n)", x=1)).then_inc(S["pt_in"], 16)
            sp.wait_ge(S["pt_in"], 16)

            def page(lp):
                return sp.value_load(pti[0:1, lp:lp + 1], min_val=0, max_val=a["cache_k_cmp"].shape[0] - 1)

            def chunk_rows(which, arrived):
                src = a[f"cache_{which}_cmp"].rearrange("g (c r) n -> g c (r n)", r=STRIDE)
                for lp in range(NPG):
                    pg = page(lp)
                    for hh in range(NKV):
                        sp.dma_start(X1[8 * lp:8 * lp + 8, D * hh:D * (hh + 1)].rearrange("c (r d) -> c r d", d=HD),
                                     src[bass.ds(pg, 1), :, :].rearrange("x c (r g d) -> (x c) r g d", g=NKV, d=HD)[:, :, hh, :])\
                            .then_inc(arrived, 16)
                r0 = SEQ // STRIDE
                for hh in range(NKV):
                    sp.dma_start(X2[r0:r0 + 2, :].rearrange("b (g r d) -> b r g d", g=NKV, d=HD)[:, :, hh, :],
                                 a[f"cmp_pe_{which}"].rearrange("(b r) d -> b r d", b=2)).then_inc(arrived, 16)

            def back(which, arrived):
                sp.wait_ge(S[f"{which}cmp_out"], 16)
                for hh in range(NKV):
                    sp.dma_start(X2[0:SEQ // STRIDE, D * hh:D * (hh + 1)].rearrange("c (r d) -> c r d", d=HD),
                                 o[f"{which}_cmp_p"].rearrange("(c r) (g d) -> c r g d", r=STRIDE, g=NKV)[:, :, hh, :])\
                        .then_inc(arrived, 16)

            sp.dma_start(w1s[:], a["cmp_w1_k"].rearrange("(k p) n -> p k n", p=P)).then_inc(S["w1_in"], 16)
            sp.dma_start(w2s[:], a["cmp_w2_k"].rearrange("(m p) n -> p m n", p=P)).then_inc(S["w2_in"], 16)
            chunk_rows("k", S["X_in"])
            sp.wait_ge(S["bl_sb"], 1)
            sp.dma_start(bline, blrow[0:NH, :].unsqueeze(1).broadcast_to([NH, P, BL])).then_inc(S["bl_out"], 16)
            sp.wait_ge(S["kv_copied"], TP)
            for i, nm in kv_out:
                if i == 2:
                    back("k", S["X_in"])
                    sp.wait_ge(S["tm_norm"], TT)
                    for j, cn in kv_out[:2]:
                        sp.dma_start(o[cn + "_s"], kvt[0:NS, TP, j * P:(j + 1) * P]).then_inc(S["kvout"], 16)
                done = S["kcmp_out"] if i == 0 else S["vcmp_out"] if i == 1 else S["kvout"]
                sp.dma_start(o[nm + "_p"].rearrange("(t p) c -> p t c", p=P),
                             kvt[:, 0:TP, i * P:(i + 1) * P]).then_inc(done, 16)
                if i in (2, 3):
                    sp.dma_start(o[nm + "_s"], kvt[0:NS, TP, i * P:(i + 1) * P]).then_inc(S["kvout"], 16)
                elif i >= 4:
                    for b in range(NB):
                        sp.dma_start(o[nm + "_s"][b, PAST - NT:PAST, :],
                                     kvt[b * NT:(b + 1) * NT, TP, i * P:(i + 1) * P]).then_inc(S["winout"], 16)
            sp.wait_ge(S["tm_done"], TT)
            for c4 in range(CC):
                if c4 == 3:
                    sp.wait_ge(S["X_ev"], 8)
                    chunk_rows("v", S["X_in"])
                    back("v", S["X_in"])
                    sp.wait_ge(S["hid_done"], 2)
                    sp.dma_start(w1s[:], a["cmp_w1_v"].rearrange("(k p) n -> p k n", p=P)).then_inc(S["w1_in"], 16)
                    sp.wait_ge(S["cv_done"], 3)
                for j in range(3):
                    sp.dma_start(wring[:, c4 % 3, 0:DC * 384].rearrange("p (c n) -> p c n", n=384)[:, :, j * P:(j + 1) * P],
                                 w_in[:, :, j * CONV + c4 * P:j * CONV + (c4 + 1) * P]).then_inc(S[f"wc{c4}"], 16)
            for nm in ("k_win", "v_win"):
                sp.dma_start(o[nm + "_s"][:, 0:PAST - NT, :], a["cache_" + nm][:, NT:PAST, :]).then_inc(S["winout"], 16)
            sp.wait_ge(S["bl_out"], 16)
            for q in range(4):
                for n in range(NH):
                    r0 = 32 * q + NT * n
                    sp.dma_start(SM[r0:r0 + NT, :], bass.AP(tensor=bline.tensor, offset=n * P * BL + BREF - PAST,
                                                            ap=[[BL - 1, NT], [1, KEYS_S]])).then_inc(S["SM_in"], 16)
            sp.wait_ge(S["hid_done"], 4)
            for lp in range(NPG):
                for name, d, arrived in (("cache_k_slc", kcache, "kc_in"), ("cache_v_slc", vcache, "vc_in")):
                    sp.dma_start(d[:, lp, :], a[name][bass.ds(page(lp), 1), :, :].rearrange("x p n -> p (x n)"))\
                        .then_inc(S[arrived], 16)
            sp.wait_ge(S["cv_done"], 9)
            sp.dma_start(vwin[:], a["cache_v_win"].rearrange("b (g p) n -> p (b g) n", p=PAGE)).then_inc(S["vc_in"], 16)
            sp.wait_ge(S["kt_done"], 4)
            sp.dma_start(kcache[:], a["cache_k_win"].rearrange("b (g p) n -> p (b g) n", p=PAGE)).then_inc(S["kc_in"], 16)
            sp.wait_ge(S["cv_ok"], CC)
            sp.wait_ge(S["cb_done"], 2)
            sp.wait_ge(S["cs_outd"], 16 * 2)
            for n in range(NH):
                sp.dma_start(M[:, n, :], bass.AP(tensor=bline.tensor, offset=n * P * BL + P - 1,
                                                 ap=[[BL - 1, P], [1, 512]])).then_inc(S["M_in"], 16)
            for i in (G0, G1, U0):
                load_piece(sp, 0, i, 0, first=True)
            sp.wait_ge(S["ss_pv"], 6)
            load_piece(sp, 0, U1, 0, first=True)
            sp.dma_start(wout[:], a["w_out"].rearrange("(c p) n -> p c n", p=P)).then_inc(S["wout_in"], 16)
            sp.dma_start(gffn[:], bcast(a["norm_ffn"], D)).then_inc(S["wout_in"], 16)
            sp.wait_ge(S["u_soft"], 2 * NH * TP)
            sp.wait_ge(S["cm_sub"], TP)
            sp.dma_start(wr[:, :, 0:NG], a["w_router_group"].rearrange("(p c) n -> p c n", c=DC)).then_inc(S["wr_in"], 16)
            sp.dma_start(wr[:, :, NG:NG + NE], a["w_router_expert"].rearrange("(p c) n -> p c n", c=DC)).then_inc(S["wr_in"], 16)
            sp.dma_start(br[:, 0:NG], bcast(a["b_router_group"], NG)).then_inc(S["wr_in"], 16)
            sp.dma_start(br[:, NG:NG + NE], bcast(a["b_router_expert"], NE)).then_inc(S["wr_in"], 16)
            for t in range(TT):
                sp.wait_ge(S["hn_done"], t + 1)
                sp.dma_start(hn_d[t * P:t * P + rows(t), :], hnt[0:rows(t), :]).then_inc(S["hn_out"], 16)
            for i in range(6):
                if i == 2:
                    sp.wait_ge(S["gath"], 16)
                load_piece(sp, 1, i, 1 - PIECES[i][2])
            with sp.Fori(2, NE) as J:
                load_round(sp, J, J, J - 1)
            sp.wait_ge(S["jei_ok"], 1)

            def expert(J):
                return sp.value_load(jtab[0:1, bass.ds(J, 1)], min_val=0, max_val=NE - 1)

            nov = sp.value_load(jtab[0:1, JOBS - 1:JOBS], min_val=0, max_val=MAXOV)
            with sp.If(nov > 0):
                with sp.Fori(NE, nov + NE) as J:
                    load_round(sp, J, expert(J), expert(J - 1))
            n = total(sp)
            e = expert(n - 1)
            for i in (D0, D1):
                load_piece(sp, n, i, e)
            sp.wait_ge(S["lo_ok"], n * 6)
            sp.dma_start(wple[:], a["w_ple"].rearrange("(p c) n -> p c n", c=2)).then_inc(S["ple_in"], 16)
            sp.wait_ge(S["used"], n * 6 + 6)
            sp.dma_start(pin[:, 0:TP, :], a["p_prompt"].rearrange("(t p) n -> p t n", p=P)).then_inc(S["ple_in"], 16)
            sp.dma_start(pin[0:NS, TP, :], a["p_sample"]).then_inc(S["ple_in"], 16)
            w = a["w_ple_gate"].rearrange("(p c) n -> p c n", c=DC)
            sp.dma_start(wpg[:, 0:4, :], w[:, 0:4, :]).then_inc(S["wpg_in"], 16)
            sp.dma_start(bpg[:], bcast(a["b_ple_gate"], D)).then_inc(S["wpg_in"], 16)
            sp.wait_ge(S["lo_ok"], n * 6 + 4)
            sp.dma_start(wpg[:, 4:8, :], w[:, 4:8, :]).then_inc(S["wpg_in"], 16)
            for t in range(TT):
                sp.wait_ge(S["f_o"], t + 1)
                to = o["y_prompt"][t * P:(t + 1) * P, :] if t < TP else o["y_sample"]
                sp.dma_start(to, sgt[0:rows(t), t % 2, :]).then_inc(S[f"f_out{t % 2}"], 16)
            sp.wait_ge(S["kvout"], 16 * 8)
            sp.wait_ge(S["kcmp_out"], 16)
            sp.wait_ge(S["vcmp_out"], 16)
            sp.wait_ge(S["winout"], 16 * (2 * NB + 2))
            sp.wait_ge(S["cs_outd"], 16 * 2)
            sp.wait_ge(S["f_out0"], 16 * 3)
            sp.wait_ge(S["f_out1"], 16 * 2)

        @block.gpsimd
        def _(pool):
            pool.sem_inc(S["ysb_free"], 1)
            pool.dma_start(gple[:], a["norm_ple"].rearrange("(p c) -> p c", c=DC)).then_inc(S["vec_in"], 16)
            for hh in range(NKV):
                pool.dma_start(gq[hh * HD:(hh + 1) * HD, :], a["q_norm"].rearrange("(p x) -> p x", x=1)).then_inc(S["vec_in"], 16)
                pool.dma_start(gk0[hh * HD:(hh + 1) * HD, :], a["k_norm"][0, :].rearrange("(p x) -> p x", x=1)).then_inc(S["vec_in"], 16)
                for i in range(2):
                    pool.dma_start(gk[:, i, hh * HD:(hh + 1) * HD], bcast(a["k_norm"][i + 1, :], HD)).then_inc(S["vec_in"], 16)
            pool.dma_start(cmb[0:12, 0, :], a["conv_w"].rearrange("k (c p) -> (k c) p", p=P)).then_inc(S["rb_in"], 16)
            pool.dma_start(tok[:], a["tok"]).then_inc(S["vec_in"], 16)
            pool.dma_start(SM[0:NBUCK, 0:NH], a["rel_bias"]).then_inc(S["rb_in"], 16)
            pool.dma_start(mixT[0:NBUCK + 1, 0:2, 0:320], a["buckets"].rearrange("b (k n) -> b k n", k=2)).then_inc(S["rb_in"], 16)
            pool.dma_start(mixT[0:2 * NB, 2, 0:512], a["state_conv"]).then_inc(S["rb_in"], 16)
            nc.gpsimd.memset(mixT[:, 6:8, 0:512], 0.0).then_inc(S["yz_ok"], 1)
            pool.wait_ge(S["yz_ok"], 1)
            pool.wait_ge(S["tm_done"], 2)
            for k in range(MAXOV * SLOTS // P):
                r0 = NE * SLOTS + k * P
                pool.dma_start(y_d[r0:r0 + P, :].rearrange("p (k n) -> p k n", k=2), mixT[:, 6:8, 0:512]).then_inc(S["yz_out"], 16)
            pool.wait_ge(S["yz_out"], 16 * (MAXOV * SLOTS // P))
            pool.wait_ge(S["cv_done"], 6)
            nc.gpsimd.memset(qz[:], 0.0).then_inc(S["yz_ok"], 1)
            pool.wait_ge(S["yz_ok"], 2)
            pool.wait_ge(S["tr_q"], TT)
            for hh in range(NKV):
                p0 = hh * HD
                nc.gpsimd.tensor_copy(qz[p0:p0 + HD, hh * G:(hh + 1) * G, :], qT[p0:p0 + HD, :, 0:SEQ]).then_inc(S["yz_ok"], 1)
            pool.wait_ge(S["z_ok"], 1)
            pool.dma_start(slot_d.rearrange("(s j) x -> s (j x)", s=SLOTS), zslot[:]).then_inc(S["z_out"], 16)
            pool.wait_ge(S["z_out"], 16)
            pool.wait_ge(S["dst_ok"], 1)
            for t in range(TT):
                for k in range(2):
                    pool.indirect_dma_start(out=slot_d, out_offset=bass.IndirectOffsetOnAxis(ap=dst[0:rows(t), k, t:t + 1], axis=0),
                                            in_=tok[0:rows(t), t:t + 1], in_offset=None).then_inc(S["sc_out"], 16)
            pool.wait_ge(S["sc_out"], 16 * 2 * TT)
            with nc.allow_non_contiguous_dma(reason="a slot index is one word"):
                pool.dma_start(sidx[:], slot_d.rearrange("(j s) x -> s (j x)", s=SLOTS)).then_inc(S["idx_in"], 16)
            pool.wait_ge(S["idx_in"], 16)
            pool.wait_ge(S["hn_out"], 16 * TT)

            def gather(J):
                pool.wait_ge(S["x_tr"], J)
                nc.gpsimd.tensor_copy(icur[:], sidx[:, J:J + 1] if isinstance(J, int) else sidx[:, bass.ds(J, 1)])\
                    .then_inc(S["ic_ok"], 1)
                pool.wait_ge(S["ic_ok"], J + 1)
                pool.sem_inc(S["passed"], 1)
                pool.indirect_dma_start(out=xg[0:SLOTS, :], out_offset=None, in_=hn_d,
                                        in_offset=bass.IndirectOffsetOnAxis(ap=icur[:, 0:1], axis=0)).then_inc(S["gath"], 16)

            def work(J, first=False, second=False, last=False):
                if not last:
                    gather(J + 1)
                if not (first or second):
                    rows_leave(J)

            def rows_leave(J):
                pool.wait_ge(S["y_ok"], J)
                pool.dma_start(y_d[bass.ds(J * SLOTS - 2 * SLOTS, SLOTS), :], ysb[0:SLOTS, :]).then_inc(S["y_out"], 16)
                pool.wait_ge(S["y_out"], J * 16 - 16)
                pool.sem_inc(S["ysb_free"], 1)

            gather(0)
            n = rounds(pool, work)
            rows_leave(n + 1)
            for t in range(TT):
                if t >= 3:
                    pool.wait_ge(S["f_h2"], t - 2)
                for k in range(2):
                    pool.indirect_dma_start(out=yga[0:rows(t), t % 3, k, :], out_offset=None, in_=y_d,
                                            in_offset=bass.IndirectOffsetOnAxis(ap=dst[0:rows(t), k, t:t + 1], axis=0))\
                        .then_inc(S[f"ya{t % 3}"], 16)

        @block.scalar
        def _(act):
            A = nc.scalar.activation
            C = ACT.Copy
            act.dma_start(gmix[:], a["norm_mix"].rearrange("(p c) -> p c", c=DC)).then_inc(S["x0_in"], 16)
            sums = []

            def root_of(x, src, n):
                A(x, src, ACT.Sqrt, scale=1.0 / n, bias=eps[0:x.shape[0], 0:1]).then_inc(S["root_ok"], 1)

            def head_roots(r, n):
                sums.append(1)
                act.wait_ge(S["ss_sum"], len(sums))
                root_of(ss12[0:r, 0:n], ss12[0:r, 0:n], HD)

            act.wait_ge(S["eps_ok"], 1)
            for t in range(TT):
                act.wait_ge(S[f"x{t}_in"], 16 if t else 32)
                A(sq[0:rows(t), :], h[0:rows(t), t, :], ACT.Square, accum_out=ssq[0:rows(t), t:t + 1]).then_inc(S["sq_done"], 1)
                act.wait_ge(S["sq_done"], t + 1)
                root_of(rn[0:rows(t), t:t + 1], ssq[0:rows(t), t:t + 1], D)
            act.wait_ge(S["vec_in"], 16 * 10)
            for t in range(TT):
                r, b = rows(t), 3 * (t % 2)
                act.wait_ge(S["tm_done"], t + 1)
                if t == 0:
                    act.wait_ge(S["bl_ps"], 1)
                    A(blrow[0:NH, :].rearrange("p (k n) -> p k n", k=2), ps[0:NH, 6:8, 0:320], C).then_inc(S["bl_sb"], 1)
                if t >= 2:
                    act.wait_ge(S["tr_done"], t - 1)
                q_to = qn[0:r, t % 2, :].rearrange("p (g h d) -> p h g d", g=G, h=NKV)
                if t == TP:
                    for q in range(2):
                        A(q_to[:, q, :, :], ps[NS * q:NS * (q + 1), b, 0:256].rearrange("p (g d) -> p g d", g=G), C)
                        A(kvt[0:r, t, 256 * q:256 * (q + 1)], ps[NS * (q + 2):NS * (q + 3), b, 0:256], C)
                        A(kvt[0:r, t, 512 + P * q:512 + P * (q + 1)], ps[NS * q:NS * (q + 1), b + 1, 0:P], C)
                    A(gates[0:r, t, :], ps[NS * 2:NS * 3, b + 1, 0:24], C).then_inc(S["kv_copied"], 1)
                else:
                    A(q_to, ps[0:r, b, :].rearrange("p (h g d) -> p h g d", h=NKV, g=G), C)
                    A(kvt[0:r, t, 0:512], ps[0:r, b + 1, :], C)
                    A(kvt[0:r, t, 512:768], ps[0:r, b + 2, 0:256], C)
                    A(gates[0:r, t, :], ps[0:r, b + 2, 256:280], C).then_inc(S["kv_copied"], 1)
                head_roots(r, 12)
                if t:
                    act.wait_ge(S["tr_done"], t)
                    A(qT[:, :, (t - 1) * P:t * P], ps[:, 6, :].rearrange("p (g n) -> p g n", g=G), C,
                      scale=gq[:, 0:1]).then_inc(S["tr_q"], 1)
            act.wait_ge(S["tr_done"], TT)
            A(qT[:, :, SEQ:N], ps[:, 6, :].rearrange("p (g n) -> p g n", g=G)[:, :, 0:NS], C,
              scale=gq[:, 0:1]).then_inc(S["tr_q"], 1)

            def hidden(i):
                act.wait_ge(S["hid_b"], i + 1)
                if i:
                    act.wait_ge(S["cb_done"], i)
                for m in range(2):
                    A(hidt[:, m, :], ps[:, 4 + m, 0:2 * XC], ACT.Gelu_apprx_tanh, bias=hb[:, m:m + 1]).then_inc(S["hid_gelu"], 1)

            def conv_xh(c4):
                act.wait_ge(S["cv_done"], 3 * c4 + 1)
                if c4:
                    act.wait_ge(S["cv_u"], c4)
                A(sq[:, 0:N].rearrange("p (k n) -> p k n", k=2), ps[:, 0:2, 0:N // 2], C).then_inc(S["cv_xh"], 1)

            act.wait_ge(S["kv_copied"], TT)
            A(gates[:], gates[:], ACT.Exp, scale=-1.0).then_inc(S["g_exp"], 1)
            hidden(0)
            head_roots(P, 2)
            head_roots(NCP, 2)
            act.wait_ge(S["cb_done"], 1)
            act.dma_start(w2s[:], a["cmp_w2_v"].rearrange("(m p) n -> p m n", p=P)).then_inc(S["w2_in"], 16)
            conv_xh(0)
            conv_xh(1)
            hidden(1)
            conv_xh(2)
            conv_xh(3)
            act.wait_ge(S["cs_out"], 1)
            act.dma_start(o["conv_p"], cs_out[0:2, :]).then_inc(S["cs_outd"], 16)
            act.dma_start(o["conv_s"], cs_out[2:18, :]).then_inc(S["cs_outd"], 16)
            for u in range(6):
                act.wait_ge(S["ss_soft"], u + 1)
                if u >= 2:
                    act.wait_ge(S["ss_tr"], u - 1)
                w = NCH if u < 2 else PAST + NS
                A(pr[:, u % 2, 0:w], sc[:, u % 2, 0:w], ACT.Exp, bias=st[:, u:u + 1], scale=-1.0,
                  accum_out=st[:, 8 + u:9 + u]).then_inc(S["ss_exp"], 1)
            def exps(u):
                w = width(u)
                act.wait_ge(S["u_soft"], u + 1)
                if u >= 2:
                    act.wait_ge(S["u_tr"], u - 1)
                A(pr[:, u % 2, 0:w], sc[:, u % 2, 0:w], ACT.Exp, bias=st[:, 16 + u % 4:17 + u % 4], scale=-1.0,
                  accum_out=st[:, 20 + u % 4:21 + u % 4]).then_inc(S["u_exp"], 1)

            def cm_exps(i):
                nk = blocks(i)
                act.wait_ge(S["cm_sub"], i + 1)
                A(cme[:, 0:NH * nk], cms[:, 0:NH * nk], ACT.Exp).then_inc(S["cm_exp"], 1)

            def cm_columns(i):
                nk = blocks(i)
                act.wait_ge(S["cm_tr"], i + 1)
                if i:
                    act.wait_ge(S["cm_pv"], i)
                A(cpT[0:nk, :, :].rearrange("p (b n) q -> p b (n q)", b=2), ps[0:nk, 6:8, :], C).then_inc(S["cm_pT"], 1)

            cm_exps(0)
            exps(0)
            exps(1)
            cm_columns(0)
            for u in range(UNITS):
                i, k = divmod(u, 2 * NH)
                w = width(u)
                act.wait_ge(S["u_tr"], u + 1)
                if u >= 2:
                    act.wait_ge(S["u_pv"], u - 1)
                A(pT[:, u % 2, 0:w], ps[:, 2 + u % 2, 0:w], C).then_inc(S["u_pT"], 1)
                if u + 2 < UNITS:
                    exps(u + 2)
                if i + 1 < TP and k == 4:
                    cm_exps(i + 1)
                if i + 1 < TP and k == 7:
                    cm_columns(i + 1)
            act.wait_ge(S["kvout"], 16 * 8)
            act.wait_ge(S["kcmp_out"], 16)
            act.wait_ge(S["vcmp_out"], 16)
            act.wait_ge(S["winout"], 16 * (2 * NB + 2))
            for t in range(TT):
                act.wait_ge(S["op_h"], t + 1)
                A(junk[0:rows(t), :], h[0:rows(t), t, :], ACT.Square, accum_out=ssq[0:rows(t), t:t + 1]).then_inc(S["sq_done"], 1)
                act.wait_ge(S["sq_done"], TT + t + 1)
                root_of(rn[0:rows(t), t:t + 1], ssq[0:rows(t), t:t + 1], D)
            act.wait_ge(S["r_log"], 1)
            A(tg[:], tg[:], ACT.Exp).then_inc(S["r_exp"], 1)
            act.wait_ge(S["r_e2"], 1)
            A(rs[:, 5, :], rs[:, 4, :], ACT.Exp).then_inc(S["r_exp"], 1)
            act.wait_ge(S["op_done"], TT)

            A(sg[:, 0:1], eps[:], ACT.Silu)

            def high(J, i):
                act.wait_ge(S[f"raw{i}"], arrival(J, i))
                act.wait_ge(S["used"], J * 6 + (i + 1))
                A(hiw[:, i, :], raw[:, i, :], C).then_inc(S["hi_ok"], 1)

            def none_high(n):
                act.wait_ge(S["hi_ok"], n)
                act.sem_inc(S["hi_ok"], 2)

            def work(J, first=False, second=False, last=False):
                if last:
                    none_high(J * 6)
                elif first:
                    high(J, G0)
                    high(J, G1)
                    none_high(2)
                    high(J, U0)
                    high(J, U1)
                    act.wait_ge(S["x_tr"], J + 1)
                    A(xpack[:, :, 0:SLOTS], ps[:, 3, :].rearrange("p (c s) -> p c s", s=SLOTS), C).then_inc(S["x_hi"], 1)
                    act.wait_ge(S["used"], J * 6 + 8)
                    A(Sg[:, 0, :], ps[:, 0, :], C).then_inc(S["gu_copied"], 1)
                    return
                else:
                    high(J, G0)
                    act.wait_ge(S["x_tr"], J + 1)
                    A(xpack[:, :, 0:SLOTS], ps[:, 3, :].rearrange("p (c s) -> p c s", s=SLOTS), C).then_inc(S["x_hi"], 1)
                act.wait_ge(S["used"], J * 6 + 6)
                A(Sg[:, 1, :], ps[:, 1, :], C).then_inc(S["gu_copied"], 1)
                if not last:
                    high(J, G1)
                if second:
                    act.wait_ge(S["jei_ok"], 1)
                    act.wait_ge(S["z_out"], 16)
                else:
                    rows_low(J)
                act.wait_ge(S["gt_done"], J)
                A(sg[:], ps[:, 2, 0:256], ACT.Silu).then_inc(S["silu_ok"], 1)
                high(J, D0)
                high(J, D1)
                if not last:
                    high(J, U0)
                    act.wait_ge(S["used"], J * 6 + 8)
                    A(Sg[:, 0, :], ps[:, 0, :], C).then_inc(S["gu_copied"], 1)
                    high(J, U1)

            def rows_low(J):
                act.wait_ge(S["used"], J * 6 + 4)
                act.wait_ge(S["y_ok"], J - 1)
                A(ylo[0:SLOTS, :].rearrange("p (k n) -> p k n", k=2), ps[SLOTS:P, 5:7, :], C).then_inc(S["ylo_ok"], 1)

            n = rounds(act, work)
            rows_low(n + 1)
            def embed_T(step, t, n, bank):
                act.wait_ge(S["f_ple"], step)
                r = P if n > 1 else NS
                A(plT[:, :, t * P:t * P + (n - 1) * P + r].rearrange("p c (t n) -> p t c n", n=r),
                  ps[:, bank, 0:n * 2 * P].rearrange("p (t c n) -> p t c n", c=2, n=P)[:, :, :, 0:r], C).then_inc(S["f_pl"], 1)

            def projected(step, t):
                r, b = rows(t), 3 * (t % 2)
                act.wait_ge(S["f_ple"], step)
                A(plo[0:r, t, :].rearrange("p (k n) -> p k n", k=2), ps[0:r, b:b + 2, :], C).then_inc(S["f_pl"], 1)

            def squares(t):
                r = rows(t)
                act.wait_ge(S["f_h2"], t + 1)
                A(junk2[0:r, :], h[0:r, t, :], ACT.Square, accum_out=ssq[0:r, t:t + 1]).then_inc(S["sq_done"], 1)
                act.wait_ge(S["sq_done"], 2 * TT + t + 1)
                root_of(rn[0:r, t:t + 1], ssq[0:r, t:t + 1], D)

            embed_T(1, 0, 2, 7)
            embed_T(2, 2, 2, 2)
            projected(3, 0)
            embed_T(4, 4, 1, 7)
            projected(5, 1)
            projected(6, 2)
            squares(0)
            projected(7, 3)
            projected(8, 4)
            for t in range(1, TT):
                squares(t)
            for t in range(TT):
                r = rows(t)
                act.wait_ge(S["f_z"], t + 1)
                A(sgt[0:r, t % 2, :], sgt[0:r, t % 2, :], ACT.Sigmoid).then_inc(S["f_sig"], 1)

        @block.tensor
        def _(pe):
            T = nc.tensor.transpose

            def mm(out, l, r, start, stop, skip=False):
                return nc.tensor.matmul(out, l, r, start=start, stop=stop, skip_group_check=skip)

            def quarters(bank, x, w):
                for c in range(DC):
                    for q in range(4):
                        last = mm(ps[NS * q:NS * (q + 1), bank, 0:D // 4], x[:, c, :], w[:, c, q * (D // 4):(q + 1) * (D // 4)],
                                  c == 0, c == DC - 1, True)
                return last

            pe.sem_inc(S["used"], 6)
            pe.wait_ge(S["cst_in"], 16)
            def token_T(t, src, b, done):
                v = src.rearrange("r (p c) -> r p c", c=DC)
                for c in range(DC):
                    last = T(ps[:, b + c // 4, (c % 4) * P:(c % 4) * P + rows(t)], v[:, :, c], eye(rows(t)))
                last.then_inc(done, 1)

            for t in range(TT):
                pe.wait_ge(S["xn_done"], t + 1)
                if t >= 2:
                    pe.wait_ge(S["xT_ok"], t - 1)
                token_T(t, xn[0:rows(t), t % 2, :], 2 * (t % 2), S["xT_t"])

            def heads_T(t):
                r = rows(t)
                pe.wait_ge(S["tm_norm"], t + 1)
                if t:
                    pe.wait_ge(S["tr_q"], t)
                    pe.wait_ge(S["tr_k"], t)
                else:
                    pe.wait_ge(S["bl_sb"], 1)
                for g in range(G):
                    T(ps[:, 6, g * P:g * P + r], qn[0:r, t % 2, g * P:(g + 1) * P], eye(r))
                T(ps[:, 7, 0:r], kvt[0:r, t, KS:KS + P], eye(r))
                T(ps[:, 7, P:P + r], kvt[0:r, t, KW:KW + P], eye(r)).then_inc(S["tr_done"], 1)

            pe.wait_ge(S["xT_ok"], TT)
            for t in range(TT):
                r, b = rows(t), 3 * (t % 2)
                if t == 1:
                    pe.wait_ge(S["cv_vecc"], 1)
                if t >= 2:
                    pe.wait_ge(S["kv_copied"], t - 1)
                if t == TP:
                    w = [wring[:, g, 0:DC * n].rearrange("p (c n) -> p c n", n=n) for g, (_, n) in enumerate(TM)]
                    for c in range(DC):
                        for q in range(4):
                            mm(ps[NS * q:NS * (q + 1), b, 0:256], xT[:, c, SEQ:N], w[q // 2][:, c, 256 * (q % 2):256 * (q % 2 + 1)],
                               c == 0, c == DC - 1, True)
                    for c in range(DC):
                        for q, n in enumerate((P, P, 24)):
                            last = mm(ps[NS * q:NS * (q + 1), b + 1, 0:n], xT[:, c, SEQ:N], w[2][:, c, P * q:P * q + n],
                                      c == 0, c == DC - 1, True)
                for g, (c0, n) in enumerate(TM if t < TP else ()):
                    if t == 0 and g < 2:
                        pe.wait_ge(S[f"wq{g}"], 16 + 16 * g)
                    w = wring[:, g, 0:DC * n].rearrange("p (c n) -> p c n", n=n)
                    for c in range(DC):
                        last = mm(ps[0:r, b + g, 0:n], xT[:, c, t * P:t * P + r], w[:, c, :], c == 0, c == DC - 1)
                last.then_inc(S["tm_done"], 1)
                if t == 0:
                    pe.wait_ge(S["rb_in"], 64)
                    pe.wait_ge(S["rb_ok"], 1)
                    for k in range(2):
                        last = mm(ps[0:NH, 6 + k, 0:320], SM[0:NBUCK + 1, 0:NH], mixT[0:NBUCK + 1, k, 0:320], True, True)
                    last.then_inc(S["bl_ps"], 1)
                    T(ps[:, 5, 0:12], cmb[0:12, 0, :], eye(12))
                    for c in range(CC):
                        last = T(ps[:, 5, 16 + 16 * c:32 + 16 * c], mixT[0:2 * NB, 2, c * P:(c + 1) * P], eye(2 * NB))
                    last.then_inc(S["cv_vec"], 1)
                if t:
                    heads_T(t - 1)

            def chunks_T(i, steps):
                pe.wait_ge(S["X_in"], 16 * NKV * (NPG + 2) * (i + 1))
                for pp in steps:
                    if pp >= 4:
                        pe.wait_ge(S["X_ev"], 8 * i + pp - 3)
                    elif i and pp % 2 == 0:
                        pe.wait_ge(S[("cv_xh", "cv_ok")[pp // 2]], 2)
                    for hh in range(NKV):
                        T(ps[:, pp % 4, hh * XC:hh * XC + NCH], X1[:, D * hh + P * pp:D * hh + P * (pp + 1)], eye(P))
                        last = T(ps[:, pp % 4, hh * XC + NCH:(hh + 1) * XC], X2[0:XC - NCH, D * hh + P * pp:D * hh + P * (pp + 1)],
                                 eye(XC - NCH))
                    last.then_inc(S["X_tr"], 1)

            def compress_hidden(i):
                if i:
                    pe.wait_ge(S["cv_u"], 2)
                pe.wait_ge(S["w1_in"], 16 * (i + 1))
                pe.wait_ge(S["X_ev"], 8 * i + 8)
                for m in range(2):
                    for k in range(16):
                        w = w1s[:, k, m * P:(m + 1) * P]
                        if k < 8:
                            last = mm(ps[:, 4 + m, 0:2 * XC], w, XT[:, k, :], k == 0, False)
                        else:
                            nxt = XT[:, k - 8, :].rearrange("p (g n) -> p g n", g=NKV)[:, :, 1:XC]
                            out = ps[:, 4 + m, 0:2 * XC].rearrange("p (g n) -> p g n", g=NKV)[:, :, 0:XC - 1]
                            last = mm(out, w, nxt, False, k == 15)
                    last.then_inc(S["hid_done"], 1)

            def compress_out(i):
                pe.wait_ge(S["hid_gelu"], 2 * i + 2)
                pe.wait_ge(S["w2_in"], 16 * (i + 1))
                if i:
                    pe.wait_ge(S["ct_ok"], 1)
                    pe.wait_ge(S["s_qbd"], 2)
                for hh in range(NKV):
                    for m in range(2):
                        mm(ps[:, 6, hh * HD:(hh + 1) * HD], hidt[:, m, hh * XC:hh * XC + NCH], w2s[:, m, :], m == 0, m == 1)
                for hh in range(NKV):
                    for m in range(2):
                        last = mm(ps[0:NCP, 7, hh * HD:(hh + 1) * HD], hidt[:, m, hh * XC + NCH:hh * XC + NCH + NCP],
                                  w2s[:, m, :], m == 0, m == 1)
                last.then_inc(S["cb_done"], 1)

            def conv(c4, j):
                if j == 0:
                    pe.wait_ge(S[f"wc{c4}"], 48)
                if c4:
                    pe.wait_ge(S[("cv_xh", "cv_ok", "cv_u")[j]], c4)
                w = wring[:, c4 % 3, 0:DC * 384].rearrange("p (c n) -> p c n", n=384)
                for half in range(2):
                    for c in range(DC):
                        last = mm(ps[:, 2 * j + half, 0:N // 2], w[:, c, j * P:(j + 1) * P],
                                  xT[:, c, half * (N // 2):(half + 1) * (N // 2)], c == 0, c == DC - 1)
                last.then_inc(S["cv_done"], 1)

            pe.wait_ge(S["kv_copied"], TT)
            chunks_T(0, range(4))
            heads_T(TP)
            chunks_T(0, range(4, 8))
            compress_hidden(0)
            conv(0, 0)
            pe.wait_ge(S["tr_q"], TT)
            pe.wait_ge(S["tr_k"], TT)
            compress_out(0)
            conv(0, 2)
            conv(0, 1)
            pe.wait_ge(S["cb_ok"], 1)
            pe.wait_ge(S["g_ok"], 1)
            for rt in range(2):
                mm(ps[:, 7, 256 + 32 * rt:280 + 32 * rt], cst[0:NS, C_SEL + rt * P:C_SEL + (rt + 1) * P], gates[0:NS, TP, :],
                   True, True, True).then_inc(S["g_ps"], 1)
            T(ps[:, 6, 256:256 + NCH], kcb, eye(P))
            T(ps[:, 6, 384:384 + NCP], kcp[0:NCP, :], eye(NCP)).then_inc(S["ct_done"], 1)
            for j in (0, 2, 1):
                conv(1, j)
            chunks_T(1, range(8))
            compress_hidden(1)
            conv(2, 0)
            compress_out(1)
            conv(2, 2)
            conv(2, 1)
            for j in (0, 2, 1):
                conv(3, j)
            pe.wait_ge(S["cv_ok"], CC)
            pe.wait_ge(S["cb_ok"], 2)
            for c in range(CC):
                last = T(ps[0:18, 7, c * P:(c + 1) * P], cs_in[:, c, :], eye(P))
            last.then_inc(S["cs_ps"], 1)

            def qrows(rt):
                return Qbd[:, 4 * rt:4 * rt + 4, :].rearrange("p b r -> p (b r)")

            def keys_T(i, n):
                pe.wait_ge(S["kc_in"], n)
                for b in range(4):
                    if i:
                        pe.wait_ge(S["kt_ok"], 4)
                        pe.wait_ge(S["ss_done"], 4)
                    for j in range(4):
                        last = T(ps[:, b, j * P:(j + 1) * P], kcache[:, 4 * b + j, :], eye(P))
                    last.then_inc(S["kt_done"], 1)

            def ss_scores(u):
                bank, rt = 4 + u % 2, u % 2
                if u >= 2:
                    pe.wait_ge(S["ss_soft"], u - 1)
                if u < 2:
                    last = mm(ps[:, bank, 0:NCH], qrows(rt), kcbT[:], True, True)
                else:
                    newT = ksT if u < 4 else kwT
                    pe.wait_ge(S["kt_ok"], 4 if u < 4 else 8)
                    mm(ps[:, bank, PAST:PAST + NS], qrows(rt), newT[:, SEQ:N], True, True, True)
                    for q in range(4):
                        b = 4 * rt + q
                        last = nc.tensor.matmul(ps[32 * q:32 * q + 32, bank, 0:PAST], Qbd[:, b, :],
                                                kcT[:, 2 * b:2 * b + 2, :].rearrange("p g n -> p (g n)"),
                                                start=True, stop=True, skip_group_check=True)
                last.then_inc(S["ss_done"], 1)

            def ss_values(u):
                rt = u % 2
                pe.wait_ge(S["ss_exp"], u + 1)
                if u:
                    pe.wait_ge(S["ss_pT"], u)
                if u < 2:
                    T(ps[:, 6, 0:P], pr[:, rt, 0:NCH], eye(P)).then_inc(S["ss_tr"], 1)
                else:
                    for j in range(2):
                        T(ps[:, 6, j * P:(j + 1) * P], pr[:, rt, j * P:(j + 1) * P], eye(P))
                    T(ps[0:NS, 6, 2 * P:3 * P], pr[:, rt, PAST:PAST + NS], eye(P)).then_inc(S["ss_tr"], 1)
                pe.wait_ge(S["ss_pT"], u + 1)
                if u:
                    pe.wait_ge(S["ss_o"], u)
                else:
                    pe.wait_ge(S["s_qbd"], 2)
                po = ps[:, 7, 0:P]
                if u < 2:
                    last = mm(po, pT[:, 0, 0:P], vcb[:], True, True)
                else:
                    pe.wait_ge(S["vc_in"], 16 * (NPG + 1))
                    vc = vcache if u < 4 else vwin
                    vn = kvt[0:NS, TP, (VS if u < 4 else VW):(VS if u < 4 else VW) + P]
                    mm(po, pT[0:NS, 0, 2 * P:3 * P], vn, True, False, True)
                    for q in range(4):
                        b = 4 * rt + q
                        for j in range(2):
                            last = mm(ps[32 * q:32 * q + 32, 7, 0:P], pT[:, 0, j * P + 32 * q:j * P + 32 * q + 32],
                                      vc[:, 2 * b + j, :], False, j == 1, True)
                last.then_inc(S["ss_pv"], 1)

            pe.wait_ge(S["cv_ok"], CC)
            pe.wait_ge(S["cs_out"], 1)
            pe.wait_ge(S["s_qbd"], 1)
            ss_scores(0)
            ss_scores(1)
            keys_T(0, 16 * NPG)
            ss_values(0)
            ss_scores(2)
            ss_values(1)
            ss_scores(3)
            keys_T(1, 16 * NPG + 16)
            ss_values(2)
            ss_scores(4)
            ss_values(3)
            ss_scores(5)
            ss_values(4)
            ss_values(5)
            pe.wait_ge(S["ss_o"], 6)
            for rt in range(2):
                last = T(ps[:, 5, rt * P:(rt + 1) * P], osam[:, rt, :], eye(P))
            last.then_inc(S["so_ps"], 1)
            pe.wait_ge(S["so_ok"], 1)

            pe.wait_ge(S["yz_ok"], 2 + NKV)

            def scores(u):
                i, k = divmod(u, 2 * NH)
                if u >= 2:
                    pe.wait_ge(S["u_soft"], u - 1)
                mm(ps[:, u % 2, 0:width(u)], qz[:, k // 2, i * P:(i + 1) * P], (ksT, kwT)[u % 2][:, 0:width(u)],
                   True, True).then_inc(S["u_s"], 1)

            def cm_scores(i):
                nk = blocks(i)
                if i:
                    pe.wait_ge(S["cm_o"], i)
                for n in range(NH):
                    last = mm(ps[:, 6 + n // G, (n % G) * nk:(n % G + 1) * nk], qz[:, n, i * P:(i + 1) * P],
                              kcpT[:, 0:nk], True, True)
                last.then_inc(S["cm_done"], 1)

            def cm_rows(i):
                nk = blocks(i)
                pe.wait_ge(S["cm_p"], i + 1)
                for n in range(NH):
                    last = T(ps[0:nk, 6 + n // 4, (n % 4) * P:(n % 4 + 1) * P], cme[:, n * nk:(n + 1) * nk], eye(P))
                last.then_inc(S["cm_tr"], 1)

            def cm_values(i):
                nk = blocks(i)
                pe.wait_ge(S["cm_pT"], i + 1)
                for n in range(NH):
                    last = mm(ps[:, 6, n * HD:(n + 1) * HD], cpT[0:nk, n, :], vcp[0:nk, HD * (n // G):HD * (n // G) + HD],
                              True, True)
                last.then_inc(S["cm_pv"], 1)

            def heads_out(i):
                pe.wait_ge(S["u_o"], 2 * NH * (i + 1))
                for c in range(CC):
                    last = T(ps[:, 5, c * P:(c + 1) * P], oacc[:, c * P:(c + 1) * P], eye(P))
                last.then_inc(S["ot_ps"], 1)

            cm_scores(0)
            scores(0)
            scores(1)
            cm_rows(0)
            cm_values(0)
            for u in range(UNITS):
                i, k = divmod(u, 2 * NH)
                pe.wait_ge(S["u_exp"], u + 1)
                if u >= 2:
                    pe.wait_ge(S["u_pT"], u - 1)
                for j in range(i + 1):
                    last = T(ps[:, 2 + u % 2, j * P:(j + 1) * P], pr[:, u % 2, j * P:(j + 1) * P], eye(P))
                last.then_inc(S["u_tr"], 1)
                if u + 2 < UNITS:
                    scores(u + 2)
                if i + 1 < TP and k == 2:
                    cm_scores(i + 1)
                if i + 1 < TP and k == 6:
                    cm_rows(i + 1)
                if i + 1 < TP and k == 10:
                    cm_values(i + 1)
                if i and k == 0:
                    heads_out(i - 1)
                if i and k == 1:
                    pe.wait_ge(S["ot_ok"], i)
                pe.wait_ge(S["u_pT"], u + 1)
                if u >= 2:
                    pe.wait_ge(S["u_o"], u - 1)
                v0 = (VS, VW)[u % 2] + HD * (k // 2 // G)
                for j in range(i + 1):
                    last = mm(ps[:, 4 + u % 2, 0:HD], pT[:, u % 2, j * P:(j + 1) * P],
                              kvt[:, j, v0:v0 + HD], j == 0, j == i)
                last.then_inc(S["u_pv"], 1)
            heads_out(TP - 1)

            def route(t):
                r = rows(t)
                pe.wait_ge(S["ht_ok"], t + 1)
                for c in range(DC):
                    last = mm(ps[0:r, 6, (NG + NE) * t:(NG + NE) * (t + 1)], xT[:, c, t * P:t * P + r], wr[:, c, :],
                              c == 0, c == DC - 1)
                last.then_inc(S["r_done"], 1)

            def next_T(t):
                pe.wait_ge(S["hn_done"], t + 1)
                if t:
                    pe.wait_ge(S["ht_ok"], t)
                token_T(t, hnt[0:rows(t), :], 4, S["ht_done"])

            pe.wait_ge(S["wout_in"], 32)
            pe.wait_ge(S["ot_ok"], TP)
            for t in range(TT):
                r = rows(t)
                if t >= 2:
                    pe.wait_ge(S["op_h"], t - 1)
                if t == TP:
                    quarters(2 * (t % 2), mixT[:, :, SEQ:N], wout).then_inc(S["op_done"], 1)
                else:
                    for half in range(2):
                        for c in range(DC):
                            last = mm(ps[0:r, 2 * (t % 2) + half, :], mixT[:, c, t * P:t * P + r],
                                      wout[:, c, half * 512:(half + 1) * 512], c == 0, c == DC - 1)
                    last.then_inc(S["op_done"], 1)
                if t == 1:
                    pe.wait_ge(S["wr_in"], 64)
                if t:
                    next_T(t - 1)
                if t >= 2:
                    route(t - 2)
            next_T(TP)
            route(TP - 1)
            route(TP)
            pe.wait_ge(S["asn_ok"], 1)
            every = ps[:, 7, 0:TT * NE]
            mm(every, cst[:, C_TRI:C_TRI + P], asn[:].rearrange("p t e -> p (t e)"), True, False)
            mm(every, cst[:, C_ONE:C_ONE + P], cum[:].rearrange("p t e -> p (t e)"), False, True)
            total_ = ps[:, 7, TT * NE:(TT + 1) * NE]
            mm(total_, cst[:, C_ONE:C_ONE + P], cum[:, TP, :], True, False)
            mm(total_, cst[0:NS, C_ONE:C_ONE + P], asn[0:NS, TP, :], False, True).then_inc(S["pf_done"], 1)
            pe.wait_ge(S["jei_ok"], 1)

            def rows_T(J):
                pe.wait_ge(S["gath"], J * 16 + 16)
                pe.wait_ge(S["x_lo"], J)
                pe.sem_inc(S["passed"], 1)
                v = xg[0:SLOTS, :].rearrange("r (p c) -> r p c", c=DC)
                for c in range(DC):
                    last = T(ps[:, 3, c * SLOTS:(c + 1) * SLOTS], v[:, :, c], eye(SLOTS))
                last.then_inc(S["x_tr"], 1)

            def piece(J, i):
                pe.wait_ge(S["lo_ok"], J * 6 + (i + 1))
                half = PIECES[i][1]
                if i in (D0, D1):
                    for j in range(2):
                        c = 2 * half + j
                        for n in range(2):
                            for w in (hiw, low):
                                last = mm(ps[:, 5 + n, :], hpack[:, c, :], w[:, i, j * D + n * 512:j * D + (n + 1) * 512],
                                          c == 0 and w is hiw, c == 3 and w is low)
                else:
                    for j in range(4):
                        c = 4 * half + j
                        for w in (hiw, low):
                            last = mm(ps[:, i // U0, :], xpack[:, c, :], w[:, i, j * 512:(j + 1) * 512],
                                      c == 0 and w is hiw, c == DC - 1 and w is low)
                last.then_inc(S["used"], 1)

            def none_used(n):
                pe.wait_ge(S["used"], n)
                pe.sem_inc(S["used"], 2)

            def work(J, first=False, second=False, last=False):
                if last:
                    none_used(J * 6 + 6)
                else:
                    pe.wait_ge(S["x_lo"], J + 1)
                    piece(J, G0)
                if not first:
                    pe.wait_ge(S["gu_copied"], J * 2)
                    pe.wait_ge(S["hT_ok"], J * 2 - 1)
                    for k in range(2):
                        v = Sg[:, k, :].rearrange("r (p c) -> r p c", c=4)
                        for c in range(4):
                            last_mm = mm(ps[:, 2, k * 256 + c * SLOTS:k * 256 + (c + 1) * SLOTS], v[:, :, c],
                                         cst[:, C_II:C_II + SLOTS], True, True)
                    last_mm.then_inc(S["gt_done"], 1)
                if not last:
                    piece(J, G1)
                if first:
                    none_used(8)
                else:
                    pe.wait_ge(S["h_ok"], J)
                    pe.wait_ge(S["y_ok"], J)
                    piece(J, D0)
                    piece(J, D1)
                if not last:
                    piece(J, U0)
                    piece(J, U1)
                    rows_T(J + 1)

            rows_T(0)
            rounds(pe, work)
            pe.wait_ge(S["ple_in"], 48)

            def embed_T(t, n, bank):
                for k in range(n):
                    r = rows(t + k)
                    v = pin[0:r, t + k, :].rearrange("r (p c) -> r p c", c=2)
                    for c in range(2):
                        last = T(ps[:, bank, (2 * k + c) * P:(2 * k + c) * P + r], v[:, :, c], eye(r))
                last.then_inc(S["f_ple"], 1)

            def project(t):
                r, b = rows(t), 3 * (t % 2)
                for half in range(2):
                    for c in range(2):
                        last = mm(ps[0:r, b + half, :], plT[:, c, t * P:t * P + r], wple[:, c, half * 512:(half + 1) * 512],
                                  c == 0, c == 1)
                last.then_inc(S["f_ple"], 1)

            embed_T(0, 2, 7)
            embed_T(2, 2, 2)
            pe.wait_ge(S["f_pl"], 1)
            project(0)
            embed_T(4, 1, 7)
            project(1)
            pe.wait_ge(S["f_pl"], 3)
            project(2)
            pe.wait_ge(S["f_pl"], 5)
            project(3)
            pe.wait_ge(S["f_pl"], 6)
            project(4)

            def normed_T(t):
                pe.wait_ge(S["f_hn"], t + 1)
                if t >= 2:
                    pe.wait_ge(S["f_hpT"], t - 1)
                token_T(t, h2n[0:rows(t), t % 2, :], 2 * (t % 2), S["f_tr"])

            pe.wait_ge(S["wpg_in"], 48)
            pe.wait_ge(S["f_pl"], 8)
            normed_T(0)
            for t in range(TT):
                r, b = rows(t), 4 + 2 * (t % 2)
                pe.wait_ge(S["f_hpT"], t + 1)
                if t >= 2:
                    pe.wait_ge(S["f_z"], t - 1)
                if t == TP:
                    quarters(b, hpT[:, t % 2, :, 0:NS], wpg).then_inc(S["f_mm"], 1)
                    break
                for half in range(2):
                    for c in range(DC):
                        last = mm(ps[0:r, b + half, :], hpT[:, t % 2, c, 0:r], wpg[:, c, half * 512:(half + 1) * 512],
                                  c == 0, c == DC - 1)
                    if half == 0 and t + 1 < TT:
                        normed_T(t + 1)
                last.then_inc(S["f_mm"], 1)

        @block.vector
        def _(dve):
            chain = Chain(dve, S["dve_chain"])
            V = nc.vector
            TTn, TS, STT = V.tensor_tensor, V.tensor_scalar, V.scalar_tensor_tensor

            roots = []

            def rms(x):
                roots.append(1)
                dve.wait_ge(S["root_ok"], len(roots))
                chain(V.reciprocal(x, x))

            def both(b, r=P):
                return ps[0:r, b:b + 2, :].rearrange("p k n -> p (k n)")

            V.memset(gates[:], 0.0)
            V.memset(eps[:], EPS).then_inc(S["eps_ok"], 1)
            for t in range(TT):
                r = rows(t)
                rms(rn[0:r, t:t + 1])
                if t >= 2:
                    dve.wait_ge(S["xT_t"], t - 1)
                TS(xn[0:r, t % 2, :], h[0:r, t, :], rn[0:r, t:t + 1], None, ALU.mult).then_inc(S["xn_done"], 1)
                if t:
                    token_cols(dve, S["xT_t"], t - 1, gmix, 2 * ((t - 1) % 2), S["xT_ok"])
            token_cols(dve, S["xT_t"], TP, gmix, 2 * (TP % 2), S["xT_ok"])
            dve.wait_ge(S["rb_in"], 64)
            V.memset(SM[NBUCK:NBUCK + 1, 0:NH], -BIG).then_inc(S["rb_ok"], 1)
            dve.wait_ge(S["vec_in"], 16 * 10)
            chain(TS(gq[:], gq[:], HD ** -0.5, None, ALU.mult))
            dve.wait_ge(S["cv_vec"], 1)
            V.tensor_copy(cwT[:], ps[:, 5, 0:12])
            V.tensor_copy(upst[:], ps[:, 5, 16:80].rearrange("p (c n) -> p c n", c=CC)).then_inc(S["cv_vecc"], 1)

            dve.wait_ge(S["cv_vecc"], 1)
            V.memset(cmb[:], -BIG)
            V.memset(nmk[:], -BIG)
            V.memset(upp[:, 0:2], 0.0)
            chain(V.memset(Qbd[:], 0.0))

            for t in range(TT):
                r = rows(t)
                dve.wait_ge(S["kv_copied"], t + 1)
                q = qn[0:r, t % 2, :]
                kk = kvt[0:r, t, KS:KW + P].rearrange("p (i n) -> p i n", n=P)[:, 0:3:2, :]
                TTn(sq[0:r, 0:512], q, q, ALU.mult)
                chain(TTn(sq[0:r, 512:768].rearrange("p (i n) -> p i n", n=P), kk, kk, ALU.mult))
                V.reduce_sum(ss12[0:r, :], sq[0:r, 0:768].rearrange("p (k d) -> p k d", d=HD), axis=X).then_inc(S["ss_sum"], 1)
                rms(ss12[0:r, :])
                r8 = ss12[0:r, 0:NH].unsqueeze(2).broadcast_to([r, NH, HD])
                TTn(q.rearrange("p (k d) -> p k d", d=HD), q.rearrange("p (k d) -> p k d", d=HD), r8, ALU.mult)
                for i, c0 in enumerate((KS, KW)):
                    x = kvt[0:r, t, c0:c0 + P]
                    r2 = ss12[0:r, NH + 2 * i:NH + 2 * i + 2].unsqueeze(2).broadcast_to([r, NKV, HD])
                    x3 = x.rearrange("p (k d) -> p k d", d=HD)
                    chain(TTn(x3, x3, r2, ALU.mult))
                    last = TTn(x, x, gk[0:r, i, :], ALU.mult)
                last.then_inc(S["tm_norm"], 1)
                dve.wait_ge(S["tr_done"], t + 1)
                V.tensor_copy(ksT[:, t * P:t * P + r], ps[:, 7, 0:r])
                V.tensor_copy(kwT[:, t * P:t * P + r], ps[:, 7, P:P + r]).then_inc(S["tr_k"], 1)

            def compress_dve(i):
                for pp in range(8):
                    dve.wait_ge(S["X_tr"], 8 * i + pp + 1)
                    if i and pp == 0:
                        dve.wait_ge(S["hid_done"], 2)
                    V.tensor_copy(XT[:, pp, :], ps[:, pp % 4, 0:2 * XC]).then_inc(S["X_ev"], 1)
                dve.wait_ge(S["hid_done"], 2 * i + 2)
                if i:
                    dve.wait_ge(S["hid_gelu"], 2)
                V.tensor_copy(hb[:], ps[:, 4:6, XC - 2]).then_inc(S["hid_b"], 1)

            def keys_norm():
                V.tensor_copy(kcb, ps[:, 6, 0:P])
                chain(V.tensor_copy(kcp[0:NCP, :], ps[0:NCP, 7, 0:P]))
                for x, r in ((kcb, P), (kcp, NCP)):
                    chain(TTn(nsq[0:r, :], x[0:r, :], x[0:r, :], ALU.mult))
                    V.reduce_sum(ss12[0:r, 0:2], nsq[0:r, :].rearrange("p (k d) -> p k d", d=HD), axis=X).then_inc(S["ss_sum"], 1)
                    rms(ss12[0:r, 0:2])
                    x3 = x[0:r, :].rearrange("p (k d) -> p k d", d=HD)
                    last = TTn(x3, x3, ss12[0:r, 0:2].unsqueeze(2).broadcast_to([r, NKV, HD]), ALU.mult)
                    if r == P:
                        chain(last)
                last.then_inc(S["cb_ok"], 1)

            def conv_dve(c4):
                dve.wait_ge(S["cv_xh"], c4 + 1)
                if c4 == 0:
                    dve.wait_ge(S["bl_out"], 16)
                NH2 = N // 2
                dve.wait_ge(S["cv_done"], 3 * c4 + 2)
                V.tensor_copy(ups[:, :, 0:2], upst[:, c4, :].rearrange("p (b k) -> p b k", k=2))
                TTn(upp[:, 2:2 + NH2], ps[:, 4, 0:NH2], sq[:, 0:NH2], ALU.mult)
                TTn(upp[:, 2 + NH2:2 + SEQ], ps[:, 5, 0:SEQ - NH2], sq[:, NH2:SEQ], ALU.mult)
                chain(TTn(ups[:, :, 2:6], ps[:, 5, SEQ - NH2:NH2].rearrange("p (b t) -> p b t", t=NT),
                          sq[:, SEQ:N].rearrange("p (b t) -> p b t", t=NT), ALU.mult))
                dve.sem_inc(S["cv_u"], 1)
                V.tensor_copy(cs_in[:, c4, 0:2], upp[:, SEQ:SEQ + 2])
                V.tensor_copy(cs_in[:, c4, 2:18].rearrange("p (b k) -> p b k", k=2), ups[:, :, NT:NT + 2])
                yp, ysm = mixT[:, c4, 0:SEQ], mixT[:, c4, SEQ:N].rearrange("p (b t) -> p b t", t=NT)
                TS(yp, upp[:, 0:SEQ], cwT[:, c4:c4 + 1], None, ALU.mult)
                chain(TS(ysm, ups[:, :, 0:NT], cwT[:, c4:c4 + 1], None, ALU.mult))
                for k in (1, 2):
                    w = cwT[:, CC * k + c4:CC * k + c4 + 1]
                    STT(yp, upp[:, k:k + SEQ], w, yp, ALU.mult, ALU.add)
                    chain(STT(ysm, ups[:, :, k:k + NT], w, ysm, ALU.mult, ALU.add))
                dve.wait_ge(S["cv_done"], 3 * c4 + 3)
                TTn(mixT[:, c4, 0:NH2], mixT[:, c4, 0:NH2], ps[:, 2, 0:NH2], ALU.mult)
                chain(TTn(mixT[:, c4, NH2:N], mixT[:, c4, NH2:N], ps[:, 3, 0:NH2], ALU.mult))
                dve.sem_inc(S["cv_ok"], 1)

            compress_dve(0)
            dve.wait_ge(S["tr_q"], TT)
            for hh in range(NKV):
                p0 = hh * HD
                last = V.tensor_copy(Qbd[p0:p0 + HD, :, 16 * hh:16 * hh + 16].rearrange("p b (g t) -> p b g t", g=G),
                                     qT[p0:p0 + HD, :, SEQ:N].rearrange("p g (b t) -> p b g t", b=NB))
            last.then_inc(S["s_qbd"], 1)

            dve.wait_ge(S["g_exp"], 1)
            chain(TS(gates[:], gates[:], 1.0, None, ALU.add))
            V.reciprocal(gates[:], gates[:]).then_inc(S["g_ok"], 1)
            dve.wait_ge(S["cb_done"], 1)
            keys_norm()
            conv_dve(0)
            dve.wait_ge(S["ct_done"], 1)
            TS(kcbT[:], ps[:, 6, 256:256 + NCH], gk0[:, 0:1], None, ALU.mult)
            TS(kcpT[:, 0:NCP], ps[:, 6, 384:384 + NCP], gk0[:, 0:1], None, ALU.mult).then_inc(S["ct_ok"], 1)
            for rt in range(2):
                dve.wait_ge(S["g_ps"], 2)
                chain(TTn(g24.rearrange("p (n k) -> p n k", k=NBR),
                          ps[:, 7, 256 + 32 * rt:280 + 32 * rt].rearrange("p (n k) -> p n k", k=NBR),
                          cst[:, C_NM:C_NM + NH].unsqueeze(2).broadcast_to([P, NH, NBR]), ALU.mult))
                chain(V.reduce_sum(gs[:, rt, :], g24.rearrange("p (n k) -> p k n", k=NBR), axis=X))
            dve.sem_inc(S["s_qbd"], 1)
            conv_dve(1)
            compress_dve(1)
            dve.wait_ge(S["cb_done"], 2)
            V.tensor_copy(vcb[:], ps[:, 6, 0:P])
            V.tensor_copy(vcp[0:NCP, :], ps[0:NCP, 7, 0:P]).then_inc(S["cb_ok"], 1)
            conv_dve(2)
            conv_dve(3)
            dve.wait_ge(S["SM_in"], 16 * 4 * NH)
            for b in range(NB):
                q0, rt = 32 * (b % 4), b // 4
                V.tensor_copy(cmb[q0:q0 + 32, rt, CS * b:CS * b + CS - 1],
                              SM[q0:q0 + 32, 2 * STRIDE - 1:2 * STRIDE - 1 + STRIDE * (CS - 2) + 1:STRIDE])
                V.tensor_copy(nmk[q0:q0 + 32, rt, NT * b:NT * b + NT], SM[q0:q0 + 32, PAST:PAST + NT])
            dve.wait_ge(S["cs_ps"], 1)
            chain(V.tensor_copy(cs_out[:], ps[0:18, 7, :]))
            dve.sem_inc(S["cs_out"], 1)

            def ss_soft(u):
                rt = u % 2
                dve.wait_ge(S["ss_done"], u + 1)
                if u >= 2:
                    dve.wait_ge(S["ss_exp"], u - 1)
                if u < 2:
                    V.tensor_tensor_reduce(sc[:, rt, 0:NCH], ps[:, 4 + rt, 0:NCH], cmb[:, rt, :], -1.0, BIG, ALU.add, ALU.min,
                                           st[:, u:u + 1]).then_inc(S["ss_soft"], 1)
                else:
                    w = PAST + NS
                    V.tensor_tensor_reduce(sc[:, rt, 0:PAST], ps[:, 4 + rt, 0:PAST], SM[:, 0:PAST], -1.0, BIG, ALU.add, ALU.min,
                                           st[:, u:u + 1])
                    chain(V.tensor_tensor_reduce(sc[:, rt, PAST:w], ps[:, 4 + rt, PAST:w], nmk[:, rt, :], -1.0, BIG, ALU.add,
                                                 ALU.min, st[:, 32 + u:33 + u]))
                    TTn(st[:, u:u + 1], st[:, u:u + 1], st[:, 32 + u:33 + u], ALU.min).then_inc(S["ss_soft"], 1)

            def ss_out(u):
                rt, br_ = u % 2, u // 2
                dve.wait_ge(S["ss_tr"], u + 1)
                if u:
                    dve.wait_ge(S["ss_pv"], u)
                if u < 2:
                    V.tensor_copy(pT[:, 0, 0:P], ps[:, 6, 0:P]).then_inc(S["ss_pT"], 1)
                else:
                    V.tensor_copy(pT[:, 0, 0:2 * P], ps[:, 6, 0:2 * P])
                    V.tensor_copy(pT[0:NS, 0, 2 * P:3 * P], ps[0:NS, 6, 2 * P:3 * P]).then_inc(S["ss_pT"], 1)
                chain(TS(st[:, 24:25], st[:, 8 + u:9 + u], 1e-30, None, ALU.max))
                chain(V.reciprocal(st[:, 24:25], st[:, 24:25]))
                chain(TTn(st[:, 24:25], st[:, 24:25], gs[:, rt, br_:br_ + 1], ALU.mult))
                chain(TS(st[:, 26:28], cst[:, C_HM:C_HM + NKV], st[:, 24:25], None, ALU.mult))
                dve.wait_ge(S["ss_pv"], u + 1)
                for hh in range(NKV):
                    if br_ == 0 and hh == 0:
                        chain(TS(osam[:, rt, 0:HD], ps[:, 7, 0:HD], st[:, 26:27], None, ALU.mult))
                    else:
                        chain(STT(osam[:, rt, 0:HD], ps[:, 7, hh * HD:(hh + 1) * HD], st[:, 26 + hh:27 + hh],
                                  osam[:, rt, 0:HD], ALU.mult, ALU.add))
                if br_ == NBR - 1:
                    chain(V.tensor_copy(osam[:, rt, HD:P], osam[:, rt, 0:HD]))
                dve.sem_inc(S["ss_o"], 1)

            ss_soft(0)
            ss_soft(1)
            for b in range(4):
                dve.wait_ge(S["kt_done"], b + 1)
                V.tensor_copy(kcT[:, 4 * b:4 * b + 4, :].rearrange("p g n -> p (g n)"), ps[:, b, :]).then_inc(S["kt_ok"], 1)
            ss_out(0)
            ss_soft(2)
            ss_out(1)
            ss_soft(3)
            for b in range(4):
                dve.wait_ge(S["kt_done"], b + 5)
                dve.wait_ge(S["ss_done"], 4)
                V.tensor_copy(kcT[:, 4 * b:4 * b + 4, :].rearrange("p g n -> p (g n)"), ps[:, b, :]).then_inc(S["kt_ok"], 1)
            ss_out(2)
            ss_soft(4)
            ss_out(3)
            ss_soft(5)
            ss_out(4)
            ss_out(5)
            dve.wait_ge(S["so_ps"], 1)
            dve.wait_ge(S["yz_out"], 16 * (MAXOV * SLOTS // P))
            for n in range(NH):
                p0 = HD * (n % 2)
                last = V.tensor_copy(
                    mixT[p0:p0 + HD, CC + n // 2, SEQ:N].rearrange("p (b t) -> p b t", t=NT),
                    ps[p0:p0 + HD, 5, 0:2 * P].rearrange("p (b n t) -> p b n t", n=NH, t=NT)[:, :, n, :])
            last.then_inc(S["so_ok"], 1)

            dve.wait_ge(S["M_in"], 16 * NH)

            def soft(u):
                i, k = divmod(u, 2 * NH)
                w = width(u)
                dve.wait_ge(S["u_s"], u + 1)
                if u >= 2:
                    dve.wait_ge(S["u_exp"], u - 1)
                V.tensor_tensor_reduce(sc[:, u % 2, 0:w], ps[:, u % 2, 0:w], M[:, k // 2, SEQ - w:SEQ], -1.0, BIG, ALU.add,
                                       ALU.min, st[:, 16 + u % 4:17 + u % 4]).then_inc(S["u_soft"], 1)

            def cm_views(i):
                nk = blocks(i)
                return [x[:, 0:NH * nk].rearrange("p (h n) -> p h n", h=NH) for x in (cms, cme)]

            def cm_soft(i):
                nk = blocks(i)
                c3, _ = cm_views(i)
                off = SEQ - P * (i + 1) + 2 * STRIDE - 1
                dve.wait_ge(S["cm_done"], i + 1)
                chain(TTn(c3.rearrange("p (b g) n -> p b g n", b=NKV),
                          ps[:, 6:8, 0:G * nk].rearrange("p b (g n) -> p b g n", g=G),
                          M[:, :, off:off + STRIDE * (nk - 1) + 1:STRIDE].rearrange("p (b g) n -> p b g n", b=NKV), ALU.add))
                chain(V.tensor_reduce(st[:, 32:40], c3, X, ALU.max))
                chain(TS(st[:, 32:40], st[:, 32:40], -0.1 * BIG, None, ALU.max))
                TTn(c3, c3, st[:, 32:40].unsqueeze(2).broadcast_to([P, NH, nk]), ALU.subtract).then_inc(S["cm_sub"], 1)

            def cm_probs(i):
                nk = blocks(i)
                _, e3 = cm_views(i)
                dve.wait_ge(S["cm_exp"], i + 1)
                gt = gates[:, i, :].rearrange("p (h k) -> p h k", k=NBR)
                chain(V.reduce_sum(st[:, 32:40], e3, axis=X))
                chain(TS(st[:, 32:40], st[:, 32:40], 1e-30, None, ALU.max))
                chain(V.reciprocal(st[:, 32:40], st[:, 32:40]))
                chain(TTn(st[:, 32:40], st[:, 32:40], gt[:, :, 0], ALU.mult))
                TTn(e3, e3, st[:, 32:40].unsqueeze(2).broadcast_to([P, NH, nk]), ALU.mult).then_inc(S["cm_p"], 1)

            def heads_out_dve(i):
                dve.wait_ge(S["ot_ps"], i + 1)
                V.tensor_copy(mixT[:, CC:DC, i * P:(i + 1) * P], ps[:, 5, :].rearrange("p (c n) -> p c n", c=CC))\
                    .then_inc(S["ot_ok"], 1)

            cm_soft(0)
            soft(0)
            soft(1)
            cm_probs(0)
            for u in range(UNITS):
                i, k = divmod(u, 2 * NH)
                n = k // 2
                if u + 2 < UNITS:
                    soft(u + 2)
                if k == 0:
                    if i:
                        heads_out_dve(i - 1)
                    dve.wait_ge(S["cm_pv"], i + 1)
                    chain(V.tensor_copy(oacc[:], ps[:, 6, :]))
                    dve.sem_inc(S["cm_o"], 1)
                if i + 1 < TP and k == 3:
                    cm_soft(i + 1)
                if i + 1 < TP and k == 5:
                    cm_probs(i + 1)
                dve.wait_ge(S["u_exp"], u + 1)
                coef = st[:, 28 + u % 4:29 + u % 4]
                chain(TS(coef, st[:, 20 + u % 4:21 + u % 4], 1e-30, None, ALU.max))
                chain(V.reciprocal(coef, coef))
                chain(TTn(coef, coef, gates[:, i, NBR * n + 1 + k % 2:NBR * n + 2 + k % 2], ALU.mult))
                dve.wait_ge(S["u_pv"], u + 1)
                if k % 2:
                    dve.wait_ge(S["u_o"], u)
                STT(oacc[:, n * HD:(n + 1) * HD], ps[:, 4 + u % 2, 0:HD], coef,
                    oacc[:, n * HD:(n + 1) * HD], ALU.mult, ALU.add).then_inc(S["u_o"], 1)
            heads_out_dve(TP - 1)

            dve.wait_ge(S["wout_in"], 32)
            dve.wait_ge(S["wr_in"], 64)
            for t in range(TT):
                r = rows(t)
                dve.wait_ge(S["op_done"], t + 1)
                if t == TP:
                    dve.wait_ge(S["kvout"], 16 * 8)
                    dve.wait_ge(S["kcmp_out"], 16)
                    dve.wait_ge(S["vcmp_out"], 16)
                    dve.wait_ge(S["winout"], 16 * (2 * NB + 2))
                    V.memset(zslot[:], 0).then_inc(S["z_ok"], 1)
                    TS(e64[:], cst[:, C_EID:C_EID + NE], float(SLOTS), None, ALU.mult)
                    V.memset(cum[:, 0, :], 0.0)
                    V.memset(lg[:], 0.0)
                if t == TP:
                    for q in range(4):
                        part = h[0:NS, TP, q * (D // 4):(q + 1) * (D // 4)]
                        last = TTn(part, part, ps[NS * q:NS * (q + 1), 2 * (t % 2), 0:D // 4], ALU.add)
                    last.then_inc(S["op_h"], 1)
                else:
                    TTn(h[0:r, t, :], h[0:r, t, :], both(2 * (t % 2), r), ALU.add).then_inc(S["op_h"], 1)
                if t:
                    token_cols(dve, S["ht_done"], t - 1, None, 4, S["ht_ok"])
                rms(rn[0:r, t:t + 1])
                if t:
                    dve.wait_ge(S["hn_out"], 16 * t)
                STT(hnt[0:r, :], h[0:r, t, :], rn[0:r, t:t + 1], gffn[0:r, :], ALU.mult, ALU.mult).then_inc(S["hn_done"], 1)
            token_cols(dve, S["ht_done"], TP, None, 4, S["ht_ok"])

            dve.wait_ge(S["r_done"], TT)
            W = NG + NE
            TTn(lg[:, 0:TP, :], ps[:, 6, 0:W * TP].rearrange("p (t n) -> p t n", n=W),
                br[:].unsqueeze(1).broadcast_to([P, TP, W]), ALU.add)
            chain(TTn(lg[0:NS, TP, :], ps[0:NS, 6, W * TP:W * TT], br[0:NS, :], ALU.add))

            def spread(x, n):
                return x.unsqueeze(2).broadcast_to([P, TT, n])

            def first_max(hot, x, m, n, tmp):
                chain(V.tensor_reduce(m, x, X, ALU.max))
                chain(TTn(tmp, x, spread(m, n), ALU.is_ge))
                desc = cst[:, C_DESC:C_DESC + n].unsqueeze(1).broadcast_to([P, TT, n])
                chain(TTn(tmp, tmp, desc, ALU.mult))
                chain(V.tensor_reduce(rs[:, 7, :], tmp, X, ALU.max))
                chain(TTn(hot, tmp, spread(rs[:, 7, :], n), ALU.is_equal))

            lgg = lg[:, :, 0:NG]
            first_max(og[:], lgg, rs[:, 0, :], NG, tg[:])
            TTn(tg[:], lgg, spread(rs[:, 0, :], NG), ALU.subtract).then_inc(S["r_log"], 1)
            chain(TS(og[:], og[:], 1.0, BIG, ALU.subtract, ALU.mult))
            chain(TTn(le[:].rearrange("p t (g e) -> p t g e", e=EG), lg[:, :, NG:W].rearrange("p t (g e) -> p t g e", e=EG),
                      og[:].unsqueeze(3).broadcast_to([P, TT, NG, EG]), ALU.add))
            first_max(oh1[:], le[:], rs[:, 1, :], NE, t32[:])
            chain(TS(t32[:], oh1[:], -3.0 * BIG, None, ALU.mult))
            chain(TTn(le[:], le[:], t32[:], ALU.add))
            first_max(oh2[:], le[:], rs[:, 2, :], NE, t32[:])
            chain(TTn(asn[:], oh1[:], oh2[:], ALU.add))
            for t in range(1, TT):
                last = TTn(cum[:, t, :], cum[:, t - 1, :], asn[:, t - 1, :], ALU.add)
                if t < TT - 1:
                    chain(last)
            last.then_inc(S["asn_ok"], 1)
            TTn(rs[:, 4, :], rs[:, 2, :], rs[:, 1, :], ALU.subtract).then_inc(S["r_e2"], 1)
            dve.wait_ge(S["r_exp"], 1)
            chain(V.reduce_sum(rs[:, 3, :], tg[:], axis=X))
            dve.wait_ge(S["r_exp"], 2)
            chain(TS(rs[:, 6, :], rs[:, 5, :], 1.0, None, ALU.add))
            chain(TTn(rs[:, 6, :], rs[:, 6, :], rs[:, 3, :], ALU.mult))
            chain(V.reciprocal(wts[:, 0, :], rs[:, 6, :]))
            chain(TTn(wts[:, 1, :], wts[:, 0, :], rs[:, 5, :], ALU.mult))
            dve.wait_ge(S["pf_done"], 1)
            cnt, nov, end, beg = (ovs[:, k, :] for k in range(4))
            chain(TS(cnt, ps[:, 7, TT * NE:(TT + 1) * NE], 1.0 / SLOTS, None, ALU.mult))
            over = jex[:].rearrange("p j e -> p (j e)")[:, 0:NE * OVMAX].rearrange("p (e k) -> p e k", k=OVMAX)
            chain(TTn(over, cnt.unsqueeze(2).broadcast_to([P, NE, OVMAX]),
                      cst[:, C_EID + 1:C_EID + 1 + OVMAX].unsqueeze(1).broadcast_to([P, NE, OVMAX]), ALU.is_gt))
            chain(V.reduce_sum(nov, over, axis=X))
            chain(V.tensor_tensor_scan(end, cst[:, C_ONE:C_ONE + NE], nov, 0.0, ALU.mult, ALU.add))
            chain(TTn(beg, end, nov, ALU.subtract))
            before = cnt
            eid = cst[:, C_EID:C_EID + NE]
            chain(TS(before, beg, float(SLOTS), float(SLOTS * (NE - 1)), ALU.mult, ALU.add))
            chain(STT(before, eid, -float(SLOTS), before, ALU.mult, ALU.add))

            def each(x):
                return x.unsqueeze(1).broadcast_to([P, TT, NE])

            rank = ps[:, 7, 0:TT * NE].rearrange("p (t e) -> p t e", e=NE)
            TTn(slot[:], rank, each(e64[:]), ALU.add)
            chain(STT(t32[:], rank, float(SLOTS), each(before), ALU.is_ge, ALU.mult))
            chain(TTn(slot[:], slot[:], t32[:], ALU.add))
            for k, oh in enumerate((oh1, oh2)):
                chain(TTn(t32[:], oh[:], slot[:], ALU.mult))
                chain(V.reduce_sum(rs[:, 6 + k, :], t32[:], axis=X))
            chain(V.tensor_copy(dst[:], rs[:, 6:8, :]))
            dve.sem_inc(S["dst_ok"], 1)
            jv = cst[:, C_EID:C_EID + MAXOV].unsqueeze(2).broadcast_to([P, MAXOV, NE])
            ev = eid.unsqueeze(1).broadcast_to([P, MAXOV, NE])
            chain(TTn(jex[:], jv, beg.unsqueeze(1).broadcast_to([P, MAXOV, NE]), ALU.is_ge))
            chain(TTn(jey[:], jv, end.unsqueeze(1).broadcast_to([P, MAXOV, NE]), ALU.is_lt))
            chain(TTn(jex[:], jex[:], jey[:], ALU.mult))
            chain(TTn(jex[:], jex[:], ev, ALU.mult))
            chain(V.reduce_sum(jef[:, NE:JOBS - 1], jex[:], axis=X))
            V.tensor_copy(jef[:, 0:NE], eid)
            chain(V.tensor_copy(jef[:, JOBS - 1:JOBS], end[:, NE - 1:NE]))
            V.tensor_copy(jtab[:], jef[:]).then_inc(S["jei_ok"], 1)

            dve.wait_ge(S["hn_out"], 16 * TT)

            def low_part(J, i):
                dve.wait_ge(S["hi_ok"], J * 6 + (i + 1))
                TTn(low[:, i, :], raw[:, i, :], hiw[:, i, :].bitcast(F32), ALU.subtract).then_inc(S["lo_ok"], 1)

            def none_low(n):
                dve.wait_ge(S["lo_ok"], n)
                dve.sem_inc(S["lo_ok"], 2)

            def work(J, first=False, second=False, last=False):
                if last:
                    none_low(J * 6)
                elif first:
                    low_part(J, G0)
                    low_part(J, G1)
                    none_low(2)
                    low_part(J, U0)
                    low_part(J, U1)
                    dve.wait_ge(S["x_hi"], J + 1)
                    TTn(xpack[:, :, SLOTS:2 * SLOTS], ps[:, 3, :].rearrange("p (c s) -> p c s", s=SLOTS),
                        xpack[:, :, 0:SLOTS].bitcast(F32), ALU.subtract).then_inc(S["x_lo"], 1)
                    return
                else:
                    low_part(J, G0)
                    dve.wait_ge(S["x_hi"], J + 1)
                    TTn(xpack[:, :, SLOTS:2 * SLOTS], ps[:, 3, :].rearrange("p (c s) -> p c s", s=SLOTS),
                        xpack[:, :, 0:SLOTS].bitcast(F32), ALU.subtract).then_inc(S["x_lo"], 1)
                    low_part(J, G1)
                dve.wait_ge(S["silu_ok"], J)
                dve.wait_ge(S["used"], J * 6 + 4)
                TTn(hT32[:].rearrange("p c s -> p (c s)"), sg[:], ps[:, 2, 256:512], ALU.mult).then_inc(S["hT_ok"], 1)
                dve.wait_ge(S["hT_ok"], J * 2)
                V.tensor_copy(hpack[:, :, 0:SLOTS], hT32[:]).then_inc(S["hT_ok"], 1)
                dve.wait_ge(S["hT_ok"], J * 2 + 1)
                TTn(hpack[:, :, SLOTS:2 * SLOTS], hT32[:], hpack[:, :, 0:SLOTS].bitcast(F32), ALU.subtract)\
                    .then_inc(S["h_ok"], 1)
                if not second:
                    rows_out(J)
                low_part(J, D0)
                low_part(J, D1)
                if not last:
                    low_part(J, U0)
                    low_part(J, U1)

            def rows_out(J):
                dve.wait_ge(S["ylo_ok"], J - 1)
                dve.wait_ge(S["ysb_free"], J - 1)
                TTn(ysb[0:SLOTS, :], both(5, SLOTS), ylo[0:SLOTS, :], ALU.add).then_inc(S["y_ok"], 1)

            dve.sem_inc(S["hT_ok"], 1)
            dve.sem_inc(S["y_ok"], 1)
            n = rounds(dve, work)
            rows_out(n + 1)

            def weigh(t):
                r = rows(t)
                dve.wait_ge(S[f"ya{t % 3}"], 32 * (t // 3 + 1))
                chain(STT(h[0:r, t, :], yga[0:r, t % 3, 0, :], wts[0:r, 0, t:t + 1], h[0:r, t, :], ALU.mult, ALU.add))
                STT(h[0:r, t, :], yga[0:r, t % 3, 1, :], wts[0:r, 1, t:t + 1], h[0:r, t, :], ALU.mult, ALU.add)\
                    .then_inc(S["f_h2"], 1)

            def normed(t):
                r = rows(t)
                rms(rn[0:r, t:t + 1])
                if t >= 2:
                    dve.wait_ge(S["f_tr"], t - 1)
                TS(h2n[0:r, t % 2, :], h[0:r, t, :], rn[0:r, t:t + 1], None, ALU.mult).then_inc(S["f_hn"], 1)

            def columns(t):
                r, b = rows(t), 2 * (t % 2)
                dve.wait_ge(S["f_tr"], t + 1)
                if t >= 2:
                    dve.wait_ge(S["f_mm"], t - 1)
                TTn(hpT[:, t % 2, :, 0:r], ps[:, b:b + 2, :].rearrange("p k (c n) -> p (k c) n", n=P)[:, :, 0:r],
                    gple[:].unsqueeze(2).broadcast_to([P, DC, r]), ALU.mult).then_inc(S["f_hpT"], 1)

            for t in range(2):
                weigh(t)
                normed(t)
                columns(t)
            weigh(2)
            normed(2)
            weigh(3)
            weigh(4)
            for t in range(TT):
                r, b = rows(t), 4 + 2 * (t % 2)
                gate = sgt[0:r, t % 2, :]
                if t >= 2:
                    dve.wait_ge(S[f"f_out{t % 2}"], 16 * (t // 2))
                dve.wait_ge(S["f_mm"], t + 1)
                if t == TP:
                    for q in range(4):
                        cols = slice(q * (D // 4), (q + 1) * (D // 4))
                        last = TTn(sgt[0:NS, t % 2, cols], ps[NS * q:NS * (q + 1), b, 0:D // 4], bpg[0:NS, cols], ALU.add)
                    last.then_inc(S["f_z"], 1)
                else:
                    TTn(gate, both(b, r), bpg[0:r, :], ALU.add).then_inc(S["f_z"], 1)
                if t + 3 < TT:
                    normed(t + 3)
                if t + 2 < TT:
                    columns(t + 2)
                dve.wait_ge(S["f_sig"], t + 1)
                chain(TTn(gate, gate, plo[0:r, t, :], ALU.mult))
                TTn(gate, gate, h[0:r, t, :], ALU.add).then_inc(S["f_o"], 1)


def kernel(**inputs):
    import concourse.bacc as _bacc
    from concourse.bass_utils import run_bass_kernel_spmd as _run

    nc = _bacc.Bacc("TRN2", target_bir_lowering=False, num_devices=1)
    consts, buckets, tok = constants()
    shapes = {
        "x_prompt": (SEQ, D), "x_sample": (NS, D), "p_prompt": (SEQ, PLE), "p_sample": (NS, PLE),
        "state_conv": (NB * 2, CONV), "page_table": (NB, PAST // PAGE), "conv_w": (3, CONV),
        "q_norm": (HD,), "k_norm": (NBR, HD), "norm_mix": (D,), "norm_ffn": (D,), "norm_ple": (D,), "b_ple_gate": (D,),
        "b_router_group": (NG,), "b_router_expert": (NE,), "rel_bias": (NBUCK, NH),
        "cache_k_win": (NB, PAST, P), "cache_v_win": (NB, PAST, P),
    }
    arrays, a, o = {}, {}, {}

    def put(name, x):
        arrays[f"in_{name}"] = x
        a[name] = nc.dram_tensor(f"in_{name}", x.shape, mybir.dt.from_np(x.dtype), kind="ExternalInput").ap()

    for name, x in inputs.items():
        x = np.ascontiguousarray(x)
        if name in shapes:
            x = x.reshape(shapes[name])
        elif name.startswith("cache_"):
            x = x.reshape(x.shape[1], PAGE, P)
        else:
            x = x.reshape(x.shape[1:])
        put(name, x)
    put("consts", consts)
    put("buckets", buckets)
    put("tok", tok)
    kv = ("k_cmp", "v_cmp", "k_slc", "v_slc", "k_win", "v_win")
    outs = [("y_prompt", (SEQ, D), (1, SEQ, D)), ("y_sample", (NS, D), (NB, NT, D))]
    outs += [(n + "_p", (SEQ, P), (1, 1, SEQ, NKV, HD)) for n in kv]
    outs += [("conv_p", (2, CONV), (1, 1, 2, CONV))]
    outs += [(n + "_s", (NS, P), (1, NB, NT, NKV, HD)) for n in kv[:4]]
    outs += [(n + "_s", (NB, PAST, P), (1, NB, PAST, NKV, HD)) for n in kv[4:]]
    outs += [("conv_s", (NB * 2, CONV), (1, NB, 2, CONV))]
    for name, shape, _ in outs:
        o[name] = nc.dram_tensor(f"out_{name}", shape, F32, kind="ExternalOutput").ap()
    build(nc, a, o)
    r = _run(nc, [arrays], core_ids=[0])
    return tuple(r.results[0][f"out_{name}"].reshape(full) for name, _, full in outs)
```
